# Optimizing a Trainium2 kernel written in Bass

```python
import math
import jax
import jax.numpy as jnp
from jax import lax
import numpy as np

D_MODEL = 1024
BATCH = 1
SEQ = 128
DEPTH = 2
DEC_BATCH = 1
DEC_SEQ = 1024
PAST_LEN = 256

GRID_W = 64
HG_HEADS = 4
HG_DK = 64
HG_DV = 64
HG_QK = HG_HEADS * HG_DK
HG_W = HG_HEADS * HG_DV
DA_HEADS = 4
DA_DQK = 64
DA_DV = 2 * DA_DQK
DA_QK = 2 * DA_HEADS * DA_DQK
DA_W = DA_HEADS * DA_DV
HY_W = D_MODEL - HG_W - DA_W
HY_ORDER = 2
HY_SHORT = 3
HY_POS_EMB = 33
HY_HIDDEN = 64
HY_SHORT_DECAY_PCT = 0.3
HY_LONG_DECAY_PCT = 1.5
HY_TARGET = 1e-2
N_EXPERTS = 16
EC_CAPACITY_FACTOR = 2
D_FF_EXPERT = 1024
N_MOD = 6
CHUNK = 32
Q_BLOCK = 128
ROPE_BASE = 10000.0
NORM_EPS = 1e-6
IN_SIZES = (HG_QK, HG_QK, HG_QK, HG_W, HG_W, DA_QK, DA_QK, DA_W, (HY_ORDER + 1) * HY_W)
D_IN = 3 * HG_QK + 2 * HG_W + 2 * DA_QK + DA_W + (HY_ORDER + 1) * HY_W

kernel_name = 'hybrid_diffusion_step'

F32 = jnp.float32

def _rmsnorm(x, g):
    x32 = x.astype(F32)
    return x32 * lax.rsqrt(jnp.mean(x32 * x32, axis=-1, keepdims=True) + NORM_EPS) * g.astype(F32)

def _split_cols(z):
    out = []
    start = 0
    for size in IN_SIZES:
        out.append(z[..., start:start + size])
        start += size
    return out

def _modulation(cond, w_mod, b_mod):
    m = jax.nn.silu(cond.astype(F32)) @ w_mod.astype(F32) + b_mod.astype(F32)
    return jnp.split(m[:, None, :], N_MOD, axis=-1)

def _gla_chunk_scan(q, k, v, logf, s0):
    n, h, L, _ = q.shape
    dv = v.shape[-1]
    nc = L // CHUNK

    def chunks(a):
        return jnp.moveaxis(a.reshape(n, h, nc, CHUNK, a.shape[-1]), 2, 0)

    lower = jnp.tril(jnp.ones((CHUNK, CHUNK), dtype=bool))[:, :, None]

    def step(state, blk):
        qc, kc, vc, gc = blk
        b = jnp.cumsum(gc, axis=2)
        o_inter = jnp.einsum('nhtk,nhkv->nhtv', qc * jnp.exp(b), state)
        rel = jnp.where(lower, b[:, :, :, None, :] - b[:, :, None, :, :], -jnp.inf)
        att = jnp.einsum('nhtk,nhtsk,nhsk->nhts', qc, jnp.exp(rel), kc)
        o = o_inter + jnp.einsum('nhts,nhsv->nhtv', att, vc)
        b_end = b[:, :, -1:, :]
        state = (jnp.exp(b_end[:, :, 0, :])[..., None] * state
                 + jnp.einsum('nhsk,nhsv->nhkv', kc * jnp.exp(b_end - b), vc))
        return state, o

    s_fin, o = lax.scan(step, s0.astype(F32), (chunks(q), chunks(k), chunks(v), chunks(logf)))
    o = jnp.moveaxis(o, 0, 2).reshape(n, h, L, dv)
    return o, s_fin

def _hgrn_mixer(hq, hff, hfb, hi, hg, lb, s0, norm_g):
    B, L, _ = hq.shape

    def heads(a, d):
        return a.reshape(B, L, HG_HEADS, d).transpose(0, 2, 1, 3)

    def gates(f_logit, lbd):
        f = heads(f_logit, HG_DK)
        lbd = lbd.reshape(HG_HEADS, 1, HG_DK)
        k = (1.0 - lbd) * jax.nn.sigmoid(-f)
        logf = jnp.logaddexp(jnp.log(lbd), jnp.log1p(-lbd) + jax.nn.log_sigmoid(f))
        return k, logf

    q = heads(hq, HG_DK)
    v = heads(hi, HG_DV)
    k_f, g_f = gates(hff, lb[0])
    k_b, g_b = gates(hfb, lb[1])

    def rev(a):
        return a[:, :, ::-1]

    o, s_fin = _gla_chunk_scan(
        jnp.concatenate([q, rev(q)], axis=0),
        jnp.concatenate([k_f, rev(k_b)], axis=0),
        jnp.concatenate([v, rev(v)], axis=0),
        jnp.concatenate([g_f, rev(g_b)], axis=0),
        s0.reshape(2 * B, HG_HEADS, HG_DK, HG_DV))
    o = o[:B] + rev(o[B:])
    o = _rmsnorm(o, norm_g).transpose(0, 2, 1, 3).reshape(B, L, HG_W)
    return o * jax.nn.silu(hg), s_fin.reshape(2, B, HG_HEADS, HG_DK, HG_DV)

def _axial_rope(x):
    L = x.shape[-2]
    n_rows = L // GRID_W
    rows, cols = jnp.meshgrid(jnp.arange(n_rows), jnp.arange(GRID_W), indexing='ij')
    half = DA_DQK // 2
    inv = ROPE_BASE ** (-jnp.arange(0, half, 2, dtype=F32) / half)

    def rot(xa, pos):
        ang = pos.reshape(-1).astype(F32)[:, None] * inv[None, :]
        ang = jnp.concatenate([ang, ang], axis=-1)
        x1, x2 = jnp.split(xa, 2, axis=-1)
        return xa * jnp.cos(ang) + jnp.concatenate([-x2, x1], axis=-1) * jnp.sin(ang)

    return jnp.concatenate([rot(x[..., :half], rows), rot(x[..., half:], cols)], axis=-1)

def _diff_attention(q, k, v, lam):
    B, H, _, Lq, _ = q.shape
    nb = Lq // Q_BLOCK
    qb = jnp.moveaxis(q.reshape(B, H, 2, nb, Q_BLOCK, DA_DQK), 3, 0)
    scale = DA_DQK ** -0.5

    def block(qblk):
        s = jnp.einsum('bhmqd,bhmkd->bhmqk', qblk, k) * scale
        p = jax.nn.softmax(s, axis=-1)
        a = p[:, :, 0] - lam * p[:, :, 1]
        return jnp.einsum('bhqk,bhkv->bhqv', a, v)

    o = lax.map(block, qb)
    return jnp.moveaxis(o, 0, 2).reshape(B, H, Lq, DA_DV)

def _hyena_filters(L, w1, b1, w2, b2, w3, freq):
    t = jnp.linspace(0.0, 1.0, L, dtype=F32)[:, None]
    bands = (HY_POS_EMB - 1) // 2
    fr = jnp.linspace(1e-4, bands - 1, bands, dtype=F32)[None, :]
    w = 2.0 * math.pi * jnp.arange(L, dtype=F32)[:, None] / L
    z = jnp.concatenate([t, jnp.cos(fr * w), -jnp.sin(fr * w)], axis=-1)
    hid = jnp.sin(freq[0].astype(F32) * (z @ w1.astype(F32) + b1.astype(F32)))
    hid = jnp.sin(freq[1].astype(F32) * (hid @ w2.astype(F32) + b2.astype(F32)))
    h = (hid @ w3.astype(F32)).reshape(L, 2, HY_ORDER, HY_W)
    max_decay = math.log(HY_TARGET) / HY_SHORT_DECAY_PCT
    min_decay = math.log(HY_TARGET) / HY_LONG_DECAY_PCT
    deltas = jnp.linspace(min_decay, max_decay, HY_W, dtype=F32)
    h = h * jnp.exp(-t[:, :, None, None] * jnp.abs(deltas))
    h = h / jnp.sum(jnp.abs(h), axis=(0, 1), keepdims=True)
    fwd, bwd = h[:, 0], h[:, 1]
    circ_filter = jnp.concatenate([fwd, jnp.zeros_like(fwd[:1]), bwd[:0:-1]], axis=0)
    return jnp.fft.rfft(circ_filter, axis=0)

def _long_conv(u, filt_f, skip):
    L = u.shape[1]
    uf = jnp.fft.rfft(u, n=2 * L, axis=1)
    y = jnp.fft.irfft(uf * filt_f[None], n=2 * L, axis=1)[:, :L]
    return y + u * skip

def _hyena_mixer(zh, filt_f, skip, conv_w, conv_b):
    L = zh.shape[1]
    pad = HY_SHORT // 2
    zp = jnp.pad(zh, ((0, 0), (pad, pad), (0, 0)))
    zc = conv_b.astype(F32)
    for j in range(HY_SHORT):
        zc = zc + zp[:, j:j + L] * conv_w[j].astype(F32)
    v, x1, x2 = jnp.split(zc, HY_ORDER + 1, axis=-1)
    z = x1 * _long_conv(v, filt_f[:, 0], skip[0].astype(F32))
    return x2 * _long_conv(z, filt_f[:, 1], skip[1].astype(F32))

def _ec_ffn(h, w_router, w_gate, w_up, w_down):
    B, T, D = h.shape
    cap = EC_CAPACITY_FACTOR * T // N_EXPERTS
    aff = jax.nn.softmax(jnp.einsum('btd,de->bte', h, w_router.astype(F32)), axis=-1)
    gate, idx = lax.top_k(jnp.swapaxes(aff, 1, 2), cap)
    xs = jax.vmap(lambda hb, ib: hb[ib])(h, idx)
    hid = (jax.nn.silu(jnp.einsum('becd,edf->becf', xs, w_gate.astype(F32)))
           * jnp.einsum('becd,edf->becf', xs, w_up.astype(F32)))
    out = jnp.einsum('becf,efd->becd', hid, w_down.astype(F32)) * gate[..., None]
    return jax.vmap(lambda ib, ob: jnp.zeros((T, D), ob.dtype).at[ib.reshape(-1)].add(ob.reshape(-1, D)))(idx, out)

def _trunk_layer(x, cond, p, layer_idx, ctx_k, ctx_v, s0):
    is_latent = ctx_k is not None
    B, L, _ = x.shape
    sh1, sc1, g1, sh2, sc2, g2 = _modulation(cond, p['w_mod'], p['b_mod'])
    h = _rmsnorm(x, p['norm_g'][0]) * (1.0 + sc1) + sh1
    z = jnp.einsum('bld,de->ble', h, p['w_in'].astype(F32))
    hq, hff, hfb, hi, hg, aq, ak, av, hy = _split_cols(z)

    if s0 is None:
        s0 = jnp.zeros((2, B, HG_HEADS, HG_DK, HG_DV), F32)
    o_hg, s_fin = _hgrn_mixer(hq, hff, hfb, hi, hg, p['lb'], s0.astype(F32), p['hgrn_norm_g'])

    qh = aq.reshape(B, L, DA_HEADS, 2, DA_DQK).transpose(0, 2, 3, 1, 4)
    kh = ak.reshape(B, L, DA_HEADS, 2, DA_DQK).transpose(0, 2, 3, 1, 4)
    vh = av.reshape(B, L, DA_HEADS, DA_DV).transpose(0, 2, 1, 3)
    if is_latent:
        qh = _axial_rope(qh)
        kh = _axial_rope(kh)
        keys = jnp.concatenate([kh, ctx_k.astype(F32)], axis=3)
        vals = jnp.concatenate([vh, ctx_v.astype(F32)], axis=2)
    else:
        keys, vals = kh, vh
    lam_init = 0.8 - 0.6 * math.exp(-0.3 * layer_idx)
    lv = p['diff_lambda'].astype(F32)
    lam = jnp.exp(jnp.sum(lv[0] * lv[1])) - jnp.exp(jnp.sum(lv[2] * lv[3])) + lam_init
    o_da = _diff_attention(qh, keys, vals, lam)
    o_da = _rmsnorm(o_da, p['diff_subln_g']) * (1.0 - lam_init)
    o_da = o_da.transpose(0, 2, 1, 3).reshape(B, L, DA_W)

    filt_f = _hyena_filters(L, p['hy_filt_w1'], p['hy_filt_b1'], p['hy_filt_w2'], p['hy_filt_b2'],
                            p['hy_filt_w3'], p['hy_filt_freq'])
    o_hy = _hyena_mixer(hy, filt_f, p['hy_skip'], p['hy_conv_w'], p['hy_conv_b'])

    mix = jnp.concatenate([o_hg, o_da, o_hy], axis=-1) @ p['w_out'].astype(F32)
    x = x + g1 * mix
    h2 = _rmsnorm(x, p['norm_g'][1]) * (1.0 + sc2) + sh2
    x = x + g2 * _ec_ffn(h2, p['w_router'], p['w_gate'], p['w_up'], p['w_down'])
    return x, kh, vh, s_fin

def setup_inputs(seed: int = 0) -> dict:
    key = jax.random.key(seed)
    ks = jax.random.split(key, 32)

    def nrm(k, shape, s):
        return jax.random.normal(k, shape, F32) * s

    return {
        'x_prompt': nrm(ks[0], (BATCH, SEQ, D_MODEL), 1.0),
        'x_sample': nrm(ks[1], (DEC_BATCH, DEC_SEQ, D_MODEL), 1.0),
        'c': nrm(ks[2], (DEC_BATCH, D_MODEL), 1.0),
        'cache_diff_k': nrm(ks[3], (DEC_BATCH, DEPTH, DA_HEADS, 2, PAST_LEN, DA_DQK), 1.0),
        'cache_diff_v': nrm(ks[4], (DEC_BATCH, DEPTH, DA_HEADS, PAST_LEN, DA_DV), 1.0),
        'state_hgrn': nrm(ks[5], (DEC_BATCH, DEPTH, 2, HG_HEADS, HG_DK, HG_DV), 0.5),
        'c_ctx': nrm(ks[6], (D_MODEL,), 1.0),
        'norm_g': 1.0 + nrm(ks[7], (DEPTH, 2, D_MODEL), 0.02),
        'final_norm_g': 1.0 + nrm(ks[8], (D_MODEL,), 0.02),
        'w_mod': nrm(ks[9], (DEPTH, D_MODEL, N_MOD * D_MODEL), 0.5 * D_MODEL ** -0.5),
        'b_mod': nrm(ks[10], (DEPTH, N_MOD * D_MODEL), 0.02),
        'w_in': nrm(ks[11], (DEPTH, D_MODEL, D_IN), D_MODEL ** -0.5),
        'w_out': nrm(ks[12], (DEPTH, D_MODEL, D_MODEL), D_MODEL ** -0.5),
        'hgrn_lb_logits': nrm(ks[13], (DEPTH, 2, HG_QK), 0.5),
        'hgrn_norm_g': 1.0 + nrm(ks[14], (DEPTH, HG_DV), 0.02),
        'diff_lambda': nrm(ks[15], (DEPTH, 4, DA_DQK), 0.1),
        'diff_subln_g': 1.0 + nrm(ks[16], (DEPTH, DA_DV), 0.02),
        'hy_conv_w': nrm(ks[17], (DEPTH, HY_SHORT, (HY_ORDER + 1) * HY_W), 0.5),
        'hy_conv_b': nrm(ks[18], (DEPTH, (HY_ORDER + 1) * HY_W), 0.02),
        'hy_filt_w1': nrm(ks[19], (DEPTH, HY_POS_EMB, HY_HIDDEN), HY_POS_EMB ** -0.5),
        'hy_filt_b1': nrm(ks[20], (DEPTH, HY_HIDDEN), 0.02),
        'hy_filt_w2': nrm(ks[21], (DEPTH, HY_HIDDEN, HY_HIDDEN), HY_HIDDEN ** -0.5),
        'hy_filt_b2': nrm(ks[22], (DEPTH, HY_HIDDEN), 0.02),
        'hy_filt_w3': nrm(ks[23], (DEPTH, HY_HIDDEN, 2 * HY_ORDER * HY_W), HY_HIDDEN ** -0.5),
        'hy_filt_freq': 1.0 + nrm(ks[24], (DEPTH, 2, HY_HIDDEN), 0.1),
        'hy_skip': nrm(ks[25], (DEPTH, HY_ORDER, HY_W), 0.5),
        'w_router': nrm(ks[26], (DEPTH, D_MODEL, N_EXPERTS), D_MODEL ** -0.5),
        'w_gate': nrm(ks[27], (DEPTH, N_EXPERTS, D_MODEL, D_FF_EXPERT), D_MODEL ** -0.5),
        'w_up': nrm(ks[28], (DEPTH, N_EXPERTS, D_MODEL, D_FF_EXPERT), D_MODEL ** -0.5),
        'w_down': nrm(ks[29], (DEPTH, N_EXPERTS, D_FF_EXPERT, D_MODEL), D_FF_EXPERT ** -0.5),
    }

def reference(x_prompt, x_sample, c, cache_diff_k, cache_diff_v, state_hgrn, c_ctx, norm_g, final_norm_g,
              w_mod, b_mod, w_in, w_out, hgrn_lb_logits, hgrn_norm_g, diff_lambda, diff_subln_g,
              hy_conv_w, hy_conv_b, hy_filt_w1, hy_filt_b1, hy_filt_w2, hy_filt_b2, hy_filt_w3, hy_filt_freq,
              hy_skip, w_router, w_gate, w_up, w_down):
    lb_cum = jnp.cumsum(jax.nn.softmax(hgrn_lb_logits.astype(F32), axis=0), axis=0)
    lb_all = lb_cum - lb_cum[:1]

    xp = x_prompt.astype(F32)
    xs = x_sample.astype(F32)
    cond_ctx = c_ctx.astype(F32)[None, :]
    cond_lat = c.astype(F32)
    new_k, new_v, new_s = [], [], []
    for l in range(DEPTH):
        p = {
            'norm_g': norm_g[l], 'w_mod': w_mod[l], 'b_mod': b_mod[l], 'w_in': w_in[l], 'w_out': w_out[l],
            'lb': lb_all[l], 'hgrn_norm_g': hgrn_norm_g[l], 'diff_lambda': diff_lambda[l],
            'diff_subln_g': diff_subln_g[l], 'hy_conv_w': hy_conv_w[l], 'hy_conv_b': hy_conv_b[l],
            'hy_filt_w1': hy_filt_w1[l], 'hy_filt_b1': hy_filt_b1[l], 'hy_filt_w2': hy_filt_w2[l],
            'hy_filt_b2': hy_filt_b2[l], 'hy_filt_w3': hy_filt_w3[l], 'hy_filt_freq': hy_filt_freq[l],
            'hy_skip': hy_skip[l], 'w_router': w_router[l], 'w_gate': w_gate[l], 'w_up': w_up[l],
            'w_down': w_down[l],
        }
        xp, k_ctx, v_ctx, s_ctx = _trunk_layer(xp, cond_ctx, p, l, None, None, None)
        new_k.append(k_ctx)
        new_v.append(v_ctx)
        new_s.append(jnp.swapaxes(s_ctx, 0, 1))
        xs, _, _, _ = _trunk_layer(xs, cond_lat, p, l, cache_diff_k[:, l], cache_diff_v[:, l],
                                   jnp.swapaxes(state_hgrn[:, l], 0, 1))

    y_prompt = _rmsnorm(xp, final_norm_g).astype(x_prompt.dtype)
    y_sample = _rmsnorm(xs, final_norm_g).astype(x_sample.dtype)
    new_cache_diff_k = jnp.stack(new_k, axis=1).astype(x_prompt.dtype)
    new_cache_diff_v = jnp.stack(new_v, axis=1).astype(x_prompt.dtype)
    new_state_hgrn = jnp.stack(new_s, axis=1).astype(x_prompt.dtype)
    return (y_prompt, y_sample, new_cache_diff_k, new_cache_diff_v, new_state_hgrn)


_drawn_inputs = setup_inputs


def setup_inputs(seed=0):
    import zlib

    import numpy as np

    out = dict(_drawn_inputs(seed))
    spreads = {}
    factors = {'state_hgrn': 8.0,
     'norm_g': 2.883,
     'final_norm_g': 8.679,
     'hgrn_norm_g': 8.0,
     'diff_lambda': 8.0,
     'diff_subln_g': 8.0,
     'hy_conv_b': 8.0,
     'hy_filt_w1': 2.741,
     'hy_filt_b1': 8.0,
     'hy_filt_b2': 8.0,
     'hy_filt_freq': 8.0,
     'cache_diff_k': 8.0,
     'cache_diff_v': 8.0}
    for name, (base, spread) in spreads.items():
        noise = np.random.default_rng([zlib.crc32(name.encode()), seed]).standard_normal(out[name].shape)
        drawn = base * np.exp(spread * noise) if base else spread * noise
        out[name] = jnp.asarray(drawn.astype(out[name].dtype))
    for name, factor in factors.items():
        out[name] = (out[name] * factor).astype(out[name].dtype)
    return out
```

```python
import math
from contextlib import ExitStack, contextmanager

import numpy as np

import concourse.bass as bass
from concourse import mybir

F32 = mybir.dt.float32
U32 = mybir.dt.uint32
I32 = mybir.dt.int32
ALU = mybir.AluOpType
ACT = mybir.ActivationFunctionType
AX = mybir.AxisListType

P = 128
D = 1024
KD = D // P
LAT, CTX = 1024, 128
TOK = LAT + CTX
NT = TOK // P
LT = LAT // P
DEPTH = 2
PAST = 256
D_IN = 3584
NMOD = 6
HEADS = 4
DQ = 64
DV = 128
HYW = 256
HID = 64
POS = 33
E = 16
CAP_L, CAP_P = 2 * LAT // E, 2 * CTX // E
CAP = CAP_L + CAP_P
FF = 1024
EPS = 1e-6
LEVELS = [64, 32, 16, 8, 4, 2, 1]
TC = 384
LAM_INIT = [0.8 - 0.6 * math.exp(-0.3 * l) for l in range(DEPTH)]


class Count:

    def __init__(self, sem):
        self.sem, self.n = sem, 0

    def done(self, ins):
        self.n += 1
        ins.then_inc(self.sem, 1)
        return self.n

    def then_wait(self, engine, ins):
        self.done(ins)
        engine.wait_ge(self.sem, self.n)


@contextmanager
def stage(nc, m, *names):
    with ExitStack() as ctx:
        sems = {n: ctx.enter_context(nc.semaphore(n)) for n in names if n[:3] != "sw_"}
        sems.update({n: m.sw_sems[n] for n in names if n[:3] == "sw_"})
        with nc.Block() as block:
            yield block, sems
        soft = [n for n in names if n[:3] == "sw_"]
        if soft:
            nc.gpsimd.dma_reset()
            nc.all_engine_barrier()
        for s in sems.values():
            nc.sync.sem_clear(s)
        nc.all_engine_barrier()


def modulation(nc, m, l):
    HB = 12
    wcols = NMOD * D // HB
    with stage(nc, m, "w_loaded0", "w_loaded1", "w_used", "small_loaded", "mod_ready", "mod_sum") as (block, s):
        @block.sync
        def _(sp):
            sp.dma_start(m.b_mod[:, :], m.d["b_mod"][l]).then_inc(s["small_loaded"], 16)
            sp.dma_start(m.norm_g[:, :], m.d["norm_g"][l]).then_inc(s["small_loaded"], 16)
            w = m.d["w_mod"][l].rearrange("(k p) (b n) -> b p k n", p=P, n=wcols)
            for b in range(HB):
                if b >= 2:
                    sp.wait_ge(s["w_used"], b - 1)
                sp.dma_start(m.W[:, b % 2], w[b]).then_inc(s[f"w_loaded{b % 2}"], 16)

        @block.tensor
        def _(pe):
            for b in range(HB):
                pe.wait_ge(s[f"w_loaded{b % 2}"], 16 * (b // 2 + 1))
                for j in range(wcols // P):
                    col = (b * (wcols // P) + j) * 2
                    for k in range(KD):
                        last = nc.tensor.matmul(m.ps[:, col:col + 2], m.W[:, b % 2, k, j * P:(j + 1) * P],
                                                m.cond[:, k, :], start=(k == 0), stop=(k == KD - 1))
                last.then_inc(s["w_used"], 1)

        @block.vector
        def _(dve):
            dve.wait_ge(s["small_loaded"], 32)
            dve.wait_ge(s["w_used"], HB)
            c = Count(s["mod_ready"])
            c.then_wait(dve, nc.vector.tensor_tensor(
                m.mod[:, :, :], m.ps[:, 0:2 * NMOD * KD].rearrange("p (j g) -> p j g", g=2),
                m.b_mod[:, :].unsqueeze(2).to_broadcast([P, NMOD * KD, 2]), ALU.add))
            for n in range(2):
                sc = m.mod[:, (3 * n + 1) * KD:(3 * n + 2) * KD, :]
                g = m.norm_g[:, n * KD:(n + 1) * KD].unsqueeze(2).to_broadcast([P, KD, 2])
                nc.vector.scalar_tensor_tensor(sc, sc, 1.0, g, ALU.add, ALU.mult)


def norm_to_channels(nc, m, n):
    shift, scale = 3 * n * KD, (3 * n + 1) * KD
    with stage(nc, m, "x_loaded0", "x_loaded1", "squared", "mean", "root", "row_scale", "row_normed", "transposed", "h_ready",
               "h_ready_act", "stored0", "stored1") as (block, s):
        @block.sync
        def _(sp):
            for t in range(NT):
                if t >= 2:
                    sp.wait_ge(s["transposed"], 2 * (t - 1))
                    if n == 1:
                        sp.wait_ge(s[f"stored{t % 2}"], 16 * (t // 2))
                sp.dma_start(m.xbuf[:, t % 2], m.x_dram[t * P:(t + 1) * P, :]).then_inc(s[f"x_loaded{t % 2}"], 16)

        @block.scalar
        def _(act):
            for t in range(NT):
                act.wait_ge(s[f"x_loaded{t % 2}"], 16 * (t // 2 + 1))
                if t >= 1:
                    act.wait_ge(s["squared"], t)
                nc.scalar.activation(m.sq[:, :], m.xbuf[:, t % 2], ACT.Square,
                                     accum_out=m.ss[:, t:t + 1]).then_inc(s["squared"], 1)
                act.wait_ge(s["mean"], t + 1)
                nc.scalar.activation(m.rt[:, t:t + 1], m.ms[:, t:t + 1], ACT.Sqrt).then_inc(s["root"], 1)
                g = 0 if t < LT else 1
                if n == 1:
                    act.wait_ge(s["row_normed"], t + 1)
                    act.dma_start(m.xn_dram[t * P:(t + 1) * P, :], m.xbuf[:, t % 2]).then_inc(s[f"stored{t % 2}"], 16)
                act.wait_ge(s["transposed"], 2 * t + 1)
                for k in range(4):
                    last = nc.scalar.activation(m.hT[:, k, t * P:(t + 1) * P], m.ps[:, (t % 2) * 1024 + k * P:
                                                                                    (t % 2) * 1024 + (k + 1) * P],
                                                ACT.Identity, bias=m.mod[:, shift + k, g:g + 1],
                                                scale=m.mod[:, scale + k, g:g + 1])
                last.then_inc(s["h_ready_act"], 1)
            if n == 1:
                act.wait_ge(s["stored0"], 16 * ((NT + 1) // 2))
                act.wait_ge(s["stored1"], 16 * (NT // 2))

        @block.vector
        def _(dve):
            c = Count(s["row_scale"])
            for t in range(NT):
                dve.wait_ge(s["squared"], t + 1)
                nc.vector.tensor_scalar(m.ms[:, t:t + 1], m.ss[:, t:t + 1], 1.0 / D, EPS, ALU.mult,
                                        ALU.add).then_inc(s["mean"], 1)
                dve.wait_ge(s["root"], t + 1)
                c.then_wait(dve, nc.vector.reciprocal(m.rs[:, t:t + 1], m.rt[:, t:t + 1]))
                nc.vector.tensor_scalar(m.xbuf[:, t % 2], m.xbuf[:, t % 2], m.rs[:, t:t + 1], None,
                                        ALU.mult).then_inc(s["row_normed"], 1)
                g = 0 if t < LT else 1
                dve.wait_ge(s["transposed"], 2 * t + 2)
                for k in range(4, 8):
                    last = nc.vector.tensor_scalar(m.hT[:, k, t * P:(t + 1) * P],
                                                   m.ps[:, (t % 2) * 1024 + k * P:(t % 2) * 1024 + (k + 1) * P],
                                                   m.mod[:, scale + k, g:g + 1], m.mod[:, shift + k, g:g + 1],
                                                   ALU.mult, ALU.add)
                last.then_inc(s["h_ready"], 1)

        @block.tensor
        def _(pe):
            for t in range(NT):
                pe.wait_ge(s["row_normed"], t + 1)
                if t >= 2:
                    pe.wait_ge(s["h_ready"], t - 1)
                    pe.wait_ge(s["h_ready_act"], t - 1)
                for k in range(KD):
                    last = nc.tensor.transpose(m.ps[:, (t % 2) * 1024 + k * P:(t % 2) * 1024 + (k + 1) * P],
                                               m.xbuf[:, t % 2, k * P:(k + 1) * P], m.ident[:, :])
                    if k in (3, 7):
                        last.then_inc(s["transposed"], 1)


def zc_slot(j):
    if j < 6:
        return "c", j
    if j < 10:
        return "t", (j - 6) * P
    if j < 18:
        return "c", j - 4
    if j < 22:
        return "t", (j - 14) * P
    return "d", j - 22


def projection(nc, m, l):
    NB, BC = 7, 4
    jobs = []
    for j in range(NB * BC):
        kind, at = zc_slot(j)
        if kind == "t":
            if j % 2 == 0:
                jobs += [("t", j, at, t) for t in range(NT)]
        else:
            jobs.append((kind, j, at, 0))
    chan = [x for x in jobs if x[0] != "t"]
    tok = [x for x in jobs if x[0] == "t"]
    with stage(nc, m, "w_loaded0", "w_loaded1", "w_used", "chan_done", "chan_taken", "tok_done", "tok_taken",
               "hy_stored0", "hy_stored1") as (block, s):
        w = m.d["w_in"][l].rearrange("(k p) (b n) -> b p k n", p=P, n=BC * P)
        first_hy = next(i for i, x in enumerate(chan) if x[0] == "d")

        @block.sync
        def _(sp):
            for b in range(NB):
                if b >= 2:
                    sp.wait_ge(s["w_used"], b - 1)
                sp.dma_start(m.W[:, b % 2], w[b]).then_inc(s[f"w_loaded{b % 2}"], 16)
            for i in range(6):
                sp.wait_ge(s["chan_taken"], first_hy + i + 1)
                sp.dma_start(m.zhy_dram[i * P:(i + 1) * P, :], m.zstage[:, i % 2]).then_inc(s[f"hy_stored{i % 2}"], 16)
            sp.wait_ge(s["hy_stored0"], 16 * 3)
            sp.wait_ge(s["hy_stored1"], 16 * 3)

        @block.tensor
        def _(pe):
            nchan = ntok = 0
            for kind, j, at, t in jobs:
                b, jj = divmod(j, BC)
                pe.wait_ge(s[f"w_loaded{b % 2}"], 16 * (b // 2 + 1))
                if kind != "t":
                    if nchan >= 2:
                        pe.wait_ge(s["chan_taken"], nchan - 1)
                    base = (nchan % 2) * 3 * 512
                    for q in range(3):
                        for k in range(KD):
                            last = nc.tensor.matmul(m.ps[:, base + q * 512:base + q * 512 + TC],
                                                    m.W[:, b % 2, k, jj * P:(jj + 1) * P],
                                                    m.hT[:, k, q * TC:(q + 1) * TC],
                                                    start=(k == 0), stop=(k == KD - 1))
                    last.then_inc(s["chan_done"], 1)
                    nchan += 1
                else:
                    if ntok >= 2:
                        pe.wait_ge(s["tok_taken"], ntok - 1)
                    base = (6 + ntok % 2) * 512
                    for k in range(KD):
                        last = nc.tensor.matmul(m.ps[:, base:base + 256], m.hT[:, k, t * P:(t + 1) * P],
                                                m.W[:, b % 2, k, jj * P:(jj + 2) * P],
                                                start=(k == 0), stop=(k == KD - 1))
                    last.then_inc(s["tok_done"], 1)
                    ntok += 1
                if jj == BC - 1 or (kind == "t" and jj == BC - 2 and t == NT - 1):
                    if kind == "t":
                        pe.wait_ge(s["tok_done"], ntok)
                    else:
                        pe.wait_ge(s["chan_done"], nchan)
                    pe.sem_inc(s["w_used"], 1)

        @block.scalar
        def _(act):
            for i, (kind, j, at, _) in enumerate(chan):
                act.wait_ge(s["chan_done"], i + 1)
                if kind == "d" and at >= 2:
                    act.wait_ge(s[f"hy_stored{at % 2}"], 16 * (at // 2))
                out = m.zc[:, at] if kind == "c" else m.zstage[:, at % 2]
                scale = DQ ** -0.5 if 10 <= j < 14 else 1.0
                base = (i % 2) * 3 * 512
                nc.scalar.activation(out.rearrange("p (q n) -> p q n", n=TC),
                                     m.ps[:, base:base + 1536].rearrange("p (q n) -> p q n", n=512)[:, :, 0:TC],
                                     ACT.Copy, scale=scale).then_inc(s["chan_taken"], 1)

        @block.vector
        def _(dve):
            for i, (_, j, at, t) in enumerate(tok):
                dve.wait_ge(s["tok_done"], i + 1)
                base = (6 + i % 2) * 512
                nc.vector.tensor_copy(m.zt[:, t, at:at + 256], m.ps[:, base:base + 256]).then_inc(s["tok_taken"], 1)

def hgrn_gates(nc, m, l):
    lb = m.lb
    with stage(nc, m, "loaded", "dve_small", "act_small", "softplus_x", "logsig", "keys", "diff",
               "softplus_d", "act_step", "gate_step") as (block, s):
        T1 = [m.qe[:, i] for i in range(4)]
        T2 = [m.ke_t.rearrange("p c i n -> p (c i n)")[:, i * TOK:(i + 1) * TOK] for i in range(4)]
        T3 = [m.A.rearrange("p i c n -> p (i c n)")[:, i * TOK:(i + 1) * TOK] for i in range(4)]
        f = [m.zc[:, 2 + i] for i in range(4)]

        @block.sync
        def _(sp):
            sp.dma_start(lb[:, 0:8], m.d["lb_logits"]).then_inc(s["loaded"], 16)
            sp.dma_start(m.lay[:, :], m.d["layer_const"][l].partition_broadcast(P)).then_inc(s["loaded"], 16)

        @block.vector
        def _(dve):
            c = Count(s["dve_small"])
            dve.wait_ge(s["loaded"], 32)
            c.then_wait(dve, nc.vector.tensor_tensor(lb[:, 8:12], lb[:, 4:8], lb[:, 0:4], ALU.subtract))
            c.then_wait(dve, nc.vector.scalar_tensor_tensor(lb[:, 12:16], lb[:, 8:12], -1.0, lb[:, 8:12],
                                                            ALU.mult, ALU.max))
            dve.wait_ge(s["act_small"], 2)
            c.then_wait(dve, nc.vector.scalar_tensor_tensor(lb[:, 16:20], lb[:, 8:12], 0.0, lb[:, 12:16],
                                                            ALU.min, ALU.subtract))
            c.then_wait(dve, nc.vector.scalar_tensor_tensor(lb[:, 20:24], lb[:, 8:12], 0.0, lb[:, 12:16],
                                                            ALU.max, ALU.add))
            c.then_wait(dve, nc.vector.tensor_scalar(lb[:, 24:28], lb[:, 16:20], m.lay[:, 0:1], m.lay[:, 1:2],
                                                     ALU.mult, ALU.add))
            c.then_wait(dve, nc.vector.tensor_scalar(lb[:, 28:32], lb[:, 20:24], m.lay[:, 0:1], -1.0,
                                                     ALU.mult, ALU.mult))
            c.then_wait(dve, nc.vector.tensor_tensor(lb[:, 32:36], lb[:, 28:32], lb[:, 24:28], ALU.subtract))
            for i in range(4):
                dve.wait_ge(s["softplus_x"], i + 1)
                nc.vector.scalar_tensor_tensor(T3[i], f[i], 0.0, T2[i], ALU.max, ALU.add)
                nc.vector.scalar_tensor_tensor(T1[i], f[i], 0.0, T2[i], ALU.min, ALU.subtract)\
                    .then_inc(s["logsig"], 1)
            dve.wait_ge(s["keys"], 4)
            g = Count(s["gate_step"])
            nc.vector.memset(m.A[:, :, :, 0], 0.0)
            for i in range(4):
                dve.wait_ge(s["diff"], i + 1)
                g.done(nc.vector.tensor_scalar(T1[i], T1[i], lb[:, 28 + i:29 + i], lb[:, 24 + i:25 + i],
                                               ALU.add, ALU.max))
            for i in range(4):
                dve.wait_ge(s["softplus_d"], i + 1)
                dve.wait_ge(s["gate_step"], i + 1)
                g.done(nc.vector.tensor_tensor(m.A[:, i, :, 1:], T1[i].rearrange("p (c t) -> p c t", t=P),
                                               T2[i].rearrange("p (c t) -> p c t", t=P), ALU.add))
            for i in range(4):
                dve.wait_ge(s["gate_step"], 4 + i + 1)
                for ch in range(NT):
                    nc.vector.tensor_tensor_scan(m.A[:, i, ch, 1:], m.ones[:, :], m.A[:, i, ch, 1:], 0.0,
                                                 ALU.mult, ALU.add)

        @block.scalar
        def _(act):
            c = Count(s["act_step"])
            act.wait_ge(s["dve_small"], 2)
            nc.scalar.activation(lb[:, 12:16], lb[:, 12:16], ACT.Exp, scale=-1.0).then_inc(s["act_small"], 1)
            act.wait_ge(s["act_small"], 1)
            nc.scalar.activation(lb[:, 12:16], lb[:, 12:16], ACT.Ln, bias=1.0).then_inc(s["act_small"], 1)

            def softplus(out):
                for i in range(4):
                    act.wait_ge(s["act_step"], c.n - 3)
                    c.done(nc.scalar.activation(T2[i], T2[i], ACT.Exp, scale=-1.0))
                for i in range(4):
                    act.wait_ge(s["act_step"], c.n - 3 + i)
                    nc.scalar.activation(T2[i], T2[i], ACT.Ln, bias=1.0).then_inc(s[out], 1)

            for i in range(4):
                c.done(nc.scalar.activation(T2[i], f[i], ACT.Abs))
            softplus("softplus_x")
            act.wait_ge(s["dve_small"], 7)
            for i in range(4):
                act.wait_ge(s["logsig"], i + 1)
                nc.scalar.activation(T2[i], T1[i], ACT.Abs, bias=lb[:, 32 + i:33 + i]).then_inc(s["diff"], 1)
            act.wait_ge(s["diff"], 4)
            softplus("softplus_d")
            for i in range(4):
                act.wait_ge(s["logsig"], i + 1)
                nc.scalar.activation(f[i], T3[i], ACT.Exp, bias=lb[:, 28 + i:29 + i], scale=-1.0)\
                    .then_inc(s["keys"], 1)


def hgrn_states(nc, m, l):
    def A(i, off):
        return m.A[:, i, :, off:off + P]

    def end(i):
        return m.A[:, i, :, P:P + 1].to_broadcast([P, NT, P])

    def tiles(x):
        return x.rearrange("p (c t) -> p c t", t=P)

    with stage(nc, m, "state_loaded", "rest", "from_a", "from_rest", "queries", "keys", "transposed", "keys_taken",
               "decay", "update", "chained", "stored", "cleared") as (block, s):
        steps = []
        for n in range(LT - 1):
            steps.append([(0, n), (1, LT - 1 - n)])
        steps.append([(0, LT), (1, LT)])

        @block.sync
        def _(sp):
            sp.wait_ge(s["cleared"], 1)
            for d in range(2):
                for ct in range(2):
                    for hh in range(2):
                        r, cols = slice(hh * DQ, (hh + 1) * DQ), slice(hh * DQ, (hh + 1) * DQ)
                        sp.dma_start(m.S[d][r, ct, 0 if d == 0 else LT - 1, cols], m.d["state"][l, d, ct, r, :])\
                            .then_inc(s["state_loaded"], 16)
            sp.wait_ge(s["chained"], 8 * LT)
            for d in range(2):
                for ct in range(2):
                    for hh in range(2):
                        r = slice(hh * DQ, (hh + 1) * DQ)
                        sp.dma_start(m.o["s"][l, d, 2 * ct + hh], m.S[d][r, ct, LT, r]).then_inc(s["stored"], 16)
            sp.wait_ge(s["stored"], 128)

        @block.gpsimd
        def _(pool):
            for d in range(2):
                last = nc.gpsimd.memset(m.S[d][:, :, :, :], 0.0)
            last.then_inc(s["cleared"], 1)

        @block.vector
        def _(dve):
            for i in range(4):
                if i >= 2:
                    dve.wait_ge(s["transposed"], i - 1)
                    dve.wait_ge(s["queries"], i - 1)
                if i < 2:
                    nc.vector.tensor_tensor(tiles(m.E[:, i % 2, 0:TOK]), end(i), A(i, 1), ALU.subtract)\
                        .then_inc(s["rest"], 1)
                else:
                    nc.vector.tensor_tensor(tiles(m.E[:, i % 2, 0:TOK]), end(i), A(i, 0), ALU.subtract)\
                        .then_inc(s["rest"], 1)
                wq, wk = (m.X, m.E) if i < 2 else (m.E, m.X)
                dve.wait_ge(s["from_a"], i + 1)
                dve.wait_ge(s["from_rest"], i + 1)
                nc.vector.tensor_tensor(m.qe[:, i], m.zc[:, i % 2], wq[:, i % 2, 0:TOK], ALU.mult)\
                    .then_inc(s["queries"], 1)
                nc.vector.tensor_tensor(wk[:, i % 2, 0:TOK], m.zc[:, 2 + i], wk[:, i % 2, 0:TOK], ALU.mult)\
                    .then_inc(s["keys"], 1)
            dve.wait_ge(s["state_loaded"], 128)
            dve.wait_ge(s["cleared"], 1)
            dve.wait_ge(s["decay"], 1)
            dve.wait_ge(s["update"], len(steps))
            for n, pair in enumerate(steps):
                for d, ch in pair:
                    for ct in range(2):
                        i = 2 * d + ct
                        if n and ch != LT:
                            dve.wait_ge(s["chained"], 8 * (n - 1) + 2 * i + 2)
                        for hh in range(2):
                            r = slice(hh * DQ, (hh + 1) * DQ)
                            u = m.ps[r, (n * 4 + i) * DQ:(n * 4 + i + 1) * DQ]
                            if ch == LT:
                                nc.vector.tensor_copy(m.S[d][r, ct, ch, r], u).then_inc(s["chained"], 1)
                            else:
                                nxt = ch + 1 if d == 0 else ch - 1
                                nc.vector.scalar_tensor_tensor(m.S[d][r, ct, nxt, r], m.S[d][r, ct, ch, r],
                                                               m.dec[r, i, ch:ch + 1], u, ALU.mult, ALU.add)\
                                    .then_inc(s["chained"], 1)

        @block.scalar
        def _(act):
            def take(i):
                act.wait_ge(s["transposed"], i + 1)
                nc.scalar.activation(m.ke_t[:, :, i, :],
                                     m.ps[:, (i % 2) * 1536:(i % 2) * 1536 + TOK].rearrange("p (c n) -> p c n", n=P),
                                     ACT.Copy).then_inc(s["keys_taken"], 1)
            nc.scalar.activation(m.dec[:, :, :], m.A[:, :, :, P], ACT.Exp).then_inc(s["decay"], 1)
            for i in range(4):
                if i >= 2:
                    take(i - 2)
                    act.wait_ge(s["queries"], i - 1)
                nc.scalar.activation(tiles(m.X[:, i % 2, 0:TOK]), A(i, 1 if i < 2 else 0), ACT.Exp)\
                    .then_inc(s["from_a"], 1)
                act.wait_ge(s["rest"], i + 1)
                nc.scalar.activation(m.E[:, i % 2, 0:TOK], m.E[:, i % 2, 0:TOK], ACT.Exp)\
                    .then_inc(s["from_rest"], 1)
            take(2)
            take(3)

        @block.tensor
        def _(pe):
            for i in range(4):
                pe.wait_ge(s["keys"], i + 1)
                if i >= 2:
                    pe.wait_ge(s["keys_taken"], i - 1)
                src = (m.E if i < 2 else m.X)[:, i % 2]
                for ch in range(NT):
                    at = (i % 2) * 1536 + ch * P
                    last = nc.tensor.transpose(m.ps[:, at:at + P], src[:, ch * P:(ch + 1) * P], m.ident[:, :])
                last.then_inc(s["transposed"], 1)
            pe.wait_ge(s["keys_taken"], 4)
            for n, pair in enumerate(steps):
                for d, ch in pair:
                    for ct in range(2):
                        i = 2 * d + ct
                        at = (n * 4 + i) * DQ
                        for hh in range(2):
                            h = 2 * ct + hh
                            last = nc.tensor.matmul(m.ps[hh * DQ:(hh + 1) * DQ, at:at + DQ],
                                                    m.ke_t[:, ch, i, hh * DQ:(hh + 1) * DQ],
                                                    m.zt[:, ch, h * DQ:(h + 1) * DQ], start=True, stop=True)
                last.then_inc(s["update"], 1)


def hgrn_outputs(nc, m, l):
    NL = len(LEVELS) + 2
    seq = [(ct, d, lev) for ct in range(2) for d in range(2) for lev in range(NL)]

    def halves(x, h):
        v = x.rearrange("p (c b two j) -> p c b two j", c=NT, two=2, j=h)
        return v[:, :, :, 0, :], v[:, :, :, 1, :]

    def q_half(x, d, h):
        return halves(x, h)[1 if d == 0 else 0]

    with stage(nc, m, "mask_loaded", "att_cleared", "span", "weight", "operand", "scores", "placed",
               "out_done", "out_taken") as (block, s):
        @block.sync
        def _(sp):
            sp.dma_start(m.mask[:, :, :, :], m.d["hg_mask"]).then_inc(s["mask_loaded"], 16)

        @block.vector
        def _(dve):
            dve.wait_ge(s["mask_loaded"], 16)

            def prepare(n):
                ct, d, lev = seq[n]
                if lev >= len(LEVELS):
                    return
                i, h, b = 2 * d + ct, LEVELS[lev], n % 2
                if n >= 2:
                    dve.wait_ge(s["scores"], n - 1)
                a = m.A[:, i]
                nb = P // (2 * h)
                lo, hi = halves(m.E[:, b, 0:TOK], h)
                mid = a[:, :, 0:P].rearrange("p c (b w) -> p c b w", w=2 * h)[:, :, :, h:h + 1]\
                    .to_broadcast([P, NT, nb, h])
                shift = 1 if d == 0 else 0
                w = a[:, :, shift:shift + P].rearrange("p c (b two j) -> p c b two j", two=2, j=h)
                left, right = w[:, :, :, 0, :], w[:, :, :, 1, :]
                nc.vector.tensor_tensor(lo, mid, left, ALU.subtract)
                nc.vector.tensor_tensor(hi, right, mid, ALU.subtract).then_inc(s["span"], 1)
                spans[n] = len(spans) + 1
                dve.wait_ge(s["weight"], spans[n])
                xlo, xhi = halves(m.X[:, b, 0:TOK], h)
                qlo, qhi = halves(m.zc[:, ct], h)
                klo, khi = halves(m.zc[:, 2 + i], h)
                x0, x1 = (klo, qhi) if d == 0 else (qlo, khi)
                nc.vector.tensor_tensor(xlo, lo, x0, ALU.mult)
                nc.vector.tensor_tensor(xhi, hi, x1, ALU.mult).then_inc(s["operand"], 1)

            def place(n):
                ct, d, lev = seq[n]
                dve.wait_ge(s["scores"], n + 1)
                if lev == 0:
                    dve.wait_ge(s["att_cleared"], 2 * ct + d + 1)
                else:
                    dve.wait_ge(s["placed"], n)
                att = m.att[:, d]
                dat = m.ps[:, (n % 2) * 2048:(n % 2 + 1) * 2048].rearrange("p (hh n) -> p hh n", hh=2)[:, :, 0:NT * 64]
                h = LEVELS[lev] if lev < len(LEVELS) else 1
                dat = dat.rearrange("p hh (c b j) -> p hh c b j", c=NT, j=h)
                msk = m.mask[:, d, lev].rearrange("p (b j) -> p b j", j=h)
                half = (1 if d == 0 else 0) if lev < len(LEVELS) else lev - len(LEVELS)
                out = att.rearrange("p hh c (b two j) -> p hh c b two j", two=2, j=h)[:, :, :, :, half, :]
                msk = msk.unsqueeze(1).unsqueeze(1).to_broadcast([P, 2, NT, 64 // h, h])
                nc.vector.copy_predicated(out, msk, dat).then_inc(s["placed"], 1)

            spans = {}
            prepare(0)
            for n in range(len(seq)):
                if n + 1 < len(seq):
                    prepare(n + 1)
                place(n)

        @block.gpsimd
        def _(pool):
            for ct in range(2):
                for d in range(2):
                    if ct:
                        pool.wait_ge(s["out_done"], 3)
                    nc.gpsimd.memset(m.att[:, d], 0.0).then_inc(s["att_cleared"], 1)

        @block.scalar
        def _(act):
            k = 0
            out_n = 0

            def take(ct):
                nonlocal out_n
                for c0 in range(0, NT, 4):
                    nch = min(4, NT - c0)
                    act.wait_ge(s["out_done"], out_n + 1)
                    at = c0 * P
                    nc.scalar.activation(m.o_sb[:, c0:c0 + nch, ct * P:(ct + 1) * P],
                                         m.ps[:, at:at + nch * P].rearrange("p (c n) -> p c n", n=P), ACT.Copy)\
                        .then_inc(s["out_taken"], 1)
                    out_n += 1
            for n, (ct, d, lev) in enumerate(seq):
                if lev < len(LEVELS):
                    k += 1
                    act.wait_ge(s["span"], k)
                    nc.scalar.activation(m.E[:, n % 2, 0:TOK], m.E[:, n % 2, 0:TOK], ACT.Exp)\
                        .then_inc(s["weight"], 1)
                if (ct, d, lev) == (1, 0, 0):
                    take(0)
            take(1)

        @block.tensor
        def _(pe):
            ops = 0
            for n, (ct, d, lev) in enumerate(seq):
                i = 2 * d + ct
                if n >= 2:
                    pe.wait_ge(s["placed"], n - 1)
                if lev < len(LEVELS):
                    ops += 1
                    pe.wait_ge(s["operand"], ops)
                for ch in range(NT):
                    for hh in range(2):
                        p0 = hh * DQ
                        at = (n % 2) * 2048 + hh * 1024 + ch * 64
                        if lev < len(LEVELS):
                            x = m.X[p0:p0 + DQ, n % 2, 0:TOK]
                            lhs = x[:, ch * P:(ch + 1) * P]
                            rhs = q_half(x, d, LEVELS[lev])[:, ch]
                        else:
                            lhs = m.zc[p0:p0 + DQ, 2 + i, ch * P:(ch + 1) * P]
                            rhs = m.zc[p0:p0 + DQ, ct, ch * P:(ch + 1) * P]\
                                .rearrange("p (j two) -> p j two", two=2)[:, :, lev - len(LEVELS)]
                        last = nc.tensor.matmul(m.ps[:, at:at + 64], lhs, rhs, start=True, stop=True)
                last.then_inc(s["scores"], 1)
                if (d, lev) != (1, NL - 1):
                    continue
                pe.wait_ge(s["placed"], n + 1)
                for ch in range(NT):
                    for hh in range(2):
                        h = 2 * ct + hh
                        out = m.ps[:, ch * P + hh * DQ:ch * P + (hh + 1) * DQ]
                        for dd in range(2):
                            last = nc.tensor.matmul(out, m.att[:, dd, hh, ch, :], m.zt[:, ch, h * DQ:(h + 1) * DQ],
                                                    start=(dd == 0), stop=(dd == 1 and ch == LT))
                        if ch < LT:
                            for dd in range(2):
                                last = nc.tensor.matmul(out, m.qe[:, 2 * dd + ct, ch * P:(ch + 1) * P],
                                                        m.S[dd][:, ct, ch, hh * DQ:(hh + 1) * DQ],
                                                        start=False, stop=(dd == 1))
                    if ch % 4 == 3 or ch == NT - 1:
                        last.then_inc(s["out_done"], 1)
                if ct == 0:
                    pe.wait_ge(s["out_taken"], 3)


def hgrn_finish(nc, m, l):
    n = NT * HEADS
    o4 = m.o_sb.rearrange("p c (h v) -> p c h v", v=DQ)
    sm = m.small[:, 0:n].rearrange("p (c h) -> p c h", h=HEADS)
    with stage(nc, m, "g_loaded", "step", "root", "gate", "out_ready", "transposed") as (block, s):
        sq = m.view(m.R_W, NT, 256)
        sq4 = sq.rearrange("p c (h v) -> p c h v", v=DQ)
        gate = m.view(m.R_W + NT * 256, NT, 256)

        @block.sync
        def _(sp):
            sp.dma_start(m.hg_gain[:, :], m.d["hgrn_norm_g"][l].partition_broadcast(P)).then_inc(s["g_loaded"], 16)

        @block.scalar
        def _(act):
            nc.scalar.activation(gate[:, :, :], m.zt[:, :, 256:512], ACT.Silu).then_inc(s["gate"], 1)
            act.wait_ge(s["step"], 3)
            nc.scalar.activation(m.small[:, 0:n], m.small[:, 0:n], ACT.Sqrt).then_inc(s["root"], 1)
            for ct in range(2):
                act.wait_ge(s["transposed"], ct + 1)
                nc.scalar.activation(m.oT[:, ct], m.ps[:, ct * 1536:ct * 1536 + TOK], ACT.Copy)

        @block.vector
        def _(dve):
            c = Count(s["step"])
            c.then_wait(dve, nc.vector.tensor_tensor(sq[:, :, :], m.o_sb[:, :, :], m.o_sb[:, :, :], ALU.mult))
            c.then_wait(dve, nc.vector.tensor_reduce(sm, sq4, AX.X, ALU.add))
            c.then_wait(dve, nc.vector.tensor_scalar(m.small[:, 0:n], m.small[:, 0:n], 1.0 / DQ, EPS, ALU.mult,
                                                     ALU.add))
            dve.wait_ge(s["root"], 1)
            c.then_wait(dve, nc.vector.reciprocal(m.small[:, 0:n], m.small[:, 0:n]))
            c.then_wait(dve, nc.vector.tensor_tensor(o4, o4, sm.unsqueeze(3).to_broadcast([P, NT, HEADS, DQ]),
                                                     ALU.mult))
            dve.wait_ge(s["g_loaded"], 16)
            c.then_wait(dve, nc.vector.tensor_tensor(o4, o4, m.hg_gain[:, :].unsqueeze(1).unsqueeze(1).to_broadcast([P, NT, HEADS, DQ]),
                                                     ALU.mult))
            dve.wait_ge(s["gate"], 1)
            nc.vector.tensor_tensor(m.o_sb[:, :, :], m.o_sb[:, :, :], gate[:, :, :], ALU.mult)\
                .then_inc(s["out_ready"], 1)

        @block.tensor
        def _(pe):
            pe.wait_ge(s["out_ready"], 1)
            for ct in range(2):
                for t in range(NT):
                    last = nc.tensor.transpose(m.ps[:, ct * 1536 + t * P:ct * 1536 + (t + 1) * P],
                                               m.o_sb[:, t, ct * P:(ct + 1) * P], m.ident[:, :])
                last.then_inc(s["transposed"], 1)

def attention_prepare(nc, m, l):
    with stage(nc, m, "tables_loaded", "keys_loaded", "values_loaded", "lambda_loaded", "shuffled", "turned", "kept",
               "transposed", "taken", "stored", "lam_step", "lam_exp") as (block, s):
        @block.sync
        def _(sp):
            sp.dma_start(m.cos[:, :], m.d["rope_cos"]).then_inc(s["tables_loaded"], 16)
            sp.dma_start(m.sin[:, :], m.d["rope_sin"]).then_inc(s["tables_loaded"], 16)
            sp.dma_start(m.lamv[:, :], m.d["diff_lambda"][l].partition_broadcast(P)).then_inc(s["lambda_loaded"], 16)
            for j in range(2):
                for h in range(HEADS):
                    sp.dma_start(m.kraw[:, j, h, :].rearrange("p (m d) -> p m d", d=DQ),
                                 m.d["cache_k"][l, h, :, j * P:(j + 1) * P, :].rearrange("m t d -> t m d"))\
                        .then_inc(s["keys_loaded"], 16)
            for j in range(2):
                sp.dma_start(m.vctx[:, j], m.d["cache_v"][l, :, j * P:(j + 1) * P, :].rearrange("h t v -> t h v"))\
                    .then_inc(s["values_loaded"], 16)
            sp.dma_start(m.o["v"][l].rearrange("h t v -> t h v"),
                         m.zt[:, LT, 512:1024].rearrange("p (h v) -> p h v", v=DV)).then_inc(s["stored"], 16)
            sp.wait_ge(s["taken"], 3)
            for h in range(HEADS):
                sp.dma_start(m.o["k"][l, h].rearrange("m t d -> t m d"),
                             m.kout[:, h].rearrange("p (m d) -> p m d", d=DQ)).then_inc(s["stored"], 16)
            sp.wait_ge(s["values_loaded"], 32)
            sp.wait_ge(s["stored"], 16 * (HEADS + 1))

        @block.gpsimd
        def _(pool):
            pool.wait_ge(s["tables_loaded"], 32)
            for i in range(8):
                pool.wait_ge(s["shuffled"], i + 1)
                x = m.zc[:, 6 + i, 0:LAT]
                nc.gpsimd.tensor_tensor(x, x, m.cos[:, :], ALU.mult).then_inc(s["kept"], 1)

        @block.vector
        def _(dve):
            c = Count(s["lam_step"])
            dve.wait_ge(s["lambda_loaded"], 16)
            v = m.lamv[:, :].rearrange("p (a b d) -> p a b d", a=2, b=2)
            c.then_wait(dve, nc.vector.tensor_tensor(v[:, :, 0], v[:, :, 0], v[:, :, 1], ALU.mult))
            c.then_wait(dve, nc.vector.tensor_reduce(m.lam[:, 0:2], v[:, :, 0], AX.X, ALU.add))
            dve.wait_ge(s["lam_exp"], 1)
            c.then_wait(dve, nc.vector.tensor_tensor(m.lam[:, 2:3], m.lam[:, 1:2], m.lam[:, 0:1], ALU.subtract))
            nc.vector.tensor_tensor(m.lam[:, 3:4], m.lam[:, 2:3], m.lay[:, 2:3], ALU.subtract)
            dve.wait_ge(s["tables_loaded"], 32)
            t = Count(s["turned"])
            for i in range(8):
                x = m.zc[:, 6 + i, 0:LAT]
                r = m.rot[:, i % 2]
                nc.vector.stream_shuffle(r, x, [(k + 16) % 32 for k in range(32)]).then_inc(s["shuffled"], 1)
                dve.wait_ge(s["shuffled"], i + 1)
                t.then_wait(dve, nc.vector.tensor_tensor(r, r, m.sin[:, :], ALU.mult))
                dve.wait_ge(s["kept"], i + 1)
                nc.vector.tensor_tensor(x, x, r, ALU.add)

        @block.scalar
        def _(act):
            act.wait_ge(s["lam_step"], 2)
            nc.scalar.activation(m.lam[:, 0:2], m.lam[:, 0:2], ACT.Exp).then_inc(s["lam_exp"], 1)
            for j in range(2):
                act.wait_ge(s["transposed"], j + 1)
                nc.scalar.activation(m.kctx[:, :, j * P:(j + 1) * P],
                                     m.ps[:, j * 512:(j + 1) * 512].rearrange("p (h n) -> p h n", n=P), ACT.Copy)\
                    .then_inc(s["taken"], 1)
            act.wait_ge(s["transposed"], 3)
            nc.scalar.activation(m.kout[:, :, :], m.ps[:, 1024:1536].rearrange("p (h n) -> p h n", n=P), ACT.Copy)\
                .then_inc(s["taken"], 1)

        @block.tensor
        def _(pe):
            pe.wait_ge(s["keys_loaded"], 16 * 8)
            for j in range(2):
                for h in range(HEADS):
                    last = nc.tensor.transpose(m.ps[:, j * 512 + h * P:j * 512 + (h + 1) * P], m.kraw[:, j, h, :],
                                               m.ident[:, :])
                last.then_inc(s["transposed"], 1)
            for h in range(HEADS):
                last = nc.tensor.transpose(m.ps[:, 1024 + h * P:1024 + (h + 1) * P], m.zc[:, 10 + h, LAT:TOK],
                                           m.ident[:, :])
            last.then_inc(s["transposed"], 1)


def attention(nc, m, l):
    jobs = [(qt, h) for qt in range(NT) for h in range(HEADS)]
    NJ = len(jobs)

    def pieces(qt, h, mp):
        r = slice(mp * DQ, (mp + 1) * DQ)
        if qt == LT:
            return [(0, m.zc[r, 10 + h, LAT:TOK])]
        return [(0, m.zc[r, 10 + h, 0:512]), (512, m.zc[r, 10 + h, 512:1024]), (1024, m.kctx[r, h, :])]

    def nkeys(qt):
        return CTX if qt == LT else LAT + PAST

    def rounds(qt):
        n = nkeys(qt) // P
        return [range(a, min(a + 4, n)) for a in range(0, n, 4)]

    first_round = [0]
    for qt, _ in jobs:
        first_round.append(first_round[-1] + len(rounds(qt)))

    with stage(nc, m, "score0", "score1", "max0", "max1", "prob0", "prob1", "ratio", "combined",
               "turned", "taken", "valued", "row_out") as (block, s):
        @block.tensor
        def _(pe):
            def score(n, mp):
                if n >= NJ:
                    return
                qt, h = jobs[n]
                if n:
                    pe.wait_ge(s[f"prob{mp}"], n)
                q = m.zc[mp * DQ:(mp + 1) * DQ, 6 + h, qt * P:(qt + 1) * P]
                for col, keys in pieces(qt, h, mp):
                    at = mp * 1536 + col
                    last = nc.tensor.matmul(m.ps[:, at:at + keys.shape[1]], q, keys, start=True, stop=True)
                last.then_inc(s[f"score{mp}"], 1)

            def turn(n, r):
                qt, h = jobs[n]
                if r >= len(rounds(qt)):
                    return
                g = first_round[n] + r
                if g:
                    pe.wait_ge(s["taken"], g)
                for k, j in enumerate(rounds(qt)[r]):
                    last = nc.tensor.transpose(m.ps[:, 3072 + k * P:3072 + (k + 1) * P],
                                               m.prob[:, n % 2, 0, j * P:(j + 1) * P], m.ident[:, :])
                last.then_inc(s["turned"], 1)

            score(0, 0)
            score(0, 1)
            for n, (qt, h) in enumerate(jobs):
                pe.wait_ge(s["combined"], n + 1)
                turn(n, 0)
                score(n + 1, 0)
                turn(n, 1)
                score(n + 1, 1)
                turn(n, 2)
                pe.wait_ge(s["taken"], first_round[n + 1])
                if n:
                    pe.wait_ge(s["row_out"], n)
                nk = nkeys(qt) // P
                for j in range(nk):
                    if qt == LT:
                        v = m.zt[:, LT, 512 + h * DV:512 + (h + 1) * DV]
                    elif j < LT:
                        v = m.zt[:, j, 512 + h * DV:512 + (h + 1) * DV]
                    else:
                        v = m.vctx[:, j - LT, h, :]
                    last = nc.tensor.matmul(m.ps[:, 3584:3584 + DV], m.aT[:, n % 2, j, :], v, start=(j == 0),
                                            stop=(j == nk - 1))
                last.then_inc(s["valued"], 1)

        @block.vector
        def _(dve):
            c = Count(s["ratio"])

            def maxima(n):
                if n >= NJ:
                    return
                for mp in range(2):
                    dve.wait_ge(s[f"score{mp}"], n + 1)
                    nc.vector.tensor_reduce(m.nmax[:, n, mp:mp + 1], m.ps[:, mp * 1536:mp * 1536 + nkeys(jobs[n][0])],
                                            AX.X, ALU.max, negate=True).then_inc(s[f"max{mp}"], 1)

            def combine(n):
                qt = jobs[n][0]
                p = m.prob[:, n % 2, :, 0:nkeys(qt)]
                dve.wait_ge(s["prob0"], n + 1)
                dve.wait_ge(s["prob1"], n + 1)
                c.then_wait(dve, nc.vector.reciprocal(m.rsum[:, n, :], m.sums[:, n, :]))
                c.then_wait(dve, nc.vector.scalar_tensor_tensor(m.mix[:, n:n + 1], m.sums[:, n, 0:1], m.lam[:, 3:4],
                                                                m.rsum[:, n, 1:2], ALU.mult, ALU.mult))
                nc.vector.scalar_tensor_tensor(p[:, 0], p[:, 1], m.mix[:, n:n + 1], p[:, 0], ALU.mult, ALU.add)\
                    .then_inc(s["combined"], 1)

            def out(n):
                qt, h = jobs[n]
                dve.wait_ge(s["valued"], n + 1)
                nc.vector.tensor_scalar(m.o_att[:, qt, h * DV:(h + 1) * DV], m.ps[:, 3584:3584 + DV],
                                        m.rsum[:, n, 0:1], None, ALU.mult).then_inc(s["row_out"], 1)

            maxima(0)
            for n in range(NJ):
                combine(n)
                maxima(n + 1)
                out(n)

        @block.scalar
        def _(act):
            def probs(n):
                if n >= NJ:
                    return
                if n >= 2:
                    act.wait_ge(s["turned"], first_round[n - 1])
                for mp in range(2):
                    act.wait_ge(s[f"max{mp}"], n + 1)
                    nk = nkeys(jobs[n][0])
                    nc.scalar.activation(m.prob[:, n % 2, mp, 0:nk], m.ps[:, mp * 1536:mp * 1536 + nk], ACT.Exp,
                                         bias=m.nmax[:, n, mp:mp + 1], accum_out=m.sums[:, n, mp:mp + 1])\
                        .then_inc(s[f"prob{mp}"], 1)

            probs(0)
            for n, (qt, h) in enumerate(jobs):
                for r, js in enumerate(rounds(qt)):
                    act.wait_ge(s["turned"], first_round[n] + r + 1)
                    if n >= 2 and r == 0:
                        act.wait_ge(s["valued"], n - 1)
                    nc.scalar.activation(m.aT[:, n % 2, js[0]:js[-1] + 1, :].rearrange("p a b -> p (a b)"),
                                         m.ps[:, 3072:3072 + len(js) * P], ACT.Copy).then_inc(s["taken"], 1)
                probs(n + 1)


def attention_finish(nc, m, l):
    n = NT * HEADS
    o4 = m.o_att.rearrange("p c (h v) -> p c h v", v=DV)
    sm = m.small[:, 0:n].rearrange("p (c h) -> p c h", h=HEADS)
    with stage(nc, m, "g_loaded", "step", "root", "out_ready", "transposed", "taken") as (block, s):
        sq = m.view(m.R_W, NT, 512)
        sq4 = sq.rearrange("p c (h v) -> p c h v", v=DV)

        @block.sync
        def _(sp):
            sp.dma_start(m.sub_gain[:, :], m.d["diff_subln_g"][l].partition_broadcast(P)).then_inc(s["g_loaded"], 16)

        @block.scalar
        def _(act):
            act.wait_ge(s["step"], 3)
            nc.scalar.activation(m.small[:, 0:n], m.small[:, 0:n], ACT.Sqrt).then_inc(s["root"], 1)
            for ct in range(4):
                act.wait_ge(s["transposed"], ct + 1)
                at = (ct % 2) * 1536
                nc.scalar.activation(m.oT[:, 2 + ct], m.ps[:, at:at + TOK], ACT.Copy).then_inc(s["taken"], 1)

        @block.vector
        def _(dve):
            c = Count(s["step"])
            c.then_wait(dve, nc.vector.tensor_tensor(sq[:, :, :], m.o_att[:, :, :], m.o_att[:, :, :], ALU.mult))
            c.then_wait(dve, nc.vector.tensor_reduce(sm, sq4, AX.X, ALU.add))
            c.then_wait(dve, nc.vector.tensor_scalar(m.small[:, 0:n], m.small[:, 0:n], 1.0 / DV, EPS, ALU.mult,
                                                     ALU.add))
            dve.wait_ge(s["root"], 1)
            c.then_wait(dve, nc.vector.reciprocal(m.small[:, 0:n], m.small[:, 0:n]))
            c.then_wait(dve, nc.vector.tensor_tensor(o4, o4, sm.unsqueeze(3).to_broadcast([P, NT, HEADS, DV]),
                                                     ALU.mult))
            dve.wait_ge(s["g_loaded"], 16)
            c.then_wait(dve, nc.vector.tensor_scalar(m.sub_gain[:, :], m.sub_gain[:, :], m.lay[:, 3:4], None,
                                                     ALU.mult))
            nc.vector.tensor_tensor(o4, o4, m.sub_gain[:, :].unsqueeze(1).unsqueeze(1)
                                    .to_broadcast([P, NT, HEADS, DV]), ALU.mult).then_inc(s["out_ready"], 1)

        @block.tensor
        def _(pe):
            pe.wait_ge(s["out_ready"], 1)
            for ct in range(4):
                if ct >= 2:
                    pe.wait_ge(s["taken"], ct - 1)
                for t in range(NT):
                    at = (ct % 2) * 1536 + t * P
                    last = nc.tensor.transpose(m.ps[:, at:at + P], m.o_att[:, t, ct * P:(ct + 1) * P], m.ident[:, :])
                last.then_inc(s["transposed"], 1)

MAGIC = 12582912.0
TWO_PI_HI = 6.28125
TWO_PI_LO = 2 * math.pi - 6.28125
PI_BELOW = 3.1415925


def hyena_filters(nc, m, l, g):
    L, nt = g.L, g.nt
    W = min(L, 512)
    halves = range(L // W)
    with stage(nc, m, "small_loaded", "decay_loaded", "biased", "hidden", "argued", "reduced", "sine", "taps_done",
               "taps", "magnitude", "mag_used", "folded", "copied", "table0", "table1", "summed", "norm",
               "spectrum", "taken", "edge") as (block, s):
        @block.sync
        def _(sp):
            for dst, src in ((m.hy_pos[0:POS, 0:L], g.pos), (m.hy_w1[0:POS, :], m.d["hy_w1"][l]),
                             (m.hy_w2[0:HID, :], m.d["hy_w2"][l]), (m.hy_w3[0:HID, :], m.d["hy_w3"][l]),
                             (m.hy_bf[0:HID, :], m.d["hy_bf"][l]), (m.alt[:, :], m.d["alt"])):
                sp.dma_start(dst, src).then_inc(s["small_loaded"], 16)
            sp.dma_start(m.decay[:, 0:nt, :], g.decay).then_inc(s["decay_loaded"], 16)
            for k in range(2 * nt):
                if k >= 2:
                    sp.wait_ge(s["spectrum"], k - 1)
                src = g.cos if k < nt else g.sin
                sp.dma_start(m.table[:, k % 2, 0:L], src[(k % nt) * P:(k % nt + 1) * P, :])\
                    .then_inc(s[f"table{k % 2}"], 16)

        @block.tensor
        def _(pe):
            pe.wait_ge(s["small_loaded"], 16 * 6)
            for h in halves:
                last = nc.tensor.matmul(m.ps[0:HID, h * 512:h * 512 + W], m.hy_w1[0:POS, :],
                                        m.hy_pos[0:POS, h * W:(h + 1) * W], start=True, stop=True)
            last.then_inc(s["hidden"], 1)
            pe.wait_ge(s["sine"], 1)
            for h in halves:
                last = nc.tensor.matmul(m.ps[0:HID, h * 512:h * 512 + W], m.hy_w2[0:HID, :],
                                        m.hy_h[0:HID, h * W:(h + 1) * W], start=True, stop=True)
            last.then_inc(s["hidden"], 1)
            pe.wait_ge(s["sine"], 2)

            def column_sums(t):
                pe.wait_ge(s["magnitude"], t + 1)
                for d in range(2):
                    last = nc.tensor.matmul(m.ps[:, 3584:4096], m.ones[:, :],
                                            m.mag[:, t % 2, d * 512:(d + 1) * 512],
                                            start=(t == 0 and d == 0), stop=(t == nt - 1 and d == 1))
                last.then_inc(s["mag_used"], 1)

            for t in range(nt):
                if t >= 2:
                    pe.wait_ge(s["taps"], t - 1)
                for d in range(2):
                    last = nc.tensor.matmul(m.ps[:, (t % 2) * 1024 + d * 512:(t % 2) * 1024 + (d + 1) * 512],
                                            m.hy_h[0:HID, t * P:(t + 1) * P], m.hy_w3[0:HID, d * 512:(d + 1) * 512],
                                            start=True, stop=True)
                last.then_inc(s["taps_done"], 1)
                if t:
                    column_sums(t - 1)
            column_sums(nt - 1)
            pe.wait_ge(s["norm"], 1)
            pe.wait_ge(s["copied"], nt)
            pe.wait_ge(s["folded"], 2 * nt)
            for part in range(2):
                if part:
                    pe.wait_ge(s["taken"], nt)
                for k in range(nt):
                    kk = part * nt + k
                    pe.wait_ge(s[f"table{kk % 2}"], 16 * (kk // 2 + 1))
                    for ft in range(nt):
                        last = nc.tensor.matmul(m.ps[:, ft * 512:(ft + 1) * 512],
                                                m.table[:, kk % 2, ft * P:(ft + 1) * P],
                                                m.hf[:, k, part * 512:(part + 1) * 512],
                                                start=(k == 0), stop=(k == nt - 1))
                    last.then_inc(s["spectrum"], 1)
            pe.wait_ge(s["taken"], 2 * nt)
            for k in range(nt):
                last = nc.tensor.matmul(m.ps[0:1, 0:512], m.alt[:, 0:1], m.hf[:, k, 0:512], start=(k == 0),
                                        stop=(k == nt - 1))
            last.then_inc(s["spectrum"], 1)

        @block.scalar
        def _(act):
            act.wait_ge(s["biased"], 1)
            for layer in range(2):
                act.wait_ge(s["hidden"], layer + 1)
                nc.scalar.activation(m.hy_a[0:HID, 0:L], m.ps[0:HID, 0:L], ACT.Identity,
                                     bias=m.hy_bf[0:HID, layer:layer + 1], scale=m.hy_bf[0:HID, 2 + layer:3 + layer])\
                    .then_inc(s["argued"], 1)
                act.wait_ge(s["reduced"], layer + 1)
                nc.scalar.activation(m.hy_h[0:HID, 0:L], m.hy_a[0:HID, 0:L], ACT.Sin).then_inc(s["sine"], 1)
            for t in range(nt):
                act.wait_ge(s["taps"], t + 1)
                if t >= 2:
                    act.wait_ge(s["mag_used"], t - 1)
                nc.scalar.activation(m.mag[:, t % 2, :], m.hf[:, t, :], ACT.Abs).then_inc(s["magnitude"], 1)
            for t in range(nt):
                act.wait_ge(s["folded"], 2 * t + 2)
                nc.scalar.activation(m.hf[:, t, 0:512], m.fold[:, t % 4, :], ACT.Copy).then_inc(s["copied"], 1)

        @block.vector
        def _(dve):
            dve.wait_ge(s["small_loaded"], 16 * 6)
            nc.vector.tensor_tensor(m.hy_bf[0:HID, 0:2], m.hy_bf[0:HID, 0:2], m.hy_bf[0:HID, 2:4], ALU.mult)\
                .then_inc(s["biased"], 1)
            a, k = m.hy_a[0:HID, 0:L], m.hy_k[0:HID, 0:L]
            c = Count(s["edge"])
            for layer in range(2):
                dve.wait_ge(s["argued"], layer + 1)
                c.then_wait(dve, nc.vector.tensor_scalar(k, a, 1.0 / (2 * math.pi), None, ALU.mult))
                c.then_wait(dve, nc.vector.tensor_scalar(k, k, MAGIC, None, ALU.add))
                c.then_wait(dve, nc.vector.tensor_scalar(k, k, MAGIC, None, ALU.subtract))
                c.then_wait(dve, nc.vector.scalar_tensor_tensor(a, k, -TWO_PI_HI, a, ALU.mult, ALU.add))
                c.then_wait(dve, nc.vector.scalar_tensor_tensor(a, k, -TWO_PI_LO, a, ALU.mult, ALU.add))
                nc.vector.tensor_scalar(a, a, PI_BELOW, -PI_BELOW, ALU.min, ALU.max).then_inc(s["reduced"], 1)
            dve.wait_ge(s["decay_loaded"], 16)
            for t in range(nt):
                dve.wait_ge(s["taps_done"], t + 1)
                nc.vector.tensor_tensor(m.hf[:, t, :].rearrange("p (a c) -> p a c", c=HYW),
                                        m.ps[:, (t % 2) * 1024:(t % 2 + 1) * 1024].rearrange("p (a c) -> p a c", c=HYW),
                                        m.decay[:, t, :].unsqueeze(1).to_broadcast([P, 4, HYW]), ALU.mult)\
                    .then_inc(s["taps"], 1)
            dve.wait_ge(s["mag_used"], nt)
            c.then_wait(dve, nc.vector.reciprocal(m.hy_rn[:, :], m.ps[:, 3584:4096]))
            nc.vector.tensor_scalar(m.hy_rn[:, :], m.hy_rn[:, :], 1.0 / L, None, ALU.mult).then_inc(s["norm"], 1)
            c.then_wait(dve, nc.vector.memset(m.hf[0:1, 0, 512:1024], 0.0))
            for t in range(nt):
                if t >= 4:
                    dve.wait_ge(s["copied"], t - 3)
                nc.vector.tensor_tensor(m.fold[:, t % 4, :], m.hf[:, t, 0:512], m.hf[:, t, 512:1024], ALU.add)\
                    .then_inc(s["folded"], 1)
                dve.wait_ge(s["folded"], 2 * t + 1)
                nc.vector.tensor_tensor(m.hf[:, t, 512:1024], m.hf[:, t, 0:512], m.hf[:, t, 512:1024],
                                        ALU.subtract).then_inc(s["folded"], 1)
            dve.wait_ge(s["norm"], 1)
            for part, f in enumerate((g.fre, g.fim)):
                dve.wait_ge(s["spectrum"], (part + 1) * nt)
                for ft in range(nt):
                    nc.vector.tensor_tensor(f[:, ft, :], m.ps[:, ft * 512:(ft + 1) * 512], m.hy_rn[:, :], ALU.mult)\
                        .then_inc(s["taken"], 1)
            dve.wait_ge(s["taken"], 2 * nt)
            c.then_wait(dve, nc.vector.memset(g.fim[0:1, 0, :], 0.0))
            c.then_wait(dve, nc.vector.tensor_copy(g.nyq[:, :], g.fre[:, 0, :]))
            c.then_wait(dve, nc.vector.tensor_scalar(g.fre[0:1, 0, :], g.fre[0:1, 0, :], 0.5, None, ALU.mult))
            dve.wait_ge(s["spectrum"], 2 * nt + 1)
            nc.vector.scalar_tensor_tensor(g.nyq[0:1, :], m.ps[0:1, 0:512], 0.5, m.hy_rn[0:1, :], ALU.mult, ALU.mult)


def hyena_short(nc, m, l):
    with stage(nc, m, "z_loaded0", "z_loaded1", "w_loaded", "tap", "mixed", "transposed", "taken") as (block, s):
        @block.sync
        def _(sp):
            for dst, src in ((m.hy_cw, "hy_conv_w"), (m.hy_cb, "hy_conv_b"), (m.hy_skip, "hy_skip")):
                sp.dma_start(dst[:, :], m.d[src][l]).then_inc(s["w_loaded"], 16)
            for n in range(2):
                sp.dma_start(m.zraw[:, 3 * n:3 * n + 3, :],
                             m.zhy_dram[3 * n * P:3 * (n + 1) * P, :].rearrange("(j p) t -> p j t", p=P))\
                    .then_inc(s[f"z_loaded{n}"], 16)

        @block.vector
        def _(dve):
            c = Count(s["tap"])
            dve.wait_ge(s["w_loaded"], 48)
            for j in range(6):
                dve.wait_ge(s[f"z_loaded{j // 3}"], 16)
                z, o = m.zraw[:, j], m.hv[:, j]
                w = [m.hy_cw[:, 3 * j + k:3 * j + k + 1] for k in range(3)]
                c.then_wait(dve, nc.vector.tensor_scalar(o, z, w[1], m.hy_cb[:, j:j + 1], ALU.mult, ALU.add))
                for a, b in ((0, LAT), (LAT, TOK)):
                    c.done(nc.vector.scalar_tensor_tensor(o[:, a + 1:b], z[:, a:b - 1], w[0], o[:, a + 1:b],
                                                          ALU.mult, ALU.add))
                dve.wait_ge(s["tap"], c.n)
                for a, b in ((0, LAT), (LAT, TOK)):
                    last = nc.vector.scalar_tensor_tensor(o[:, a:b - 1], z[:, a + 1:b], w[2], o[:, a:b - 1],
                                                          ALU.mult, ALU.add)
                    c.done(last)
            for j in range(2):
                dve.wait_ge(s["transposed"], j + 1)
                nc.vector.tensor_copy(m.hu[:, :, j * P:(j + 1) * P],
                                      m.ps[:, j * 1536:j * 1536 + TOK].rearrange("p (t n) -> p t n", n=P))

        @block.tensor
        def _(pe):
            for j in range(2):
                pe.wait_ge(s["tap"], 5 * (j + 1))
                for t in range(NT):
                    last = nc.tensor.transpose(m.ps[:, j * 1536 + t * P:j * 1536 + (t + 1) * P],
                                               m.hv[:, j, t * P:(t + 1) * P], m.ident[:, :])
                last.then_inc(s["transposed"], 1)


def hyena_conv(nc, m, l, g, order):
    L, nt, t0 = g.L, g.nt, g.t0
    W = min(L, 512)
    nh = L // W
    cols = slice(order * HYW, (order + 1) * HYW)
    ur = m.ps[:, 0:nt * HYW].rearrange("p (f c) -> p f c", c=HYW)
    ui = m.ps[:, 2048:2048 + nt * HYW].rearrange("p (f c) -> p f c", c=HYW)
    src = m.hv[:, 0:2, t0:t0 + L]
    gate = m.hv[:, 2 + 2 * order:4 + 2 * order, t0:t0 + L]
    with stage(nc, m, "fc0", "fc1", "fs0", "fs1", "forward", "product", "spectra", "inverse", "result",
               "transposed") as (block, s):
        @block.sync
        def _(sp):
            for k in range(2 * nt):
                if k >= 2:
                    sp.wait_ge(s["forward"], min(k - 1, nt))
                    if k - 2 >= nt:
                        sp.wait_ge(s["inverse"], k - 1 - nt)
                rows = slice((k % nt) * P, (k % nt + 1) * P)
                sp.dma_start(m.tcos[:, k % 2, 0:L], g.cos[rows, :]).then_inc(s[f"fc{k % 2}"], 16)
                sp.dma_start(m.tsin[:, k % 2, 0:L], (g.sin if k < nt else g.sin_t)[rows, :])\
                    .then_inc(s[f"fs{k % 2}"], 16)

        @block.tensor
        def _(pe):
            for k in range(nt):
                pe.wait_ge(s[f"fc{k % 2}"], 16 * (k // 2 + 1))
                pe.wait_ge(s[f"fs{k % 2}"], 16 * (k // 2 + 1))
                for table, out in ((m.tcos, ur), (m.tsin, ui)):
                    for ft in range(nt):
                        last = nc.tensor.matmul(out[:, ft, :], table[:, k % 2, ft * P:(ft + 1) * P],
                                                m.hu[:, t0 // P + k, :], start=(k == 0 and ft % 2 == 0),
                                                stop=(k == nt - 1), skip_group_check=True)
                last.then_inc(s["forward"], 1)
            pe.wait_ge(s["spectra"], 2)
            for k in range(nt):
                kk = nt + k
                pe.wait_ge(s[f"fc{kk % 2}"], 16 * (kk // 2 + 1))
                pe.wait_ge(s[f"fs{kk % 2}"], 16 * (kk // 2 + 1))
                for part, table in enumerate((m.tcos, m.tsin)):
                    for ct in range(2):
                        for h in range(nh):
                            at = (ct * 2 + h) * 512
                            last = nc.tensor.matmul(m.ps[:, at:at + W], m.hy[:, part, k, ct * P:(ct + 1) * P],
                                                    table[:, kk % 2, h * W:(h + 1) * W],
                                                    start=(k == 0 and part == 0), stop=(k == nt - 1 and part == 1))
                last.then_inc(s["inverse"], 1)
            if order == 0:
                pe.wait_ge(s["result"], 4)
                for ct in range(2):
                    for t in range(nt):
                        at = 2048 + ct * 1024 + t * P
                        last = nc.tensor.transpose(m.ps[:, at:at + P], src[:, ct, t * P:(t + 1) * P], m.ident[:, :])
                    last.then_inc(s["transposed"], 1)

        @block.vector
        def _(dve):
            fre, fim = g.fre[:, :, cols], g.fim[:, :, cols]
            yr, yi, tmp = m.hy[:, 0, 0:nt], m.hy[:, 1, 0:nt], m.htmp[:, 0:nt, :]
            dve.wait_ge(s["forward"], nt)
            c = Count(s["product"])
            c.done(nc.vector.tensor_tensor(yr, ur, fre, ALU.mult))
            c.then_wait(dve, nc.vector.tensor_tensor(tmp, ui, fim, ALU.mult))
            nc.vector.tensor_tensor(yr, yr, tmp, ALU.subtract).then_inc(s["spectra"], 1)
            dve.wait_ge(s["spectra"], 1)
            c.then_wait(dve, nc.vector.tensor_tensor(yi, ur, fim, ALU.mult))
            if nt > 1:
                c.done(nc.vector.tensor_tensor(tmp[:, 1:nt], ui[:, 1:nt], fre[:, 1:nt], ALU.mult))
            c.then_wait(dve, nc.vector.tensor_tensor(tmp[:, 0], ui[:, 0], g.nyq[:, cols], ALU.mult))
            nc.vector.tensor_tensor(yi, yi, tmp, ALU.add).then_inc(s["spectra"], 1)
            dve.wait_ge(s["inverse"], nt)
            r = Count(s["result"])
            for ct in range(2):
                y = m.ps[:, ct * 1024:ct * 1024 + L]
                r.then_wait(dve, nc.vector.scalar_tensor_tensor(src[:, ct], src[:, ct],
                                                                m.hy_skip[:, 2 * order + ct:2 * order + ct + 1], y,
                                                                ALU.mult, ALU.add))
                out = src[:, ct] if order == 0 else m.oT[:, 6 + ct, t0:t0 + L]
                r.done(nc.vector.tensor_tensor(out, src[:, ct], gate[:, ct], ALU.mult))
            if order == 0:
                for ct in range(2):
                    dve.wait_ge(s["transposed"], ct + 1)
                    nc.vector.tensor_copy(m.hu[:, t0 // P:t0 // P + nt, ct * P:(ct + 1) * P],
                                          m.ps[:, 2048 + ct * 1024:2048 + ct * 1024 + L]
                                          .rearrange("p (t n) -> p t n", n=P))


def hyena(nc, m, l):
    for g in (m.geo_lat, m.geo_ctx):
        hyena_filters(nc, m, l, g)
    hyena_short(nc, m, l)
    for g in (m.geo_lat, m.geo_ctx):
        for order in range(2):
            hyena_conv(nc, m, l, g, order)

def gate_rows(nc, m, block_engines, s, which):
    dve, pe = block_engines
    col = (3 * which + 2) * KD
    if dve is not None:
        c = 0
        for g in range(2):
            for k in range(KD):
                n = g * KD + k
                if n >= 4:
                    dve.wait_ge(s["diag_used"], n - 3)
                nc.vector.tensor_scalar(m.diag[:, n % 4, :], m.ident[:, :], m.mod[:, col + k, g:g + 1], None,
                                        ALU.mult).then_inc(s["diag"], 1)
    if pe is not None:
        for g in range(2):
            for k in range(KD):
                n = g * KD + k
                pe.wait_ge(s["diag"], n + 1)
                nc.tensor.matmul(m.ps[:, 2048 + n * P:2048 + (n + 1) * P], m.ones[:, :], m.diag[:, n % 4, :],
                                 start=True, stop=True).then_inc(s["diag_used"], 1)


def output_projection(nc, m, l):
    with stage(nc, m, "w_loaded", "x_loaded0", "x_loaded1", "x_loaded2", "diag", "diag_used", "rows_ready", "projected",
               "scaled", "updated", "stored0", "stored1", "stored2") as (block, s):
        @block.sync
        def _(sp):
            sp.dma_start(m.wo[:, :, :], m.d["w_out"][l].rearrange("(k p) n -> p k n", p=P)).then_inc(s["w_loaded"], 16)
            for t in range(NT):
                if t >= 3:
                    sp.wait_ge(s[f"stored{t % 3}"], 16 * (t // 3))
                sp.dma_start(m.xr[:, t % 3], m.x_dram[t * P:(t + 1) * P, :]).then_inc(s[f"x_loaded{t % 3}"], 16)

        @block.tensor
        def _(pe):
            gate_rows(nc, m, (None, pe), s, 0)
            pe.wait_ge(s["w_loaded"], 16)
            for t in range(NT):
                if t >= 2:
                    pe.wait_ge(s["scaled"], t - 1)
                for h in range(2):
                    for k in range(KD):
                        at = (t % 2) * 1024 + h * 512
                        last = nc.tensor.matmul(m.ps[:, at:at + 512], m.oT[:, k, t * P:(t + 1) * P],
                                                m.wo[:, k, h * 512:(h + 1) * 512], start=(k == 0), stop=(k == KD - 1))
                last.then_inc(s["projected"], 1)

        @block.vector
        def _(dve):
            gate_rows(nc, m, (dve, None), s, 0)
            dve.wait_ge(s["rows_ready"], 1)
            for t in range(NT):
                g = 0 if t < LT else 1
                dve.wait_ge(s["projected"], t + 1)
                if t >= 2:
                    dve.wait_ge(s["updated"], t - 1)
                nc.vector.tensor_tensor(m.dx[:, t % 2], m.ps[:, (t % 2) * 1024:(t % 2 + 1) * 1024], m.gb[:, g, :],
                                        ALU.mult).then_inc(s["scaled"], 1)
                dve.wait_ge(s[f"x_loaded{t % 3}"], 16 * (t // 3 + 1))
                dve.wait_ge(s["scaled"], t + 1)
                nc.vector.tensor_tensor(m.xr[:, t % 3], m.xr[:, t % 3], m.dx[:, t % 2], ALU.add)\
                    .then_inc(s["updated"], 1)

        @block.scalar
        def _(act):
            act.wait_ge(s["diag_used"], 16)
            nc.scalar.activation(m.gb.rearrange("p g n -> p (g n)"), m.ps[:, 2048:4096], ACT.Copy)\
                .then_inc(s["rows_ready"], 1)
            for t in range(NT):
                act.wait_ge(s["updated"], t + 1)
                act.dma_start(m.x_dram[t * P:(t + 1) * P, :], m.xr[:, t % 3]).then_inc(s[f"stored{t % 3}"], 16)
            for b in range(3):
                act.wait_ge(s[f"stored{b}"], 16 * 3)


def route(nc, m, l):
    with stage(nc, m, "w_loaded", "logits", "centred", "exps", "aff", "turned", "aff_t", "top", "found", "cast",
               "sel_turned", "sel_ready") as (block, s):
        RL, RP = CAP_L // 8, CAP_P // 8

        @block.sync
        def _(sp):
            sp.dma_start(m.wr[:, :, :], m.d["w_router"][l].rearrange("(k p) e -> p k e", p=P))\
                .then_inc(s["w_loaded"], 16)

        @block.tensor
        def _(pe):
            pe.wait_ge(s["w_loaded"], 16)
            for t in range(NT):
                for k in range(KD):
                    last = nc.tensor.matmul(m.ps[:, t * E:(t + 1) * E], m.hT[:, k, t * P:(t + 1) * P],
                                            m.wr[:, k, :], start=(k == 0), stop=(k == KD - 1))
            last.then_inc(s["logits"], 1)
            pe.wait_ge(s["aff"], 1)
            for t in range(NT):
                last = nc.tensor.transpose(m.ps[0:E, 512 + t * P:512 + (t + 1) * P], m.aff[:, t, :], m.ident[:, :])
            last.then_inc(s["turned"], 1)
            pe.wait_ge(s["cast"], 2)
            for n, src in enumerate((m.topv, m.topf)):
                nc.tensor.transpose(m.ps[:, 2048 + n * 32:2048 + n * 32 + E], src[0:E, 0:CAP_L], m.ident[0:E, 0:E])
                last = nc.tensor.transpose(m.ps[0:CAP_P, 2560 + n * 32:2560 + n * 32 + E], src[0:E, CAP_L:CAP],
                                           m.ident[0:E, 0:E])
            last.then_inc(s["sel_turned"], 1)

        @block.scalar
        def _(act):
            act.wait_ge(s["centred"], 1)
            nc.scalar.activation(m.aff[:, :, :], m.aff[:, :, :], ACT.Exp).then_inc(s["exps"], 1)
            act.wait_ge(s["turned"], 1)
            nc.scalar.activation(m.aff_t[0:E, :], m.ps[0:E, 512:512 + TOK], ACT.Copy).then_inc(s["aff_t"], 1)

        @block.vector
        def _(dve):
            c = Count(s["found"])
            sm = m.small[:, 0:NT]
            lg = m.ps[:, 0:NT * E].rearrange("p (t e) -> p t e", e=E)
            dve.wait_ge(s["logits"], 1)
            c.then_wait(dve, nc.vector.tensor_reduce(sm, lg, AX.X, ALU.max))
            nc.vector.tensor_tensor(m.aff[:, :, :], lg, sm.unsqueeze(2).to_broadcast([P, NT, E]), ALU.subtract)\
                .then_inc(s["centred"], 1)
            dve.wait_ge(s["exps"], 1)
            c.then_wait(dve, nc.vector.tensor_reduce(sm, m.aff[:, :, :], AX.X, ALU.add))
            c.then_wait(dve, nc.vector.reciprocal(sm, sm))
            nc.vector.tensor_tensor(m.aff[:, :, :], m.aff[:, :, :], sm.unsqueeze(2).to_broadcast([P, NT, E]),
                                    ALU.mult).then_inc(s["aff"], 1)
            dve.wait_ge(s["aff_t"], 1)
            for a, b, r0, rounds in ((0, LAT, 0, RL), (LAT, TOK, CAP_L, RP)):
                v = m.aff_t[0:E, a:b]
                for r in range(rounds):
                    best = m.topv[0:E, r0 + 8 * r:r0 + 8 * (r + 1)]
                    c.then_wait(dve, nc.vector.max(best, v))
                    c.done(nc.vector.max_index(m.topi[0:E, r0 + 8 * r:r0 + 8 * (r + 1)], best, v))
                    dve.wait_ge(s["found"], c.n)
                    c.then_wait(dve, nc.vector.match_replace(v, best, v, -1.0))
            nc.vector.tensor_copy(m.topf[0:E, 0:CAP_L], m.topi[0:E, 0:CAP_L]).then_inc(s["cast"], 1)
            nc.vector.tensor_scalar(m.topf[0:E, CAP_L:CAP], m.topi[0:E, CAP_L:CAP], float(LAT), None, ALU.add)\
                .then_inc(s["cast"], 1)
            dve.wait_ge(s["sel_turned"], 1)
            nc.vector.tensor_copy(m.gate_l[:, 0:E], m.ps[:, 2048:2048 + E])
            nc.vector.tensor_copy(m.idx_l[:, 0:E], m.ps[:, 2080:2080 + E])
            nc.vector.tensor_copy(m.gate_p[0:CAP_P, 0:E], m.ps[0:CAP_P, 2560:2560 + E])
            nc.vector.tensor_copy(m.idx_p[0:CAP_P, 0:E], m.ps[0:CAP_P, 2592:2592 + E])
            nc.vector.memset(m.idx_l[:, E:E + 1], 0)
            nc.vector.memset(m.idx_p[0:CAP_P, E:E + 1], 0)


def experts(nc, m, l):
    CH = ("gate0", "up0", "gate1", "up1", "down0", "down1")
    KG = [(0, 3), (3, 6), (6, 8)]
    names = [f"w_{c}" for c in CH] + [f"w_{c}_used" for c in CH]
    with stage(nc, m, *names, "zeros", "cleared", "index", "go", "sw_rows_l0", "sw_rows_l1", "sw_rows_p0", "sw_rows_p1", "rows_turned", "x_ready", "gu_done",
               "silu", "hid_ready", "down_done", "y_ready", "y_turned", "gates", "out_l", "out_p",
               "sw_scattered_l", "sw_scattered_p") as (block, s):

        @block.sync
        def _(sp):
            sp.wait_ge(s["zeros"], 1)
            for t in range(NT):
                sp.dma_start(m.acc_dram[t * P:(t + 1) * P, :], m.zero[:, :]).then_inc(s["cleared"], 16)
            wg = m.d["w_gate"][l].rearrange("(i j) (k p) (h n) -> i j h p k n", j=2, p=P, n=512)
            wu = m.d["w_up"][l].rearrange("(i j) (k p) (h n) -> i j h p k n", j=2, p=P, n=512)
            wd = m.d["w_down"][l].rearrange("(i j) (k p) (h n) -> i j h p k n", j=2, p=P, n=512)
            with sp.Fori(0, E // 2) as i:
                for j in range(2):
                    for c, (w, h) in enumerate(((wg, 0), (wu, 0), (wg, 1), (wu, 1), (wd, 0), (wd, 1))):
                        sp.wait_ge(s[f"w_{CH[c]}_used"], i * 2 + j + 1)
                        sp.dma_start(m.wbuf[:, c], w[i, j, h]).then_inc(s[f"w_{CH[c]}"], 16)

        @block.gpsimd
        def _(pool):
            nc.gpsimd.memset(m.zero[:, :], 0.0).then_inc(s["zeros"], 1)
            pool.wait_ge(s["cleared"], 16 * NT)

            def gather(e, j, first=False):
                if not first:
                    pool.wait_ge(s["rows_turned"], 6 * (e - 1) + 1)
                nc.gpsimd.tensor_copy(m.ib_l[:, j:j + 1], m.idx_l[:, bass.ds(e, 1)])
                nc.gpsimd.tensor_copy(m.ib_p[0:CAP_P, j:j + 1], m.idx_p[0:CAP_P, bass.ds(e, 1)])\
                    .then_inc(s["index"], 1)
                pool.wait_ge(s["index"], e + 1)
                pool.sem_inc(s["go"], 1)
                pool.indirect_dma_start(m.rows_l[:, j], None, m.xn_dram,
                                        bass.IndirectOffsetOnAxis(ap=m.ib_l[:, j:j + 1], axis=0))\
                    .then_inc(s[f"sw_rows_l{j}"], 16)
                pool.indirect_dma_start(m.rows_p[0:CAP_P, j], None, m.xn_dram,
                                        bass.IndirectOffsetOnAxis(ap=m.ib_p[0:CAP_P, j:j + 1], axis=0))\
                    .then_inc(s[f"sw_rows_p{j}"], 16)

            gather(0, 0, True)
            with pool.Fori(0, E // 2) as i:
                for j in range(2):
                    e = i * 2 + j
                    gather(e + 1, (j + 1) % 2)
                    pool.wait_ge(s["out_l"], e + 2)
                    pool.wait_ge(s["out_p"], e + 2)
                    pool.sem_inc(s["go"], 1)
                    pool.indirect_dma_start(m.acc_dram, bass.IndirectOffsetOnAxis(ap=m.ib_l[:, j:j + 1], axis=0),
                                            m.y_l[:, j], None, compute_op=ALU.add).then_inc(s["sw_scattered_l"], 16)
                    pool.indirect_dma_start(m.acc_dram,
                                            bass.IndirectOffsetOnAxis(ap=m.ib_p[0:CAP_P, j:j + 1], axis=0),
                                            m.y_p[0:CAP_P, j], None, compute_op=ALU.add)\
                        .then_inc(s["sw_scattered_p"], 16)
                    pool.wait_ge(s["sw_scattered_l"], e * 16 + 16)
                    pool.wait_ge(s["sw_scattered_p"], e * 16 + 16)
            pool.wait_ge(s["sw_rows_l0"], 16 * (E // 2 + 1))
            pool.wait_ge(s["sw_rows_p0"], 16 * (E // 2 + 1))

        @block.tensor
        def _(pe):
            def turn_rows(e, i, j):
                pe.wait_ge(s[f"sw_rows_l{j}"], (i + 1) * 16)
                pe.wait_ge(s[f"sw_rows_p{j}"], (i + 1) * 16)
                for g, (a, b) in enumerate(KG):
                    at0 = (6 + g % 2) * 512
                    pe.wait_ge(s["x_ready"], e * 3 + max(g - 1, 0) + 1)
                    for k in range(a, b):
                        at = at0 + (k - a) * CAP
                        nc.tensor.transpose(m.ps[:, at:at + CAP_L], m.rows_l[:, j, k * P:(k + 1) * P], m.ident[:, :])
                        last = nc.tensor.transpose(m.ps[:, at + CAP_L:at + CAP], m.rows_p[0:CAP_P, j, k * P:(k + 1) * P],
                                                   m.ident[0:CAP_P, 0:CAP_P])
                    last.then_inc(s["rows_turned"], 2)

            for n in [f"w_{c}_used" for c in CH] + ["rows_turned"]:
                pe.sem_inc(s[n], 1)
            with pe.Fori(0, E // 2) as i:
                for j in range(2):
                    e = i * 2 + j
                    turn_rows(e, i, j)
                    pe.wait_ge(s["x_ready"], e * 3 + 4)
                    pe.wait_ge(s["out_l"], e + 1)
                    pe.wait_ge(s["out_p"], e + 1)
                    for h in range(2):
                        pe.wait_ge(s[f"w_gate{h}"], (e + 1) * 16)
                        pe.wait_ge(s[f"w_up{h}"], (e + 1) * 16)
                        for q in range(4):
                            n = h * 4 + q
                            if n >= 2:
                                pe.wait_ge(s["hid_ready"], e * 8 + n)
                            for which in range(2):
                                at = ((n % 2) * 2 + which) * 512
                                for k in range(KD):
                                    last = nc.tensor.matmul(m.ps[:, at:at + CAP],
                                                            m.wbuf[:, 2 * h + which, k, q * P:(q + 1) * P],
                                                            m.xe[:, k, :], start=(k == 0), stop=(k == KD - 1))
                            last.then_inc(s["gu_done"], 1)
                        pe.wait_ge(s["gu_done"], e * 8 + h * 4 + 4)
                        pe.sem_inc(s[f"w_gate{h}_used"], 1)
                        pe.sem_inc(s[f"w_up{h}_used"], 1)
                    pe.wait_ge(s["hid_ready"], e * 8 + 9)
                    for h in range(2):
                        pe.wait_ge(s[f"w_down{h}"], (e + 1) * 16)
                        for q in range(4):
                            n = h * 4 + q
                            if n >= 2:
                                pe.wait_ge(s["y_ready"], e * 8 + n - 1)
                            at = (4 + n % 2) * 512
                            for k in range(KD):
                                last = nc.tensor.matmul(m.ps[:, at:at + CAP], m.wbuf[:, 4 + h, k, q * P:(q + 1) * P],
                                                        m.hid[:, k, :], start=(k == 0), stop=(k == KD - 1))
                            last.then_inc(s["down_done"], 1)
                        pe.wait_ge(s["down_done"], e * 8 + h * 4 + 4)
                        pe.sem_inc(s[f"w_down{h}_used"], 1)
                    pe.wait_ge(s["y_ready"], e * 8 + 8)
                    for k in range(KD):
                        last = nc.tensor.transpose(m.ps[:, k * P:(k + 1) * P], m.yT[:, k, 0:CAP_L], m.ident[:, :])
                    last.then_inc(s["y_turned"], 1)
                    for k in range(KD):
                        last = nc.tensor.transpose(m.ps[0:CAP_P, 1024 + k * P:1024 + (k + 1) * P],
                                                   m.yT[:, k, CAP_L:CAP], m.ident[:, :])
                    last.then_inc(s["y_turned"], 1)

        @block.scalar
        def _(act):
            act.sem_inc(s["out_p"], 1)
            with act.Fori(0, E // 2) as i:
                for j in range(2):
                    e = i * 2 + j
                    for n in range(8):
                        act.wait_ge(s["gu_done"], e * 8 + n + 1)
                        act.wait_ge(s["hid_ready"], e * 8 + max(n - 1, 0) + 1)
                        at = (n % 2) * 1024
                        nc.scalar.activation(m.sg[:, n % 2, :], m.ps[:, at:at + CAP], ACT.Silu)\
                            .then_inc(s["silu"], 1)
                    for n in range(8):
                        act.wait_ge(s["down_done"], e * 8 + n + 1)
                        at = (4 + n % 2) * 512
                        nc.scalar.activation(m.yT[:, n, :], m.ps[:, at:at + CAP], ACT.Copy).then_inc(s["y_ready"], 1)
                    act.wait_ge(s["y_turned"], e * 2 + 2)
                    act.wait_ge(s["gates"], e + 1)
                    nc.scalar.activation(m.y_p[0:CAP_P, j], m.ps[0:CAP_P, 1024:2048], ACT.Copy,
                                         scale=m.gb_p[0:CAP_P, j:j + 1]).then_inc(s["out_p"], 1)

        @block.vector
        def _(dve):
            for n in ("x_ready", "hid_ready", "out_l"):
                dve.sem_inc(s[n], 1)
            with dve.Fori(0, E // 2) as i:
                for j in range(2):
                    e = i * 2 + j
                    for g, (a, b) in enumerate(KG):
                        dve.wait_ge(s["rows_turned"], e * 6 + 2 * g + 3)
                        at0 = (6 + g % 2) * 512
                        for k in range(a, b):
                            for q, (c0, c1) in enumerate(((0, CAP_L), (CAP_L, CAP))):
                                at = at0 + (k - a) * CAP
                                last = nc.vector.tensor_scalar(m.xe[:, k, c0:c1], m.ps[:, at + c0:at + c1],
                                                               m.mod[:, 4 * KD + k, q:q + 1],
                                                               m.mod[:, 3 * KD + k, q:q + 1], ALU.mult, ALU.add)
                        last.then_inc(s["x_ready"], 1)
                    nc.vector.tensor_copy(m.gb_l[:, j:j + 1], m.gate_l[:, bass.ds(e, 1)])
                    nc.vector.tensor_copy(m.gb_p[0:CAP_P, j:j + 1], m.gate_p[0:CAP_P, bass.ds(e, 1)])\
                        .then_inc(s["gates"], 1)
                    for n in range(8):
                        dve.wait_ge(s["silu"], e * 8 + n + 1)
                        at = (n % 2) * 1024 + 512
                        nc.vector.tensor_tensor(m.hid[:, n, :], m.sg[:, n % 2, :], m.ps[:, at:at + CAP], ALU.mult)\
                            .then_inc(s["hid_ready"], 1)
                    dve.wait_ge(s["y_turned"], e * 2 + 1)
                    dve.wait_ge(s["gates"], e + 1)
                    nc.vector.tensor_scalar(m.y_l[:, j], m.ps[:, 0:1024], m.gb_l[:, j:j + 1], None, ALU.mult)\
                        .then_inc(s["out_l"], 1)


def expert_residual(nc, m, l):
    with stage(nc, m, "x_loaded0", "x_loaded1", "diag", "diag_used", "rows_ready", "scaled", "updated", "stored0",
               "stored1") as (block, s):
        @block.sync
        def _(sp):
            for t in range(NT):
                if t >= 2:
                    sp.wait_ge(s[f"stored{t % 2}"], 16 * (t // 2))
                sp.dma_start(m.xr[:, t % 2], m.x_dram[t * P:(t + 1) * P, :]).then_inc(s[f"x_loaded{t % 2}"], 16)
                sp.dma_start(m.dx[:, t % 2], m.acc_dram[t * P:(t + 1) * P, :]).then_inc(s[f"x_loaded{t % 2}"], 16)

        @block.tensor
        def _(pe):
            gate_rows(nc, m, (None, pe), s, 1)

        @block.vector
        def _(dve):
            gate_rows(nc, m, (dve, None), s, 1)
            dve.wait_ge(s["rows_ready"], 1)
            c = Count(s["scaled"])
            for t in range(NT):
                dve.wait_ge(s[f"x_loaded{t % 2}"], 32 * (t // 2 + 1))
                c.then_wait(dve, nc.vector.tensor_tensor(m.dx[:, t % 2], m.dx[:, t % 2],
                                                         m.gb[:, 0 if t < LT else 1, :], ALU.mult))
                nc.vector.tensor_tensor(m.xr[:, t % 2], m.xr[:, t % 2], m.dx[:, t % 2], ALU.add)\
                    .then_inc(s["updated"], 1)

        @block.scalar
        def _(act):
            act.wait_ge(s["diag_used"], 16)
            nc.scalar.activation(m.gb.rearrange("p g n -> p (g n)"), m.ps[:, 2048:4096], ACT.Copy)\
                .then_inc(s["rows_ready"], 1)
            for t in range(NT):
                act.wait_ge(s["updated"], t + 1)
                act.dma_start(m.x_dram[t * P:(t + 1) * P, :], m.xr[:, t % 2]).then_inc(s[f"stored{t % 2}"], 16)
            act.wait_ge(s["stored0"], 16 * ((NT + 1) // 2))
            act.wait_ge(s["stored1"], 16 * (NT // 2))


def epilogue(nc, m):
    with stage(nc, m, "g_loaded", "x_loaded0", "x_loaded1", "squared", "mean", "root", "inverse", "scaled", "gained",
               "stored0", "stored1") as (block, s):
        gain = m.gb[:, 0, :]

        @block.sync
        def _(sp):
            sp.dma_start(gain, m.d["final_norm_g"].partition_broadcast(P)).then_inc(s["g_loaded"], 16)
            for t in range(NT + 1):
                if t < NT:
                    if t >= 2:
                        sp.wait_ge(s[f"stored{t % 2}"], 16 * (t // 2))
                    sp.dma_start(m.xr[:, t % 2], m.x_dram[t * P:(t + 1) * P, :]).then_inc(s[f"x_loaded{t % 2}"], 16)
                if t:
                    u = t - 1
                    sp.wait_ge(s["gained"], u + 1)
                    sp.dma_start(m.o["x"][u * P:(u + 1) * P, :], m.xr[:, u % 2]).then_inc(s[f"stored{u % 2}"], 16)
            sp.wait_ge(s["stored0"], 16 * ((NT + 1) // 2))
            sp.wait_ge(s["stored1"], 16 * (NT // 2))

        @block.scalar
        def _(act):
            for t in range(NT):
                act.wait_ge(s[f"x_loaded{t % 2}"], 16 * (t // 2 + 1))
                if t:
                    act.wait_ge(s["squared"], t)
                nc.scalar.activation(m.dx[:, 0], m.xr[:, t % 2], ACT.Square, accum_out=m.ss[:, t:t + 1])\
                    .then_inc(s["squared"], 1)
                act.wait_ge(s["mean"], t + 1)
                nc.scalar.activation(m.rt[:, t:t + 1], m.ms[:, t:t + 1], ACT.Sqrt).then_inc(s["root"], 1)

        @block.vector
        def _(dve):
            c = Count(s["inverse"])
            dve.wait_ge(s["g_loaded"], 16)
            for t in range(NT):
                dve.wait_ge(s["squared"], t + 1)
                nc.vector.tensor_scalar(m.ms[:, t:t + 1], m.ss[:, t:t + 1], 1.0 / D, EPS, ALU.mult,
                                        ALU.add).then_inc(s["mean"], 1)
                dve.wait_ge(s["root"], t + 1)
                c.then_wait(dve, nc.vector.reciprocal(m.rs[:, t:t + 1], m.rt[:, t:t + 1]))
                nc.vector.scalar_tensor_tensor(m.xr[:, t % 2], m.xr[:, t % 2], m.rs[:, t:t + 1], gain,
                                               ALU.mult, ALU.mult).then_inc(s["gained"], 1)


def norm_two(nc, m, l):
    norm_to_channels(nc, m, 1)


class Mem:
    pass


ARENA = 52400


def build(nc, d, outs):
    m = Mem()
    m.d = d
    m.o = outs
    with ExitStack() as ctx:
        def sb(name, shape, dt=F32):
            return ctx.enter_context(nc.sbuf_tensor(name, shape, dt))

        m.ps = ctx.enter_context(nc.psum_tensor("ps", [P, 8 * 512], F32))
        m.ident = sb("ident", [P, P])
        m.ones = sb("ones", [P, P])
        m.cond = sb("cond", [P, KD, 2])
        m.mod = sb("mod", [P, NMOD * KD, 2])
        m.b_mod = sb("b_mod_sb", [P, NMOD * KD])
        m.norm_g = sb("norm_g_sb", [P, 2 * KD])
        m.ss, m.ms, m.rt, m.rs = (sb(n, [P, 16]) for n in ("ss", "ms", "rt", "rs"))
        m.small = sb("small", [P, 64])
        m.dec = sb("dec", [P, 4, NT])
        m.lb = sb("lb", [P, 36])
        m.lam = sb("lam", [P, 4])
        m.lay = sb("lay", [P, 4])
        m.hg_gain = sb("hg_gain", [P, DQ])
        arena = sb("arena", [P, ARENA])

        def view(at, *dims):
            n = int(np.prod(dims))
            assert at + n <= ARENA, (at, dims)
            a = arena[:, at:at + n]
            names = "abcd"[:len(dims)]
            if len(dims) == 1:
                return a
            return a.rearrange(f"p ({' '.join(names)}) -> p {' '.join(names)}", **dict(zip(names, dims)))
        m.view = view
        m.R_OT, m.R_ZC, m.R_ZT, m.R_W, m.R_FREE = 0, 9216, 25344, 34560, 42752
        m.hT = m.oT = view(m.R_OT, KD, TOK)
        m.zc = view(m.R_ZC, 14, TOK)
        m.zt = view(m.R_ZT, NT, D)
        m.W = view(m.R_W, 2, KD, 512)
        m.xbuf = view(m.R_W, 2, D)
        m.sq = view(m.R_W + 2 * D, D)
        m.qe = view(2 * TOK, 4, TOK)
        m.S = [view(6 * TOK, 2, NT, P), view(49572, 2, NT, P)]
        m.A = view(m.R_W, 4, NT, P + 1)
        m.X = view(39204, 2, TOK)
        m.E = view(41508, 2, TOK)
        m.ke_t = view(43812, NT, 4, P)
        m.att = view(43812, 2, 2, NT, P)
        m.mask = view(48420, 2, 9, 64).bitcast(U32)
        m.o_sb = m.zt[:, :, 0:256]
        m.kraw = view(34560, 2, HEADS, P)
        m.kctx = view(35584, HEADS, PAST)
        m.vctx = view(36608, 2, HEADS, DV)
        m.cos, m.sin = view(37632, LAT), view(38656, LAT)
        m.rot = view(39680, 2, LAT)
        m.prob = view(41728, 2, 2, LAT + PAST)
        m.aT = view(46848, 2, (LAT + PAST) // P, P)
        m.kout = view(49408, HEADS, P)
        m.lamv = view(49920, 4 * DQ)
        m.nmax, m.sums, m.rsum = (view(50176 + 80 * j, 40, 2) for j in range(3))
        m.mix = view(50416, 40)
        m.sub_gain = view(50456, DV)
        m.o_att = view(m.R_ZC, NT, 512)
        m.hy_pos, m.hy_h, m.hy_a, m.hy_k = (view(9216 + 1024 * j, 1024) for j in range(4))
        m.hy_w3 = view(13312, 1024)
        m.hy_w1, m.hy_w2 = view(14336, HID), view(14400, HID)
        m.hy_bf = view(14464, 4)
        m.mag = view(16128, 2, 1024)
        m.fold = view(18176, 4, 512)
        m.decay = view(20224, LT, HYW)
        m.zraw = view(9216, 6, TOK)
        m.hv = view(16128, 6, TOK)
        m.hf = view(23040, LT, 1024)
        m.hy = view(23040, 2, LT, HYW)
        m.htmp = view(27136, LT, HYW)
        m.table = view(43520, 2, 1024)
        m.tcos, m.tsin = m.table, view(45568, 2, 1024)
        m.hu = view(47616, NT, HYW)
        m.hy_rn = view(49920, 512)
        m.alt = sb("alt_sb", [P, 1])
        m.hy_cw, m.hy_cb, m.hy_skip = sb("hy_cw", [P, 18]), sb("hy_cb", [P, 6]), sb("hy_sk", [P, 4])

        def geometry(name, length, t0, at, nyq_at):
            g = Mem()
            n = length // P
            g.L, g.nt, g.t0 = length, n, t0
            g.fre, g.fim, g.nyq = view(at, n, 512), view(at + 512 * n, n, 512), view(nyq_at, 512)
            g.pos, g.decay, g.cos, g.sin, g.sin_t = (d[f"{k}_{name}"] for k in
                                                     ("pos", "decay", "dft_cos", "dft_sin", "dft_sin_t"))
            return g
        m.geo_lat = geometry("lat", LAT, 0, 31232, 39424)
        m.geo_ctx = geometry("ctx", CTX, LAT, 39936, 40960)
        m.wo = view(m.R_W, KD, D)
        m.xr = view(9216, 3, D)
        m.dx = view(12288, 2, D)
        m.gb = view(14336, 2, D)
        m.diag = view(16384, 4, P)
        m.wr = view(9216, KD, E)
        m.aff = view(9344, NT, E)
        m.aff_t = view(9488, TOK)
        m.topv, m.topf = view(10640, CAP), view(10784, CAP)
        m.topi = view(10928, CAP).bitcast(U32)
        m.gate_l, m.gate_p = view(11072, E), view(11088, E)
        m.idx_l, m.idx_p = view(11104, E + 1).bitcast(I32), view(11121, E + 1).bitcast(I32)
        m.ib_l, m.ib_p = view(11138, 2).bitcast(I32), view(11140, 2).bitcast(I32)
        m.gb_l, m.gb_p = view(11142, 2), view(11144, 2)
        m.zero = view(11264, D)
        m.rows_l, m.rows_p = view(12288, 2, D), view(14336, 2, D)
        m.y_l, m.y_p = view(16384, 2, D), view(18432, 2, D)
        m.xe, m.hid, m.yT = (view(20480 + 1152 * j, KD, CAP) for j in range(3))
        m.sg = view(23936, 2, CAP)
        m.wbuf = view(24576, 6, KD, 512)
        m.acc_dram = nc.dram_tensor("expert_sum", (TOK, D), F32, kind="Internal").ap()
        m.zstage = view(m.R_FREE, 2, TOK)

        m.x_dram = nc.dram_tensor("x_rows", (TOK, D), F32, kind="Internal").ap()
        m.xn_dram = nc.dram_tensor("x_normed", (TOK, D), F32, kind="Internal").ap()
        m.zhy_dram = nc.dram_tensor("z_hyena", (6 * P, TOK), F32, kind="Internal").ap()
        m.sw_sems = {n: ctx.enter_context(nc.semaphore(n)) for n in
                     ("sw_rows_l0", "sw_rows_l1", "sw_rows_p0", "sw_rows_p1", "sw_scattered_l", "sw_scattered_p")}
        prologue(nc, m)
        with nc.Fori(0, DEPTH) as l:
            modulation(nc, m, l)
            norm_to_channels(nc, m, 0)
            projection(nc, m, l)
            hgrn_gates(nc, m, l)
            hgrn_states(nc, m, l)
            hgrn_outputs(nc, m, l)
            hgrn_finish(nc, m, l)
            attention_prepare(nc, m, l)
            attention(nc, m, l)
            attention_finish(nc, m, l)
            hyena(nc, m, l)
            output_projection(nc, m, l)
            norm_two(nc, m, l)
            route(nc, m, l)
            experts(nc, m, l)
            expert_residual(nc, m, l)
        epilogue(nc, m)


def prologue(nc, m):
    with stage(nc, m, "loaded", "copied", "silu") as (block, s):
        @block.sync
        def _(sp):
            sp.dma_start(m.x_dram, m.d["x"]).then_inc(s["copied"], 16)
            sp.dma_start(m.cond[:, :, :], m.d["cond"]).then_inc(s["loaded"], 16)
            sp.dma_start(m.ident[:, :], m.d["ident"]).then_inc(s["loaded"], 16)
            sp.wait_ge(s["copied"], 16)
            sp.wait_ge(s["loaded"], 32)

        @block.vector
        def _(dve):
            nc.vector.memset(m.ones[:, :], 1.0)

        @block.scalar
        def _(act):
            act.wait_ge(s["loaded"], 32)
            nc.scalar.activation(m.cond[:, :, :], m.cond[:, :, :], ACT.Silu)


def host_arrays(i):
    f = np.float32
    a = {}
    a["x"] = np.concatenate([i["x_sample"][0], i["x_prompt"][0]], axis=0)
    a["cond"] = np.ascontiguousarray(np.stack([i["c"][0], i["c_ctx"]], axis=-1).reshape(KD, P, 2).transpose(1, 0, 2))
    a["w_mod"] = i["w_mod"]
    a["b_mod"] = np.ascontiguousarray(i["b_mod"].reshape(DEPTH, NMOD * KD, P).transpose(0, 2, 1))
    a["norm_g"] = np.ascontiguousarray(i["norm_g"].reshape(DEPTH, 2 * KD, P).transpose(0, 2, 1))
    a["w_in"] = i["w_in"]
    a["ident"] = np.eye(P, dtype=f)
    a["lb_logits"] = np.ascontiguousarray(i["hgrn_lb_logits"].reshape(DEPTH * 4, P).T)
    a["layer_const"] = np.array([[min(l, 1), (min(l, 1) - 1) * 1e30, LAM_INIT[l], 1 - LAM_INIT[l]]
                                 for l in range(2)], dtype=f)
    a["state"] = i["state_hgrn"][0].reshape(2, 2, 2, P, DQ)
    a["hgrn_norm_g"] = i["hgrn_norm_g"]
    mask = np.zeros((P, 2, len(LEVELS) + 2, 64), np.uint32)
    key = np.arange(P)[:, None]
    col = np.arange(64)
    for n, h in enumerate(LEVELS):
        blk = (col // h)[None]
        mask[:, 0, n] = (key // (2 * h) == blk) & (key % (2 * h) < h)
        mask[:, 1, n] = (key // (2 * h) == blk) & (key % (2 * h) >= h)
    for par in range(2):
        mask[:, :, len(LEVELS) + par] = (key == 2 * col + par)[:, None]
    a["hg_mask"] = mask
    pos = np.arange(LAT)
    sub = np.arange(P) % DQ
    inv = (f(10000.0) ** (-np.arange(0, 32, 2).astype(f) / f(32))).astype(f)
    where = np.where((sub < 32)[:, None], (pos // 64)[None], (pos % 64)[None]).astype(f)
    ang = where * inv[sub % 16][:, None]
    a["rope_cos"] = np.cos(ang).astype(f)
    a["rope_sin"] = (np.sin(ang) * np.where(sub % 32 < 16, -1, 1)[:, None]).astype(f)
    a["cache_k"] = i["cache_diff_k"][0]
    a["cache_v"] = i["cache_diff_v"][0]
    a["diff_lambda"] = i["diff_lambda"].reshape(DEPTH, 4 * DQ)
    a["diff_subln_g"] = i["diff_subln_g"]
    a["hy_w1"], a["hy_w2"], a["hy_w3"] = i["hy_filt_w1"], i["hy_filt_w2"], i["hy_filt_w3"]
    a["hy_bf"] = np.stack([i["hy_filt_b1"], i["hy_filt_b2"], i["hy_filt_freq"][:, 0], i["hy_filt_freq"][:, 1]], axis=-1)
    a["hy_conv_w"] = np.ascontiguousarray(i["hy_conv_w"].reshape(DEPTH, 3, 6, P).transpose(0, 3, 2, 1).reshape(DEPTH, P, 18))
    a["hy_conv_b"] = np.ascontiguousarray(i["hy_conv_b"].reshape(DEPTH, 6, P).transpose(0, 2, 1))
    a["hy_skip"] = np.ascontiguousarray(i["hy_skip"].reshape(DEPTH, 4, P).transpose(0, 2, 1))
    a["alt"] = np.where(np.arange(P) % 2, -1, 1).astype(f)[:, None]
    lo, hi = math.log(1e-2) / 1.5, math.log(1e-2) / 0.3
    deltas = np.linspace(lo, hi, HYW, dtype=f)
    for name, length in (("lat", LAT), ("ctx", CTX)):
        t = np.linspace(0.0, 1.0, length, dtype=f)[:, None]
        fr = np.linspace(1e-4, (POS - 1) // 2 - 1, (POS - 1) // 2, dtype=f)[None]
        w = (f(2.0 * math.pi) * np.arange(length, dtype=f)[:, None] / f(length)).astype(f)
        a[f"pos_{name}"] = np.ascontiguousarray(np.concatenate([t, np.cos(fr * w), -np.sin(fr * w)], axis=-1).T)
        a[f"decay_{name}"] = np.ascontiguousarray(np.exp(-t * np.abs(deltas)).astype(f)
                                                  .reshape(length // P, P, HYW).transpose(1, 0, 2))
        n = np.arange(length)
        ang = np.pi * (np.outer(n, n) % (2 * length)) / length
        a[f"dft_cos_{name}"] = np.cos(ang).astype(f)
        sin = np.sin(ang)
        sin[:, 0] = np.where(n % 2, -1, 1)
        a[f"dft_sin_{name}"] = sin.astype(f)
        a[f"dft_sin_t_{name}"] = np.ascontiguousarray(sin.T.astype(f))
    for n in ("w_out", "w_router", "w_gate", "w_up", "w_down", "final_norm_g"):
        a[n] = i[n]
    return a


OUTS = {"x": (TOK, D), "k": (DEPTH, HEADS, 2, CTX, DQ), "v": (DEPTH, HEADS, CTX, DV),
        "s": (DEPTH, 2, HEADS, DQ, DQ)}


def kernel(**inputs):
    import concourse.bacc as bacc
    from concourse.bass_utils import run_bass_kernel_spmd

    nc = bacc.Bacc("TRN2", target_bir_lowering=False, num_devices=1)
    arrays = {n: np.ascontiguousarray(a) for n, a in host_arrays(inputs).items()}
    ins = {n: nc.dram_tensor("in_" + n, a.shape, mybir.dt.from_np(a.dtype), kind="ExternalInput").ap()
           for n, a in arrays.items()}
    outs = {n: nc.dram_tensor("out_" + n, shape, F32, kind="ExternalOutput").ap() for n, shape in OUTS.items()}
    build(nc, ins, outs)
    r = run_bass_kernel_spmd(nc, [{"in_" + n: a for n, a in arrays.items()}], core_ids=[0]).results[0]
    x = r["out_x"]
    return (x[LAT:][None], x[:LAT][None], r["out_k"][None], r["out_v"][None], r["out_s"][None])
```

```python
import math
from contextlib import ExitStack, contextmanager

import numpy as np

import concourse.bass as bass
from concourse import mybir

F32 = mybir.dt.float32
U32 = mybir.dt.uint32
I32 = mybir.dt.int32
ALU = mybir.AluOpType
ACT = mybir.ActivationFunctionType
AX = mybir.AxisListType

P = 128
D = 1024
KD = D // P
LAT, CTX = 1024, 128
TOK = LAT + CTX
NT = TOK // P
LT = LAT // P
DEPTH = 2
PAST = 256
D_IN = 3584
NMOD = 6
HEADS = 4
DQ = 64
DV = 128
HYW = 256
HID = 64
POS = 33
E = 16
CAP_L, CAP_P = 2 * LAT // E, 2 * CTX // E
CAP = CAP_L + CAP_P
FF = 1024
EPS = 1e-6
LEVELS = [64, 32, 16, 8, 4, 2, 1]
TC = 384
LAM_INIT = [0.8 - 0.6 * math.exp(-0.3 * l) for l in range(DEPTH)]


class Count:

    def __init__(self, sem):
        self.sem, self.n = sem, 0

    def done(self, ins):
        self.n += 1
        ins.then_inc(self.sem, 1)
        return self.n

    def then_wait(self, engine, ins):
        self.done(ins)
        engine.wait_ge(self.sem, self.n)


@contextmanager
def stage(nc, m, *names):
    with ExitStack() as ctx:
        sems = {n: ctx.enter_context(nc.semaphore(n)) for n in names if n[:3] != "sw_"}
        sems.update({n: m.sw_sems[n] for n in names if n[:3] == "sw_"})
        with nc.Block() as block:
            yield block, sems
        soft = [n for n in names if n[:3] == "sw_"]
        if soft:
            nc.gpsimd.dma_reset()
            nc.all_engine_barrier()
        for s in sems.values():
            nc.sync.sem_clear(s)
        nc.all_engine_barrier()


def modulation(nc, m, l):
    NBUF, PC = 6, 512
    HB = NMOD * D // PC
    with stage(nc, m, *(f"w_loaded{b}" for b in range(NBUF)), "w_used", "small_loaded", "rows_kept", "turned",
               "mod_ready") as (block, s):
        @block.sync
        def _(sp):
            sp.dma_start(m.b_mod[:, :], m.d["b_mod"][l]).then_inc(s["small_loaded"], 16)
            sp.dma_start(m.norm_g[:, :], m.d["norm_g"][l]).then_inc(s["small_loaded"], 16)
            w = m.d["w_mod"][l].rearrange("(k p) (b n) -> b p k n", p=P, n=PC)
            for b in range(HB):
                if b >= NBUF:
                    sp.wait_ge(s["w_used"], b - NBUF + 1)
                sp.dma_start(m.wbuf[:, b % NBUF], w[b]).then_inc(s[f"w_loaded{b % NBUF}"], 16)

        @block.tensor
        def _(pe):
            def turn(b):
                pe.wait_ge(s["rows_kept"], b + 1)
                for q in range(PC // P):
                    at = 3584 + (b * (PC // P) + q) * 2
                    last = nc.tensor.transpose(m.ps[:, at:at + 2],
                                               m.mod_rows[0:2, b * PC + q * P:b * PC + (q + 1) * P], m.ident[0:2, 0:2])
                last.then_inc(s["turned"], 1)

            for b in range(HB):
                pe.wait_ge(s[f"w_loaded{b % NBUF}"], 16 * (b // NBUF + 1))
                if b >= 4:
                    pe.wait_ge(s["rows_kept"], b - 3)
                for k in range(KD):
                    last = nc.tensor.matmul(m.ps[0:2, (b % 4) * 512:(b % 4 + 1) * 512], m.cond[:, k, :],
                                            m.wbuf[:, b % NBUF, k, :], start=(k == 0), stop=(k == KD - 1))
                last.then_inc(s["w_used"], 1)
                if b >= 1:
                    turn(b - 1)
            turn(HB - 1)

        @block.scalar
        def _(act):
            for b in range(HB):
                act.wait_ge(s["w_used"], b + 1)
                nc.scalar.activation(m.mod_rows[0:2, b * PC:(b + 1) * PC],
                                     m.ps[0:2, (b % 4) * 512:(b % 4 + 1) * 512], ACT.Copy).then_inc(s["rows_kept"], 1)

        @block.vector
        def _(dve):
            dve.wait_ge(s["small_loaded"], 32)
            dve.wait_ge(s["turned"], HB)
            c = Count(s["mod_ready"])
            c.then_wait(dve, nc.vector.tensor_tensor(
                m.mod[:, :, :], m.ps[:, 3584:3584 + 2 * NMOD * KD].rearrange("p (j g) -> p j g", g=2),
                m.b_mod[:, :].unsqueeze(2).to_broadcast([P, NMOD * KD, 2]), ALU.add))
            for n in range(2):
                sc = m.mod[:, (3 * n + 1) * KD:(3 * n + 2) * KD, :]
                g = m.norm_g[:, n * KD:(n + 1) * KD].unsqueeze(2).to_broadcast([P, KD, 2])
                nc.vector.scalar_tensor_tensor(sc, sc, 1.0, g, ALU.add, ALU.mult)


def norm_to_channels(nc, m, n):
    shift, scale = 3 * n * KD, (3 * n + 1) * KD
    G = 3
    with stage(nc, m, *(f"x_loaded{t}" for t in range(NT)), "squared", "mean", "root", "inverse", "row_normed",
               "transposed", "h_ready", "h_ready_act", "stored") as (block, s):
        @block.sync
        def _(sp):
            for t in range(NT):
                sp.dma_start(m.xbuf[:, t], m.x_dram[t * P:(t + 1) * P, :]).then_inc(s[f"x_loaded{t}"], 16)
            if n == 1:
                for t in range(NT):
                    sp.wait_ge(s["row_normed"], t + 1)
                    sp.dma_start(m.xn_dram[t * P:(t + 1) * P, :], m.xbuf[:, t]).then_inc(s["stored"], 16)
                sp.wait_ge(s["stored"], 16 * NT)

        @block.scalar
        def _(act):
            def squares(a):
                for t in range(a * G, (a + 1) * G):
                    act.wait_ge(s[f"x_loaded{t}"], 16)
                    if t >= 1:
                        act.wait_ge(s["squared"], t)
                    nc.scalar.activation(m.sq[:, :], m.xbuf[:, t], ACT.Square,
                                         accum_out=m.ss[:, t:t + 1]).then_inc(s["squared"], 1)
                act.wait_ge(s["mean"], a + 1)
                nc.scalar.activation(m.rt[:, a * G:(a + 1) * G], m.ms[:, a * G:(a + 1) * G], ACT.Sqrt)                    .then_inc(s["root"], 1)

            def shape_h(a):
                for t in range(a * G, (a + 1) * G):
                    g = 0 if t < LT else 1
                    act.wait_ge(s["transposed"], 2 * t + 1)
                    for k in range(4):
                        at = (t % 4) * 1024 + k * P
                        last = nc.scalar.activation(m.hT[:, k, t * P:(t + 1) * P], m.ps[:, at:at + P], ACT.Identity,
                                                    bias=m.mod[:, shift + k, g:g + 1],
                                                    scale=m.mod[:, scale + k, g:g + 1])
                    last.then_inc(s["h_ready_act"], 1)

            squares(0)
            squares(1)
            shape_h(0)
            squares(2)
            shape_h(1)
            shape_h(2)

        @block.vector
        def _(dve):
            def inverse(a):
                r = slice(a * G, (a + 1) * G)
                dve.wait_ge(s["squared"], (a + 1) * G)
                nc.vector.tensor_scalar(m.ms[:, r], m.ss[:, r], 1.0 / D, EPS, ALU.mult, ALU.add)                    .then_inc(s["mean"], 1)
                dve.wait_ge(s["root"], a + 1)
                nc.vector.reciprocal(m.rs[:, r], m.rt[:, r]).then_inc(s["inverse"], 1)
                dve.wait_ge(s["inverse"], a + 1)

            def norm_row(t):
                nc.vector.tensor_scalar(m.xbuf[:, t], m.xbuf[:, t], m.rs[:, t:t + 1], None,
                                        ALU.mult).then_inc(s["row_normed"], 1)

            def shape_h(t):
                g = 0 if t < LT else 1
                dve.wait_ge(s["transposed"], 2 * t + 2)
                for k in range(4, 8):
                    at = (t % 4) * 1024 + k * P
                    last = nc.vector.tensor_scalar(m.hT[:, k, t * P:(t + 1) * P], m.ps[:, at:at + P],
                                                   m.mod[:, scale + k, g:g + 1], m.mod[:, shift + k, g:g + 1],
                                                   ALU.mult, ALU.add)
                last.then_inc(s["h_ready"], 1)

            inverse(0)
            for t in range(G):
                norm_row(t)
            for a in range(1, NT // G):
                inverse(a)
                for t in range(a * G, (a + 1) * G):
                    norm_row(t)
                    shape_h(t - G)
            for t in range(NT - G, NT):
                shape_h(t)

        @block.tensor
        def _(pe):
            for t in range(NT):
                pe.wait_ge(s["row_normed"], t + 1)
                if t >= 4:
                    pe.wait_ge(s["h_ready"], t - 3)
                    pe.wait_ge(s["h_ready_act"], t - 3)
                for k in range(KD):
                    last = nc.tensor.transpose(m.ps[:, (t % 4) * 1024 + k * P:(t % 4) * 1024 + (k + 1) * P],
                                               m.xbuf[:, t, k * P:(k + 1) * P], m.ident[:, :])
                    if k in (3, 7):
                        last.then_inc(s["transposed"], 1)


def zc_slot(j):
    if j < 6:
        return "c", j
    if j < 10:
        return "t", (j - 6) * P
    if j < 18:
        return "c", j - 4
    if j < 22:
        return "t", (j - 14) * P
    return "d", j - 22


def projection(nc, m, l):
    NB, BC = 7, 4
    jobs = []
    for j in range(NB * BC):
        kind, at = zc_slot(j)
        if kind == "t":
            if j % 2 == 0:
                jobs += [("t", j, at, t) for t in range(NT)]
        else:
            jobs.append((kind, j, at, 0))
    chan = [x for x in jobs if x[0] != "t"]
    tok = [x for x in jobs if x[0] == "t"]
    with stage(nc, m, "w_loaded0", "w_loaded1", "w_used", "chan_done", "chan_taken", "tok_done", "tok_taken",
               "hy_stored0", "hy_stored1") as (block, s):
        w = m.d["w_in"][l].rearrange("(k p) (b n) -> b p k n", p=P, n=BC * P)
        first_hy = next(i for i, x in enumerate(chan) if x[0] == "d")

        @block.sync
        def _(sp):
            for b in range(NB):
                if b >= 2:
                    sp.wait_ge(s["w_used"], b - 1)
                sp.dma_start(m.W[:, b % 2], w[b]).then_inc(s[f"w_loaded{b % 2}"], 16)
            for i in range(6):
                sp.wait_ge(s["chan_taken"], first_hy + i + 1)
                sp.dma_start(m.zhy_dram[i * P:(i + 1) * P, :], m.zstage[:, i % 2]).then_inc(s[f"hy_stored{i % 2}"], 16)
            sp.wait_ge(s["hy_stored0"], 16 * 3)
            sp.wait_ge(s["hy_stored1"], 16 * 3)

        @block.tensor
        def _(pe):
            nchan = ntok = 0
            for kind, j, at, t in jobs:
                b, jj = divmod(j, BC)
                pe.wait_ge(s[f"w_loaded{b % 2}"], 16 * (b // 2 + 1))
                if kind != "t":
                    if nchan >= 2:
                        pe.wait_ge(s["chan_taken"], nchan - 1)
                    base = (nchan % 2) * 3 * 512
                    for q in range(3):
                        for k in range(KD):
                            last = nc.tensor.matmul(m.ps[:, base + q * 512:base + q * 512 + TC],
                                                    m.W[:, b % 2, k, jj * P:(jj + 1) * P],
                                                    m.hT[:, k, q * TC:(q + 1) * TC],
                                                    start=(k == 0), stop=(k == KD - 1))
                    last.then_inc(s["chan_done"], 1)
                    nchan += 1
                else:
                    if ntok >= 2:
                        pe.wait_ge(s["tok_taken"], ntok - 1)
                    base = (6 + ntok % 2) * 512
                    for k in range(KD):
                        last = nc.tensor.matmul(m.ps[:, base:base + 256], m.hT[:, k, t * P:(t + 1) * P],
                                                m.W[:, b % 2, k, jj * P:(jj + 2) * P],
                                                start=(k == 0), stop=(k == KD - 1))
                    last.then_inc(s["tok_done"], 1)
                    ntok += 1
                if jj == BC - 1 or (kind == "t" and jj == BC - 2 and t == NT - 1):
                    if kind == "t":
                        pe.wait_ge(s["tok_done"], ntok)
                    else:
                        pe.wait_ge(s["chan_done"], nchan)
                    pe.sem_inc(s["w_used"], 1)

        @block.scalar
        def _(act):
            for i, (kind, j, at, _) in enumerate(chan):
                act.wait_ge(s["chan_done"], i + 1)
                if kind == "d" and at >= 2:
                    act.wait_ge(s[f"hy_stored{at % 2}"], 16 * (at // 2))
                out = m.zc[:, at] if kind == "c" else m.zstage[:, at % 2]
                scale = DQ ** -0.5 if 10 <= j < 14 else 1.0
                base = (i % 2) * 3 * 512
                nc.scalar.activation(out.rearrange("p (q n) -> p q n", n=TC),
                                     m.ps[:, base:base + 1536].rearrange("p (q n) -> p q n", n=512)[:, :, 0:TC],
                                     ACT.Copy, scale=scale).then_inc(s["chan_taken"], 1)

        @block.vector
        def _(dve):
            for i, (_, j, at, t) in enumerate(tok):
                dve.wait_ge(s["tok_done"], i + 1)
                base = (6 + i % 2) * 512
                nc.vector.tensor_copy(m.zt[:, t, at:at + 256], m.ps[:, base:base + 256]).then_inc(s["tok_taken"], 1)

def hgrn_gates(nc, m, l):
    lb = m.lb
    with stage(nc, m, "loaded", "dve_small", "act_small", "softplus_x", "logsig", "keys", "diff",
               "softplus_d", "act_step", "gate_step") as (block, s):
        T1 = [m.qe[:, i] for i in range(4)]
        T2 = [m.ke_t.rearrange("p c i n -> p (c i n)")[:, i * TOK:(i + 1) * TOK] for i in range(4)]
        T3 = [m.A.rearrange("p i c n -> p (i c n)")[:, i * TOK:(i + 1) * TOK] for i in range(4)]
        f = [m.zc[:, 2 + i] for i in range(4)]

        @block.sync
        def _(sp):
            sp.dma_start(lb[:, 0:8], m.d["lb_logits"]).then_inc(s["loaded"], 16)
            sp.dma_start(m.lay[:, :], m.d["layer_const"][l].partition_broadcast(P)).then_inc(s["loaded"], 16)

        @block.vector
        def _(dve):
            c = Count(s["dve_small"])
            dve.wait_ge(s["loaded"], 32)
            c.then_wait(dve, nc.vector.tensor_tensor(lb[:, 8:12], lb[:, 4:8], lb[:, 0:4], ALU.subtract))
            c.then_wait(dve, nc.vector.scalar_tensor_tensor(lb[:, 12:16], lb[:, 8:12], -1.0, lb[:, 8:12],
                                                            ALU.mult, ALU.max))
            dve.wait_ge(s["act_small"], 2)
            c.then_wait(dve, nc.vector.scalar_tensor_tensor(lb[:, 16:20], lb[:, 8:12], 0.0, lb[:, 12:16],
                                                            ALU.min, ALU.subtract))
            c.then_wait(dve, nc.vector.scalar_tensor_tensor(lb[:, 20:24], lb[:, 8:12], 0.0, lb[:, 12:16],
                                                            ALU.max, ALU.add))
            c.then_wait(dve, nc.vector.tensor_scalar(lb[:, 24:28], lb[:, 16:20], m.lay[:, 0:1], m.lay[:, 1:2],
                                                     ALU.mult, ALU.add))
            c.then_wait(dve, nc.vector.tensor_scalar(lb[:, 28:32], lb[:, 20:24], m.lay[:, 0:1], -1.0,
                                                     ALU.mult, ALU.mult))
            c.then_wait(dve, nc.vector.tensor_tensor(lb[:, 32:36], lb[:, 28:32], lb[:, 24:28], ALU.subtract))
            for i in range(4):
                dve.wait_ge(s["softplus_x"], i + 1)
                nc.vector.scalar_tensor_tensor(T3[i], f[i], 0.0, T2[i], ALU.max, ALU.add)
                nc.vector.scalar_tensor_tensor(T1[i], f[i], 0.0, T2[i], ALU.min, ALU.subtract)\
                    .then_inc(s["logsig"], 1)
            dve.wait_ge(s["keys"], 4)
            g = Count(s["gate_step"])
            nc.vector.memset(m.A[:, :, :, 0], 0.0)
            for i in range(4):
                dve.wait_ge(s["diff"], i + 1)
                g.done(nc.vector.tensor_scalar(T1[i], T1[i], lb[:, 28 + i:29 + i], lb[:, 24 + i:25 + i],
                                               ALU.add, ALU.max))
            for i in range(4):
                dve.wait_ge(s["softplus_d"], i + 1)
                dve.wait_ge(s["gate_step"], i + 1)
                g.done(nc.vector.tensor_tensor(m.A[:, i, :, 1:], T1[i].rearrange("p (c t) -> p c t", t=P),
                                               T2[i].rearrange("p (c t) -> p c t", t=P), ALU.add))
            for i in range(4):
                dve.wait_ge(s["gate_step"], 4 + i + 1)
                for ch in range(NT):
                    nc.vector.tensor_tensor_scan(m.A[:, i, ch, 1:], m.ones[:, :], m.A[:, i, ch, 1:], 0.0,
                                                 ALU.mult, ALU.add)

        @block.scalar
        def _(act):
            c = Count(s["act_step"])
            act.wait_ge(s["dve_small"], 2)
            nc.scalar.activation(lb[:, 12:16], lb[:, 12:16], ACT.Exp, scale=-1.0).then_inc(s["act_small"], 1)
            act.wait_ge(s["act_small"], 1)
            nc.scalar.activation(lb[:, 12:16], lb[:, 12:16], ACT.Ln, bias=1.0).then_inc(s["act_small"], 1)

            def softplus(out):
                for i in range(4):
                    act.wait_ge(s["act_step"], c.n - 3)
                    c.done(nc.scalar.activation(T2[i], T2[i], ACT.Exp, scale=-1.0))
                for i in range(4):
                    act.wait_ge(s["act_step"], c.n - 3 + i)
                    nc.scalar.activation(T2[i], T2[i], ACT.Ln, bias=1.0).then_inc(s[out], 1)

            for i in range(4):
                c.done(nc.scalar.activation(T2[i], f[i], ACT.Abs))
            softplus("softplus_x")
            act.wait_ge(s["dve_small"], 7)
            for i in range(4):
                act.wait_ge(s["logsig"], i + 1)
                nc.scalar.activation(T2[i], T1[i], ACT.Abs, bias=lb[:, 32 + i:33 + i]).then_inc(s["diff"], 1)
            act.wait_ge(s["diff"], 4)
            softplus("softplus_d")
            for i in range(4):
                act.wait_ge(s["logsig"], i + 1)
                nc.scalar.activation(f[i], T3[i], ACT.Exp, bias=lb[:, 28 + i:29 + i], scale=-1.0)\
                    .then_inc(s["keys"], 1)


def hgrn_states(nc, m, l):
    def A(i, off):
        return m.A[:, i, :, off:off + P]

    def end(i):
        return m.A[:, i, :, P:P + 1].to_broadcast([P, NT, P])

    def tiles(x):
        return x.rearrange("p (c t) -> p c t", t=P)

    with stage(nc, m, "state_loaded", "rest", "from_a", "from_rest", "queries", "keys", "transposed", "keys_taken",
               "decay", "update", "chained", "stored", "cleared") as (block, s):
        steps = []
        for n in range(LT - 1):
            steps.append([(0, n), (1, LT - 1 - n)])
        steps.append([(0, LT), (1, LT)])

        @block.sync
        def _(sp):
            sp.wait_ge(s["cleared"], 1)
            for d in range(2):
                for ct in range(2):
                    for hh in range(2):
                        r, cols = slice(hh * DQ, (hh + 1) * DQ), slice(hh * DQ, (hh + 1) * DQ)
                        sp.dma_start(m.S[d][r, ct, 0 if d == 0 else LT - 1, cols], m.d["state"][l, d, ct, r, :])\
                            .then_inc(s["state_loaded"], 16)
            sp.wait_ge(s["chained"], 8 * LT)
            for d in range(2):
                for ct in range(2):
                    for hh in range(2):
                        r = slice(hh * DQ, (hh + 1) * DQ)
                        sp.dma_start(m.o["s"][l, d, 2 * ct + hh], m.S[d][r, ct, LT, r]).then_inc(s["stored"], 16)
            sp.wait_ge(s["stored"], 128)

        @block.gpsimd
        def _(pool):
            for d in range(2):
                last = nc.gpsimd.memset(m.S[d][:, :, :, :], 0.0)
            last.then_inc(s["cleared"], 1)

        @block.vector
        def _(dve):
            for i in range(4):
                if i >= 2:
                    dve.wait_ge(s["transposed"], i - 1)
                    dve.wait_ge(s["queries"], i - 1)
                if i < 2:
                    nc.vector.tensor_tensor(tiles(m.E[:, i % 2, 0:TOK]), end(i), A(i, 1), ALU.subtract)\
                        .then_inc(s["rest"], 1)
                else:
                    nc.vector.tensor_tensor(tiles(m.E[:, i % 2, 0:TOK]), end(i), A(i, 0), ALU.subtract)\
                        .then_inc(s["rest"], 1)
                wq, wk = (m.X, m.E) if i < 2 else (m.E, m.X)
                dve.wait_ge(s["from_a"], i + 1)
                dve.wait_ge(s["from_rest"], i + 1)
                nc.vector.tensor_tensor(m.qe[:, i], m.zc[:, i % 2], wq[:, i % 2, 0:TOK], ALU.mult)\
                    .then_inc(s["queries"], 1)
                nc.vector.tensor_tensor(wk[:, i % 2, 0:TOK], m.zc[:, 2 + i], wk[:, i % 2, 0:TOK], ALU.mult)\
                    .then_inc(s["keys"], 1)
            dve.wait_ge(s["state_loaded"], 128)
            dve.wait_ge(s["cleared"], 1)
            dve.wait_ge(s["decay"], 1)
            dve.wait_ge(s["update"], len(steps))
            for n, pair in enumerate(steps):
                for d, ch in pair:
                    for ct in range(2):
                        i = 2 * d + ct
                        if n and ch != LT:
                            dve.wait_ge(s["chained"], 8 * (n - 1) + 2 * i + 2)
                        for hh in range(2):
                            r = slice(hh * DQ, (hh + 1) * DQ)
                            u = m.ps[r, (n * 4 + i) * DQ:(n * 4 + i + 1) * DQ]
                            if ch == LT:
                                nc.vector.tensor_copy(m.S[d][r, ct, ch, r], u).then_inc(s["chained"], 1)
                            else:
                                nxt = ch + 1 if d == 0 else ch - 1
                                nc.vector.scalar_tensor_tensor(m.S[d][r, ct, nxt, r], m.S[d][r, ct, ch, r],
                                                               m.dec[r, i, ch:ch + 1], u, ALU.mult, ALU.add)\
                                    .then_inc(s["chained"], 1)

        @block.scalar
        def _(act):
            def take(i):
                act.wait_ge(s["transposed"], i + 1)
                nc.scalar.activation(m.ke_t[:, :, i, :],
                                     m.ps[:, (i % 2) * 1536:(i % 2) * 1536 + TOK].rearrange("p (c n) -> p c n", n=P),
                                     ACT.Copy).then_inc(s["keys_taken"], 1)
            nc.scalar.activation(m.dec[:, :, :], m.A[:, :, :, P], ACT.Exp).then_inc(s["decay"], 1)
            for i in range(4):
                if i >= 2:
                    take(i - 2)
                    act.wait_ge(s["queries"], i - 1)
                nc.scalar.activation(tiles(m.X[:, i % 2, 0:TOK]), A(i, 1 if i < 2 else 0), ACT.Exp)\
                    .then_inc(s["from_a"], 1)
                act.wait_ge(s["rest"], i + 1)
                nc.scalar.activation(m.E[:, i % 2, 0:TOK], m.E[:, i % 2, 0:TOK], ACT.Exp)\
                    .then_inc(s["from_rest"], 1)
            take(2)
            take(3)

        @block.tensor
        def _(pe):
            for i in range(4):
                pe.wait_ge(s["keys"], i + 1)
                if i >= 2:
                    pe.wait_ge(s["keys_taken"], i - 1)
                src = (m.E if i < 2 else m.X)[:, i % 2]
                for ch in range(NT):
                    at = (i % 2) * 1536 + ch * P
                    last = nc.tensor.transpose(m.ps[:, at:at + P], src[:, ch * P:(ch + 1) * P], m.ident[:, :])
                last.then_inc(s["transposed"], 1)
            pe.wait_ge(s["keys_taken"], 4)
            for n, pair in enumerate(steps):
                for d, ch in pair:
                    for ct in range(2):
                        i = 2 * d + ct
                        at = (n * 4 + i) * DQ
                        for hh in range(2):
                            h = 2 * ct + hh
                            last = nc.tensor.matmul(m.ps[hh * DQ:(hh + 1) * DQ, at:at + DQ],
                                                    m.ke_t[:, ch, i, hh * DQ:(hh + 1) * DQ],
                                                    m.zt[:, ch, h * DQ:(h + 1) * DQ], start=True, stop=True)
                last.then_inc(s["update"], 1)


def hgrn_outputs(nc, m, l):
    NL = len(LEVELS) + 1
    seq = [(ct, d, lev) for ct in range(2) for d in range(2) for lev in range(NL)]
    GROUPS = [(0, 4), (4, 8), (8, NT)]
    NG = len(GROUPS)
    freed = []
    for ct, d, lev in seq:
        freed += [("placed", sum(f[0] == "placed" for f in freed) + g + 1) for g in range(NG)]
        if (d, lev) == (1, NL - 1):
            freed += [("out_taken", ct * NG + g + 1) for g in range(NG)]

    def halves(x, h):
        v = x.rearrange("p (c b two j) -> p c b two j", c=NT, two=2, j=h)
        return v[:, :, :, 0, :], v[:, :, :, 1, :]

    slots = [NG * (n + ct) for n, (ct, _, _) in enumerate(seq)]
    out_slots = [NG * (2 * NL), NG * (4 * NL + 1)]
    with stage(nc, m, "mask_loaded", "att_cleared", "span", "weight", "operand", "scores", "placed",
               "out_done", "out_taken") as (block, s):
        @block.sync
        def _(sp):
            sp.dma_start(m.mask[:, :, :, :], m.d["hg_mask"]).then_inc(s["mask_loaded"], 16)

        @block.vector
        def _(dve):
            dve.wait_ge(s["mask_loaded"], 16)

            def prepare(n):
                ct, d, lev = seq[n]
                if lev >= len(LEVELS):
                    return
                i, h, b = 2 * d + ct, LEVELS[lev], n % 2
                if n >= 2:
                    dve.wait_ge(s["scores"], NG * (n - 1))
                a = m.A[:, i]
                nb = P // (2 * h)
                lo, hi = halves(m.E[:, b, 0:TOK], h)
                mid = a[:, :, 0:P].rearrange("p c (b w) -> p c b w", w=2 * h)[:, :, :, h:h + 1]\
                    .to_broadcast([P, NT, nb, h])
                shift = 1 if d == 0 else 0
                w = a[:, :, shift:shift + P].rearrange("p c (b two j) -> p c b two j", two=2, j=h)
                left, right = w[:, :, :, 0, :], w[:, :, :, 1, :]
                nc.vector.tensor_tensor(lo, mid, left, ALU.subtract)
                nc.vector.tensor_tensor(hi, right, mid, ALU.subtract).then_inc(s["span"], 1)
                spans[n] = len(spans) + 1
                dve.wait_ge(s["weight"], spans[n])
                xlo, xhi = halves(m.X[:, b, 0:TOK], h)
                qlo, qhi = halves(m.zc[:, ct], h)
                klo, khi = halves(m.zc[:, 2 + i], h)
                x0, x1 = (klo, qhi) if d == 0 else (qlo, khi)
                nc.vector.tensor_tensor(xlo, lo, x0, ALU.mult)
                nc.vector.tensor_tensor(xhi, hi, x1, ALU.mult).then_inc(s["operand"], 1)

            def place(n):
                ct, d, lev = seq[n]
                if lev == 0:
                    dve.wait_ge(s["att_cleared"], 2 * ct + d + 1)
                for g, (c0, c1) in enumerate(GROUPS):
                    dve.wait_ge(s["scores"], NG * n + g + 1)
                    if lev:
                        dve.wait_ge(s["placed"], NG * (n - 1) + g + 1)
                    slot = slots[n] + g
                    dat = m.ps[:, (slot % 4) * 1024:(slot % 4 + 1) * 1024]\
                        .rearrange("p (hh n) -> p hh n", hh=2)[:, :, 0:(c1 - c0) * P]
                    h = LEVELS[lev] if lev < len(LEVELS) else 1
                    dat = dat.rearrange("p hh (c b two j) -> p hh c b two j", c=c1 - c0, two=2, j=h)
                    out = m.att[:, d][:, :, c0:c1].rearrange("p hh c (b two j) -> p hh c b two j", two=2, j=h)
                    parts = [(lev, 1 if d == 0 else 0)] if lev < len(LEVELS) else [(lev, 0), (lev + 1, 1)]
                    for mk, half in parts:
                        msk = m.mask[:, d, mk].rearrange("p (b j) -> p b j", j=h)\
                            .unsqueeze(1).unsqueeze(1).to_broadcast([P, 2, c1 - c0, 64 // h, h])
                        last = nc.vector.copy_predicated(out[:, :, :, :, half, :], msk, dat[:, :, :, :, half, :])
                    last.then_inc(s["placed"], 1)

            spans = {}
            prepare(0)
            for n in range(len(seq)):
                if n + 1 < len(seq):
                    prepare(n + 1)
                place(n)

        @block.gpsimd
        def _(pool):
            for ct in range(2):
                for d in range(2):
                    if ct:
                        pool.wait_ge(s["out_done"], NG)
                    nc.gpsimd.memset(m.att[:, d], 0.0).then_inc(s["att_cleared"], 1)

        @block.scalar
        def _(act):
            k = 0

            def take(ct):
                for g, (c0, c1) in enumerate(GROUPS):
                    act.wait_ge(s["out_done"], ct * NG + g + 1)
                    at = ((out_slots[ct] + g) % 4) * 1024
                    nc.scalar.activation(m.o_sb[:, c0:c1, ct * P:(ct + 1) * P],
                                         m.ps[:, at:at + (c1 - c0) * P].rearrange("p (c n) -> p c n", n=P), ACT.Copy)\
                        .then_inc(s["out_taken"], 1)
            for n, (ct, d, lev) in enumerate(seq):
                if lev < len(LEVELS):
                    k += 1
                    act.wait_ge(s["span"], k)
                    nc.scalar.activation(m.E[:, n % 2, 0:TOK], m.E[:, n % 2, 0:TOK], ACT.Exp)\
                        .then_inc(s["weight"], 1)
                if (ct, d, lev) == (1, 0, 0):
                    take(0)
            take(1)

        @block.tensor
        def _(pe):
            ops = 0
            for n, (ct, d, lev) in enumerate(seq):
                i = 2 * d + ct
                if lev < len(LEVELS):
                    ops += 1
                    pe.wait_ge(s["operand"], ops)
                for g, (c0, c1) in enumerate(GROUPS):
                    u = slots[n] + g
                    if u >= 4:
                        pe.wait_ge(s[freed[u - 4][0]], freed[u - 4][1])
                    for ch in range(c0, c1):
                        for hh in range(2):
                            r = slice(hh * DQ, (hh + 1) * DQ)
                            at = (u % 4) * 1024 + hh * 512 + (ch - c0) * P
                            if lev < len(LEVELS):
                                lhs = rhs = m.X[r, n % 2, ch * P:(ch + 1) * P]
                            else:
                                lhs = m.zc[r, 2 + i, ch * P:(ch + 1) * P]
                                rhs = m.zc[r, ct, ch * P:(ch + 1) * P]
                            last = nc.tensor.matmul(m.ps[:, at:at + P], lhs, rhs, start=True, stop=True)
                    last.then_inc(s["scores"], 1)
                if (d, lev) != (1, NL - 1):
                    continue
                for g, (c0, c1) in enumerate(GROUPS):
                    u = out_slots[ct] + g
                    pe.wait_ge(s["placed"], NG * n + g + 1)
                    pe.wait_ge(s[freed[u - 4][0]], freed[u - 4][1])
                    for ch in range(c0, c1):
                        at = (u % 4) * 1024 + (ch - c0) * P
                        if ch < LT:
                            for dd in range(2):
                                nc.tensor.matmul(m.ps[:, at:at + P], m.qe[:, 2 * dd + ct, ch * P:(ch + 1) * P],
                                                 m.S[dd][:, ct, ch, :], start=(dd == 0), stop=False)
                        for hh in range(2):
                            h = 2 * ct + hh
                            out = m.ps[:, at + hh * DQ:at + (hh + 1) * DQ]
                            for dd in range(2):
                                last = nc.tensor.matmul(out, m.att[:, dd, hh, ch, :], m.zt[:, ch, h * DQ:(h + 1) * DQ],
                                                        start=(ch == LT and dd == 0),
                                                        stop=(dd == 1 and (hh == 1 or ch == LT)))
                    last.then_inc(s["out_done"], 1)


def hgrn_finish(nc, m, l):
    n = NT * HEADS
    o4 = m.o_sb.rearrange("p c (h v) -> p c h v", v=DQ)
    sm = m.small[:, 0:n].rearrange("p (c h) -> p c h", h=HEADS)
    with stage(nc, m, "g_loaded", "step", "root", "gate", "out_ready", "transposed") as (block, s):
        sq = m.view(m.R_W, NT, 256)
        sq4 = sq.rearrange("p c (h v) -> p c h v", v=DQ)
        gate = m.view(m.R_W + NT * 256, NT, 256)

        @block.sync
        def _(sp):
            sp.dma_start(m.hg_gain[:, :], m.d["hgrn_norm_g"][l].partition_broadcast(P)).then_inc(s["g_loaded"], 16)

        @block.scalar
        def _(act):
            nc.scalar.activation(gate[:, :, :], m.zt[:, :, 256:512], ACT.Silu).then_inc(s["gate"], 1)
            act.wait_ge(s["step"], 3)
            nc.scalar.activation(m.small[:, 0:n], m.small[:, 0:n], ACT.Sqrt).then_inc(s["root"], 1)
            for ct in range(2):
                act.wait_ge(s["transposed"], ct + 1)
                nc.scalar.activation(m.oT[:, ct], m.ps[:, ct * 1536:ct * 1536 + TOK], ACT.Copy)

        @block.vector
        def _(dve):
            c = Count(s["step"])
            c.then_wait(dve, nc.vector.tensor_tensor(sq[:, :, :], m.o_sb[:, :, :], m.o_sb[:, :, :], ALU.mult))
            c.then_wait(dve, nc.vector.tensor_reduce(sm, sq4, AX.X, ALU.add))
            c.then_wait(dve, nc.vector.tensor_scalar(m.small[:, 0:n], m.small[:, 0:n], 1.0 / DQ, EPS, ALU.mult,
                                                     ALU.add))
            dve.wait_ge(s["root"], 1)
            c.then_wait(dve, nc.vector.reciprocal(m.small[:, 0:n], m.small[:, 0:n]))
            c.then_wait(dve, nc.vector.tensor_tensor(o4, o4, sm.unsqueeze(3).to_broadcast([P, NT, HEADS, DQ]),
                                                     ALU.mult))
            dve.wait_ge(s["g_loaded"], 16)
            c.then_wait(dve, nc.vector.tensor_tensor(o4, o4, m.hg_gain[:, :].unsqueeze(1).unsqueeze(1).to_broadcast([P, NT, HEADS, DQ]),
                                                     ALU.mult))
            dve.wait_ge(s["gate"], 1)
            nc.vector.tensor_tensor(m.o_sb[:, :, :], m.o_sb[:, :, :], gate[:, :, :], ALU.mult)\
                .then_inc(s["out_ready"], 1)

        @block.tensor
        def _(pe):
            pe.wait_ge(s["out_ready"], 1)
            for ct in range(2):
                for t in range(NT):
                    last = nc.tensor.transpose(m.ps[:, ct * 1536 + t * P:ct * 1536 + (t + 1) * P],
                                               m.o_sb[:, t, ct * P:(ct + 1) * P], m.ident[:, :])
                last.then_inc(s["transposed"], 1)

def attention_prepare(nc, m, l):
    with stage(nc, m, "tables_loaded", "keys_loaded", "values_loaded", "lambda_loaded", "shuffled", "turned", "kept",
               "transposed", "taken", "stored", "lam_step", "lam_exp") as (block, s):
        @block.sync
        def _(sp):
            sp.dma_start(m.cos[:, :], m.d["rope_cos"]).then_inc(s["tables_loaded"], 16)
            sp.dma_start(m.sin[:, :], m.d["rope_sin"]).then_inc(s["tables_loaded"], 16)
            sp.dma_start(m.lamv[:, :], m.d["diff_lambda"][l].partition_broadcast(P)).then_inc(s["lambda_loaded"], 16)
            for j in range(2):
                for h in range(HEADS):
                    sp.dma_start(m.kraw[:, j, h, :].rearrange("p (m d) -> p m d", d=DQ),
                                 m.d["cache_k"][l, h, :, j * P:(j + 1) * P, :].rearrange("m t d -> t m d"))\
                        .then_inc(s["keys_loaded"], 16)
            for j in range(2):
                sp.dma_start(m.vctx[:, j], m.d["cache_v"][l, :, j * P:(j + 1) * P, :].rearrange("h t v -> t h v"))\
                    .then_inc(s["values_loaded"], 16)
            sp.dma_start(m.o["v"][l].rearrange("h t v -> t h v"),
                         m.zt[:, LT, 512:1024].rearrange("p (h v) -> p h v", v=DV)).then_inc(s["stored"], 16)
            sp.wait_ge(s["taken"], 3)
            for h in range(HEADS):
                sp.dma_start(m.o["k"][l, h].rearrange("m t d -> t m d"),
                             m.kout[:, h].rearrange("p (m d) -> p m d", d=DQ)).then_inc(s["stored"], 16)
            sp.wait_ge(s["values_loaded"], 32)
            sp.wait_ge(s["stored"], 16 * (HEADS + 1))

        @block.gpsimd
        def _(pool):
            pool.wait_ge(s["tables_loaded"], 32)
            for i in range(8):
                pool.wait_ge(s["shuffled"], i + 1)
                x = m.zc[:, 6 + i, 0:LAT]
                nc.gpsimd.tensor_tensor(x, x, m.cos[:, :], ALU.mult).then_inc(s["kept"], 1)

        @block.vector
        def _(dve):
            c = Count(s["lam_step"])
            dve.wait_ge(s["lambda_loaded"], 16)
            v = m.lamv[:, :].rearrange("p (a b d) -> p a b d", a=2, b=2)
            c.then_wait(dve, nc.vector.tensor_tensor(v[:, :, 0], v[:, :, 0], v[:, :, 1], ALU.mult))
            c.then_wait(dve, nc.vector.tensor_reduce(m.lam[:, 0:2], v[:, :, 0], AX.X, ALU.add))
            dve.wait_ge(s["lam_exp"], 1)
            c.then_wait(dve, nc.vector.tensor_tensor(m.lam[:, 2:3], m.lam[:, 1:2], m.lam[:, 0:1], ALU.subtract))
            nc.vector.tensor_tensor(m.lam[:, 3:4], m.lam[:, 2:3], m.lay[:, 2:3], ALU.subtract)
            dve.wait_ge(s["tables_loaded"], 32)
            t = Count(s["turned"])
            for i in range(8):
                x = m.zc[:, 6 + i, 0:LAT]
                r = m.rot[:, i % 2]
                nc.vector.stream_shuffle(r, x, [(k + 16) % 32 for k in range(32)]).then_inc(s["shuffled"], 1)
                dve.wait_ge(s["shuffled"], i + 1)
                t.then_wait(dve, nc.vector.tensor_tensor(r, r, m.sin[:, :], ALU.mult))
                dve.wait_ge(s["kept"], i + 1)
                nc.vector.tensor_tensor(x, x, r, ALU.add)

        @block.scalar
        def _(act):
            act.wait_ge(s["lam_step"], 2)
            nc.scalar.activation(m.lam[:, 0:2], m.lam[:, 0:2], ACT.Exp).then_inc(s["lam_exp"], 1)
            for j in range(2):
                act.wait_ge(s["transposed"], j + 1)
                nc.scalar.activation(m.kctx[:, :, j * P:(j + 1) * P],
                                     m.ps[:, j * 512:(j + 1) * 512].rearrange("p (h n) -> p h n", n=P), ACT.Copy)\
                    .then_inc(s["taken"], 1)
            act.wait_ge(s["transposed"], 3)
            nc.scalar.activation(m.kout[:, :, :], m.ps[:, 1024:1536].rearrange("p (h n) -> p h n", n=P), ACT.Copy)\
                .then_inc(s["taken"], 1)

        @block.tensor
        def _(pe):
            pe.wait_ge(s["keys_loaded"], 16 * 8)
            for j in range(2):
                for h in range(HEADS):
                    last = nc.tensor.transpose(m.ps[:, j * 512 + h * P:j * 512 + (h + 1) * P], m.kraw[:, j, h, :],
                                               m.ident[:, :])
                last.then_inc(s["transposed"], 1)
            for h in range(HEADS):
                last = nc.tensor.transpose(m.ps[:, 1024 + h * P:1024 + (h + 1) * P], m.zc[:, 10 + h, LAT:TOK],
                                           m.ident[:, :])
            last.then_inc(s["transposed"], 1)


def attention(nc, m, l):
    jobs = [(qt, h) for qt in range(NT) for h in range(HEADS)]
    NJ = len(jobs)

    def pieces(qt, h, mp):
        r = slice(mp * DQ, (mp + 1) * DQ)
        if qt == LT:
            return [(0, m.zc[r, 10 + h, LAT:TOK])]
        return [(0, m.zc[r, 10 + h, 0:512]), (512, m.zc[r, 10 + h, 512:1024]), (1024, m.kctx[r, h, :])]

    def nkeys(qt):
        return CTX if qt == LT else LAT + PAST

    def rounds(qt):
        n = nkeys(qt) // P
        return [range(a, min(a + 4, n)) for a in range(0, n, 4)]

    first_round = [0]
    for qt, _ in jobs:
        first_round.append(first_round[-1] + len(rounds(qt)))

    with stage(nc, m, "score0", "score1", "max0", "max1", "prob0", "prob1", "ratio", "combined",
               "turned", "taken", "valued", "row_out") as (block, s):
        @block.tensor
        def _(pe):
            def score(n, mp):
                if n >= NJ:
                    return
                qt, h = jobs[n]
                if n:
                    pe.wait_ge(s[f"prob{mp}"], n)
                q = m.zc[mp * DQ:(mp + 1) * DQ, 6 + h, qt * P:(qt + 1) * P]
                for col, keys in pieces(qt, h, mp):
                    at = mp * 1536 + col
                    last = nc.tensor.matmul(m.ps[:, at:at + keys.shape[1]], q, keys, start=True, stop=True)
                last.then_inc(s[f"score{mp}"], 1)

            def turn(n, r):
                qt, h = jobs[n]
                if r >= len(rounds(qt)):
                    return
                g = first_round[n] + r
                if g:
                    pe.wait_ge(s["taken"], g)
                for k, j in enumerate(rounds(qt)[r]):
                    last = nc.tensor.transpose(m.ps[:, 3072 + k * P:3072 + (k + 1) * P],
                                               m.prob[:, n % 2, 0, j * P:(j + 1) * P], m.ident[:, :])
                last.then_inc(s["turned"], 1)

            score(0, 0)
            score(0, 1)
            for n, (qt, h) in enumerate(jobs):
                pe.wait_ge(s["combined"], n + 1)
                turn(n, 0)
                score(n + 1, 0)
                turn(n, 1)
                score(n + 1, 1)
                turn(n, 2)
                pe.wait_ge(s["taken"], first_round[n + 1])
                if n:
                    pe.wait_ge(s["row_out"], n)
                nk = nkeys(qt) // P
                for j in range(nk):
                    if qt == LT:
                        v = m.zt[:, LT, 512 + h * DV:512 + (h + 1) * DV]
                    elif j < LT:
                        v = m.zt[:, j, 512 + h * DV:512 + (h + 1) * DV]
                    else:
                        v = m.vctx[:, j - LT, h, :]
                    last = nc.tensor.matmul(m.ps[:, 3584:3584 + DV], m.aT[:, n % 2, j, :], v, start=(j == 0),
                                            stop=(j == nk - 1))
                last.then_inc(s["valued"], 1)

        @block.vector
        def _(dve):
            c = Count(s["ratio"])

            def maxima(n):
                if n >= NJ:
                    return
                for mp in range(2):
                    dve.wait_ge(s[f"score{mp}"], n + 1)
                    nc.vector.tensor_reduce(m.nmax[:, n, mp:mp + 1], m.ps[:, mp * 1536:mp * 1536 + nkeys(jobs[n][0])],
                                            AX.X, ALU.max, negate=True).then_inc(s[f"max{mp}"], 1)

            def combine(n):
                qt = jobs[n][0]
                p = m.prob[:, n % 2, :, 0:nkeys(qt)]
                dve.wait_ge(s["prob0"], n + 1)
                dve.wait_ge(s["prob1"], n + 1)
                c.then_wait(dve, nc.vector.reciprocal(m.rsum[:, n, :], m.sums[:, n, :]))
                c.then_wait(dve, nc.vector.scalar_tensor_tensor(m.mix[:, n:n + 1], m.sums[:, n, 0:1], m.lam[:, 3:4],
                                                                m.rsum[:, n, 1:2], ALU.mult, ALU.mult))
                nc.vector.scalar_tensor_tensor(p[:, 0], p[:, 1], m.mix[:, n:n + 1], p[:, 0], ALU.mult, ALU.add)\
                    .then_inc(s["combined"], 1)

            def out(n):
                qt, h = jobs[n]
                dve.wait_ge(s["valued"], n + 1)
                nc.vector.tensor_scalar(m.o_att[:, qt, h * DV:(h + 1) * DV], m.ps[:, 3584:3584 + DV],
                                        m.rsum[:, n, 0:1], None, ALU.mult).then_inc(s["row_out"], 1)

            maxima(0)
            for n in range(NJ):
                combine(n)
                maxima(n + 1)
                out(n)

        @block.scalar
        def _(act):
            def probs(n):
                if n >= NJ:
                    return
                if n >= 2:
                    act.wait_ge(s["turned"], first_round[n - 1])
                for mp in range(2):
                    act.wait_ge(s[f"max{mp}"], n + 1)
                    nk = nkeys(jobs[n][0])
                    nc.scalar.activation(m.prob[:, n % 2, mp, 0:nk], m.ps[:, mp * 1536:mp * 1536 + nk], ACT.Exp,
                                         bias=m.nmax[:, n, mp:mp + 1], accum_out=m.sums[:, n, mp:mp + 1])\
                        .then_inc(s[f"prob{mp}"], 1)

            probs(0)
            for n, (qt, h) in enumerate(jobs):
                for r, js in enumerate(rounds(qt)):
                    act.wait_ge(s["turned"], first_round[n] + r + 1)
                    if n >= 2 and r == 0:
                        act.wait_ge(s["valued"], n - 1)
                    nc.scalar.activation(m.aT[:, n % 2, js[0]:js[-1] + 1, :].rearrange("p a b -> p (a b)"),
                                         m.ps[:, 3072:3072 + len(js) * P], ACT.Copy).then_inc(s["taken"], 1)
                probs(n + 1)


def attention_finish(nc, m, l):
    n = NT * HEADS
    o4 = m.o_att.rearrange("p c (h v) -> p c h v", v=DV)
    sm = m.small[:, 0:n].rearrange("p (c h) -> p c h", h=HEADS)
    with stage(nc, m, "g_loaded", "step", "root", "out_ready", "transposed", "taken") as (block, s):
        sq = m.view(m.R_W, NT, 512)
        sq4 = sq.rearrange("p c (h v) -> p c h v", v=DV)

        @block.sync
        def _(sp):
            sp.dma_start(m.sub_gain[:, :], m.d["diff_subln_g"][l].partition_broadcast(P)).then_inc(s["g_loaded"], 16)

        @block.scalar
        def _(act):
            act.wait_ge(s["step"], 3)
            nc.scalar.activation(m.small[:, 0:n], m.small[:, 0:n], ACT.Sqrt).then_inc(s["root"], 1)
            for ct in range(4):
                act.wait_ge(s["transposed"], ct + 1)
                at = (ct % 2) * 1536
                nc.scalar.activation(m.oT[:, 2 + ct], m.ps[:, at:at + TOK], ACT.Copy).then_inc(s["taken"], 1)

        @block.vector
        def _(dve):
            c = Count(s["step"])
            c.then_wait(dve, nc.vector.tensor_tensor(sq[:, :, :], m.o_att[:, :, :], m.o_att[:, :, :], ALU.mult))
            c.then_wait(dve, nc.vector.tensor_reduce(sm, sq4, AX.X, ALU.add))
            c.then_wait(dve, nc.vector.tensor_scalar(m.small[:, 0:n], m.small[:, 0:n], 1.0 / DV, EPS, ALU.mult,
                                                     ALU.add))
            dve.wait_ge(s["root"], 1)
            c.then_wait(dve, nc.vector.reciprocal(m.small[:, 0:n], m.small[:, 0:n]))
            c.then_wait(dve, nc.vector.tensor_tensor(o4, o4, sm.unsqueeze(3).to_broadcast([P, NT, HEADS, DV]),
                                                     ALU.mult))
            dve.wait_ge(s["g_loaded"], 16)
            c.then_wait(dve, nc.vector.tensor_scalar(m.sub_gain[:, :], m.sub_gain[:, :], m.lay[:, 3:4], None,
                                                     ALU.mult))
            nc.vector.tensor_tensor(o4, o4, m.sub_gain[:, :].unsqueeze(1).unsqueeze(1)
                                    .to_broadcast([P, NT, HEADS, DV]), ALU.mult).then_inc(s["out_ready"], 1)

        @block.tensor
        def _(pe):
            pe.wait_ge(s["out_ready"], 1)
            for ct in range(4):
                if ct >= 2:
                    pe.wait_ge(s["taken"], ct - 1)
                for t in range(NT):
                    at = (ct % 2) * 1536 + t * P
                    last = nc.tensor.transpose(m.ps[:, at:at + P], m.o_att[:, t, ct * P:(ct + 1) * P], m.ident[:, :])
                last.then_inc(s["transposed"], 1)

MAGIC = 12582912.0
TWO_PI_HI = 6.28125
TWO_PI_LO = 2 * math.pi - 6.28125
PI_BELOW = 3.1415925


def hyena_filters(nc, m, l, g):
    L, nt = g.L, g.nt
    W = min(L, 512)
    halves = range(L // W)
    with stage(nc, m, "small_loaded", "decay_loaded", "biased", "hidden", "argued", "reduced", "sine", "taps_done",
               "taps", "magnitude", "mag_used", "folded", "copied", "table0", "table1", "summed", "norm",
               "spectrum", "taken", "edge") as (block, s):
        @block.sync
        def _(sp):
            for dst, src in ((m.hy_pos[0:POS, 0:L], g.pos), (m.hy_w1[0:POS, :], m.d["hy_w1"][l]),
                             (m.hy_w2[0:HID, :], m.d["hy_w2"][l]), (m.hy_w3[0:HID, :], m.d["hy_w3"][l]),
                             (m.hy_bf[0:HID, :], m.d["hy_bf"][l]), (m.alt[:, :], m.d["alt"])):
                sp.dma_start(dst, src).then_inc(s["small_loaded"], 16)
            sp.dma_start(m.decay[:, 0:nt, :], g.decay).then_inc(s["decay_loaded"], 16)
            for k in range(2 * nt):
                if k >= 2:
                    sp.wait_ge(s["spectrum"], k - 1)
                src = g.cos if k < nt else g.sin
                sp.dma_start(m.table[:, k % 2, 0:L], src[(k % nt) * P:(k % nt + 1) * P, :])\
                    .then_inc(s[f"table{k % 2}"], 16)

        @block.tensor
        def _(pe):
            pe.wait_ge(s["small_loaded"], 16 * 6)
            for h in halves:
                last = nc.tensor.matmul(m.ps[0:HID, h * 512:h * 512 + W], m.hy_w1[0:POS, :],
                                        m.hy_pos[0:POS, h * W:(h + 1) * W], start=True, stop=True)
            last.then_inc(s["hidden"], 1)
            pe.wait_ge(s["sine"], 1)
            for h in halves:
                last = nc.tensor.matmul(m.ps[0:HID, h * 512:h * 512 + W], m.hy_w2[0:HID, :],
                                        m.hy_h[0:HID, h * W:(h + 1) * W], start=True, stop=True)
            last.then_inc(s["hidden"], 1)
            pe.wait_ge(s["sine"], 2)

            def column_sums(t):
                pe.wait_ge(s["magnitude"], t + 1)
                for d in range(2):
                    last = nc.tensor.matmul(m.ps[:, 3584:4096], m.ones[:, :],
                                            m.mag[:, t % 2, d * 512:(d + 1) * 512],
                                            start=(t == 0 and d == 0), stop=(t == nt - 1 and d == 1))
                last.then_inc(s["mag_used"], 1)

            for t in range(nt):
                if t >= 2:
                    pe.wait_ge(s["taps"], t - 1)
                for d in range(2):
                    last = nc.tensor.matmul(m.ps[:, (t % 2) * 1024 + d * 512:(t % 2) * 1024 + (d + 1) * 512],
                                            m.hy_h[0:HID, t * P:(t + 1) * P], m.hy_w3[0:HID, d * 512:(d + 1) * 512],
                                            start=True, stop=True)
                last.then_inc(s["taps_done"], 1)
                if t:
                    column_sums(t - 1)
            column_sums(nt - 1)
            pe.wait_ge(s["norm"], 1)
            pe.wait_ge(s["copied"], nt)
            pe.wait_ge(s["folded"], 2 * nt)
            for part in range(2):
                if part:
                    pe.wait_ge(s["taken"], nt)
                for k in range(nt):
                    kk = part * nt + k
                    pe.wait_ge(s[f"table{kk % 2}"], 16 * (kk // 2 + 1))
                    for ft in range(nt):
                        last = nc.tensor.matmul(m.ps[:, ft * 512:(ft + 1) * 512],
                                                m.table[:, kk % 2, ft * P:(ft + 1) * P],
                                                m.hf[:, k, part * 512:(part + 1) * 512],
                                                start=(k == 0), stop=(k == nt - 1))
                    last.then_inc(s["spectrum"], 1)
            pe.wait_ge(s["taken"], 2 * nt)
            for k in range(nt):
                last = nc.tensor.matmul(m.ps[0:1, 0:512], m.alt[:, 0:1], m.hf[:, k, 0:512], start=(k == 0),
                                        stop=(k == nt - 1))
            last.then_inc(s["spectrum"], 1)

        @block.scalar
        def _(act):
            act.wait_ge(s["biased"], 1)
            for layer in range(2):
                act.wait_ge(s["hidden"], layer + 1)
                nc.scalar.activation(m.hy_a[0:HID, 0:L], m.ps[0:HID, 0:L], ACT.Identity,
                                     bias=m.hy_bf[0:HID, layer:layer + 1], scale=m.hy_bf[0:HID, 2 + layer:3 + layer])\
                    .then_inc(s["argued"], 1)
                act.wait_ge(s["reduced"], layer + 1)
                nc.scalar.activation(m.hy_h[0:HID, 0:L], m.hy_a[0:HID, 0:L], ACT.Sin).then_inc(s["sine"], 1)
            for t in range(nt):
                act.wait_ge(s["taps"], t + 1)
                if t >= 2:
                    act.wait_ge(s["mag_used"], t - 1)
                nc.scalar.activation(m.mag[:, t % 2, :], m.hf[:, t, :], ACT.Abs).then_inc(s["magnitude"], 1)
            for t in range(nt):
                act.wait_ge(s["folded"], 2 * t + 2)
                nc.scalar.activation(m.hf[:, t, 0:512], m.fold[:, t % 4, :], ACT.Copy).then_inc(s["copied"], 1)

        @block.vector
        def _(dve):
            dve.wait_ge(s["small_loaded"], 16 * 6)
            nc.vector.tensor_tensor(m.hy_bf[0:HID, 0:2], m.hy_bf[0:HID, 0:2], m.hy_bf[0:HID, 2:4], ALU.mult)\
                .then_inc(s["biased"], 1)
            a, k = m.hy_a[0:HID, 0:L], m.hy_k[0:HID, 0:L]
            c = Count(s["edge"])
            for layer in range(2):
                dve.wait_ge(s["argued"], layer + 1)
                c.then_wait(dve, nc.vector.tensor_scalar(k, a, 1.0 / (2 * math.pi), None, ALU.mult))
                c.then_wait(dve, nc.vector.tensor_scalar(k, k, MAGIC, None, ALU.add))
                c.then_wait(dve, nc.vector.tensor_scalar(k, k, MAGIC, None, ALU.subtract))
                c.then_wait(dve, nc.vector.scalar_tensor_tensor(a, k, -TWO_PI_HI, a, ALU.mult, ALU.add))
                c.then_wait(dve, nc.vector.scalar_tensor_tensor(a, k, -TWO_PI_LO, a, ALU.mult, ALU.add))
                nc.vector.tensor_scalar(a, a, PI_BELOW, -PI_BELOW, ALU.min, ALU.max).then_inc(s["reduced"], 1)
            dve.wait_ge(s["decay_loaded"], 16)
            for t in range(nt):
                dve.wait_ge(s["taps_done"], t + 1)
                nc.vector.tensor_tensor(m.hf[:, t, :].rearrange("p (a c) -> p a c", c=HYW),
                                        m.ps[:, (t % 2) * 1024:(t % 2 + 1) * 1024].rearrange("p (a c) -> p a c", c=HYW),
                                        m.decay[:, t, :].unsqueeze(1).to_broadcast([P, 4, HYW]), ALU.mult)\
                    .then_inc(s["taps"], 1)
            dve.wait_ge(s["mag_used"], nt)
            c.then_wait(dve, nc.vector.reciprocal(m.hy_rn[:, :], m.ps[:, 3584:4096]))
            nc.vector.tensor_scalar(m.hy_rn[:, :], m.hy_rn[:, :], 1.0 / L, None, ALU.mult).then_inc(s["norm"], 1)
            c.then_wait(dve, nc.vector.memset(m.hf[0:1, 0, 512:1024], 0.0))
            for t in range(nt):
                if t >= 4:
                    dve.wait_ge(s["copied"], t - 3)
                nc.vector.tensor_tensor(m.fold[:, t % 4, :], m.hf[:, t, 0:512], m.hf[:, t, 512:1024], ALU.add)\
                    .then_inc(s["folded"], 1)
                dve.wait_ge(s["folded"], 2 * t + 1)
                nc.vector.tensor_tensor(m.hf[:, t, 512:1024], m.hf[:, t, 0:512], m.hf[:, t, 512:1024],
                                        ALU.subtract).then_inc(s["folded"], 1)
            dve.wait_ge(s["norm"], 1)
            for part, f in enumerate((g.fre, g.fim)):
                dve.wait_ge(s["spectrum"], (part + 1) * nt)
                for ft in range(nt):
                    nc.vector.tensor_tensor(f[:, ft, :], m.ps[:, ft * 512:(ft + 1) * 512], m.hy_rn[:, :], ALU.mult)\
                        .then_inc(s["taken"], 1)
            dve.wait_ge(s["taken"], 2 * nt)
            c.then_wait(dve, nc.vector.memset(g.fim[0:1, 0, :], 0.0))
            c.then_wait(dve, nc.vector.tensor_copy(g.nyq[:, :], g.fre[:, 0, :]))
            c.then_wait(dve, nc.vector.tensor_scalar(g.fre[0:1, 0, :], g.fre[0:1, 0, :], 0.5, None, ALU.mult))
            dve.wait_ge(s["spectrum"], 2 * nt + 1)
            nc.vector.scalar_tensor_tensor(g.nyq[0:1, :], m.ps[0:1, 0:512], 0.5, m.hy_rn[0:1, :], ALU.mult, ALU.mult)


def hyena_short(nc, m, l):
    with stage(nc, m, "z_loaded0", "z_loaded1", "w_loaded", "tap", "mixed", "transposed", "taken") as (block, s):
        @block.sync
        def _(sp):
            for dst, src in ((m.hy_cw, "hy_conv_w"), (m.hy_cb, "hy_conv_b"), (m.hy_skip, "hy_skip")):
                sp.dma_start(dst[:, :], m.d[src][l]).then_inc(s["w_loaded"], 16)
            for n in range(2):
                sp.dma_start(m.zraw[:, 3 * n:3 * n + 3, :],
                             m.zhy_dram[3 * n * P:3 * (n + 1) * P, :].rearrange("(j p) t -> p j t", p=P))\
                    .then_inc(s[f"z_loaded{n}"], 16)

        @block.vector
        def _(dve):
            c = Count(s["tap"])
            dve.wait_ge(s["w_loaded"], 48)
            for j in range(6):
                dve.wait_ge(s[f"z_loaded{j // 3}"], 16)
                z, o = m.zraw[:, j], m.hv[:, j]
                w = [m.hy_cw[:, 3 * j + k:3 * j + k + 1] for k in range(3)]
                c.then_wait(dve, nc.vector.tensor_scalar(o, z, w[1], m.hy_cb[:, j:j + 1], ALU.mult, ALU.add))
                for a, b in ((0, LAT), (LAT, TOK)):
                    c.done(nc.vector.scalar_tensor_tensor(o[:, a + 1:b], z[:, a:b - 1], w[0], o[:, a + 1:b],
                                                          ALU.mult, ALU.add))
                dve.wait_ge(s["tap"], c.n)
                for a, b in ((0, LAT), (LAT, TOK)):
                    last = nc.vector.scalar_tensor_tensor(o[:, a:b - 1], z[:, a + 1:b], w[2], o[:, a:b - 1],
                                                          ALU.mult, ALU.add)
                    c.done(last)
            for j in range(2):
                dve.wait_ge(s["transposed"], j + 1)
                nc.vector.tensor_copy(m.hu[:, :, j * P:(j + 1) * P],
                                      m.ps[:, j * 1536:j * 1536 + TOK].rearrange("p (t n) -> p t n", n=P))

        @block.tensor
        def _(pe):
            for j in range(2):
                pe.wait_ge(s["tap"], 5 * (j + 1))
                for t in range(NT):
                    last = nc.tensor.transpose(m.ps[:, j * 1536 + t * P:j * 1536 + (t + 1) * P],
                                               m.hv[:, j, t * P:(t + 1) * P], m.ident[:, :])
                last.then_inc(s["transposed"], 1)


def hyena_conv(nc, m, l, g, order):
    L, nt, t0 = g.L, g.nt, g.t0
    W = min(L, 512)
    nh = L // W
    cols = slice(order * HYW, (order + 1) * HYW)
    ur = m.ps[:, 0:nt * HYW].rearrange("p (f c) -> p f c", c=HYW)
    ui = m.ps[:, 2048:2048 + nt * HYW].rearrange("p (f c) -> p f c", c=HYW)
    src = m.hv[:, 0:2, t0:t0 + L]
    gate = m.hv[:, 2 + 2 * order:4 + 2 * order, t0:t0 + L]
    with stage(nc, m, "fc0", "fc1", "fs0", "fs1", "forward", "product", "spectra", "inverse", "result",
               "transposed") as (block, s):
        @block.sync
        def _(sp):
            for k in range(2 * nt):
                if k >= 2:
                    sp.wait_ge(s["forward"], min(k - 1, nt))
                    if k - 2 >= nt:
                        sp.wait_ge(s["inverse"], k - 1 - nt)
                rows = slice((k % nt) * P, (k % nt + 1) * P)
                sp.dma_start(m.tcos[:, k % 2, 0:L], g.cos[rows, :]).then_inc(s[f"fc{k % 2}"], 16)
                sp.dma_start(m.tsin[:, k % 2, 0:L], (g.sin if k < nt else g.sin_t)[rows, :])\
                    .then_inc(s[f"fs{k % 2}"], 16)

        @block.tensor
        def _(pe):
            for k in range(nt):
                pe.wait_ge(s[f"fc{k % 2}"], 16 * (k // 2 + 1))
                pe.wait_ge(s[f"fs{k % 2}"], 16 * (k // 2 + 1))
                for table, out in ((m.tcos, ur), (m.tsin, ui)):
                    for ft in range(nt):
                        last = nc.tensor.matmul(out[:, ft, :], table[:, k % 2, ft * P:(ft + 1) * P],
                                                m.hu[:, t0 // P + k, :], start=(k == 0 and ft % 2 == 0),
                                                stop=(k == nt - 1), skip_group_check=True)
                last.then_inc(s["forward"], 1)
            pe.wait_ge(s["spectra"], 2)
            for k in range(nt):
                kk = nt + k
                pe.wait_ge(s[f"fc{kk % 2}"], 16 * (kk // 2 + 1))
                pe.wait_ge(s[f"fs{kk % 2}"], 16 * (kk // 2 + 1))
                for part, table in enumerate((m.tcos, m.tsin)):
                    for ct in range(2):
                        for h in range(nh):
                            at = (ct * 2 + h) * 512
                            last = nc.tensor.matmul(m.ps[:, at:at + W], m.hy[:, part, k, ct * P:(ct + 1) * P],
                                                    table[:, kk % 2, h * W:(h + 1) * W],
                                                    start=(k == 0 and part == 0), stop=(k == nt - 1 and part == 1))
                last.then_inc(s["inverse"], 1)
            if order == 0:
                pe.wait_ge(s["result"], 4)
                for ct in range(2):
                    for t in range(nt):
                        at = 2048 + ct * 1024 + t * P
                        last = nc.tensor.transpose(m.ps[:, at:at + P], src[:, ct, t * P:(t + 1) * P], m.ident[:, :])
                    last.then_inc(s["transposed"], 1)

        @block.vector
        def _(dve):
            fre, fim = g.fre[:, :, cols], g.fim[:, :, cols]
            yr, yi, tmp = m.hy[:, 0, 0:nt], m.hy[:, 1, 0:nt], m.htmp[:, 0:nt, :]
            dve.wait_ge(s["forward"], nt)
            c = Count(s["product"])
            c.done(nc.vector.tensor_tensor(yr, ur, fre, ALU.mult))
            c.then_wait(dve, nc.vector.tensor_tensor(tmp, ui, fim, ALU.mult))
            nc.vector.tensor_tensor(yr, yr, tmp, ALU.subtract).then_inc(s["spectra"], 1)
            dve.wait_ge(s["spectra"], 1)
            c.then_wait(dve, nc.vector.tensor_tensor(yi, ur, fim, ALU.mult))
            if nt > 1:
                c.done(nc.vector.tensor_tensor(tmp[:, 1:nt], ui[:, 1:nt], fre[:, 1:nt], ALU.mult))
            c.then_wait(dve, nc.vector.tensor_tensor(tmp[:, 0], ui[:, 0], g.nyq[:, cols], ALU.mult))
            nc.vector.tensor_tensor(yi, yi, tmp, ALU.add).then_inc(s["spectra"], 1)
            dve.wait_ge(s["inverse"], nt)
            r = Count(s["result"])
            for ct in range(2):
                y = m.ps[:, ct * 1024:ct * 1024 + L]
                r.then_wait(dve, nc.vector.scalar_tensor_tensor(src[:, ct], src[:, ct],
                                                                m.hy_skip[:, 2 * order + ct:2 * order + ct + 1], y,
                                                                ALU.mult, ALU.add))
                out = src[:, ct] if order == 0 else m.oT[:, 6 + ct, t0:t0 + L]
                r.done(nc.vector.tensor_tensor(out, src[:, ct], gate[:, ct], ALU.mult))
            if order == 0:
                for ct in range(2):
                    dve.wait_ge(s["transposed"], ct + 1)
                    nc.vector.tensor_copy(m.hu[:, t0 // P:t0 // P + nt, ct * P:(ct + 1) * P],
                                          m.ps[:, 2048 + ct * 1024:2048 + ct * 1024 + L]
                                          .rearrange("p (t n) -> p t n", n=P))


def hyena(nc, m, l):
    for g in (m.geo_lat, m.geo_ctx):
        hyena_filters(nc, m, l, g)
    hyena_short(nc, m, l)
    for g in (m.geo_lat, m.geo_ctx):
        for order in range(2):
            hyena_conv(nc, m, l, g, order)

def gate_rows(nc, m, block_engines, s, which):
    dve, pe = block_engines
    col = (3 * which + 2) * KD
    if dve is not None:
        c = 0
        for g in range(2):
            for k in range(KD):
                n = g * KD + k
                if n >= 4:
                    dve.wait_ge(s["diag_used"], n - 3)
                nc.vector.tensor_scalar(m.diag[:, n % 4, :], m.ident[:, :], m.mod[:, col + k, g:g + 1], None,
                                        ALU.mult).then_inc(s["diag"], 1)
    if pe is not None:
        for g in range(2):
            for k in range(KD):
                n = g * KD + k
                pe.wait_ge(s["diag"], n + 1)
                nc.tensor.matmul(m.ps[:, 2048 + n * P:2048 + (n + 1) * P], m.ones[:, :], m.diag[:, n % 4, :],
                                 start=True, stop=True).then_inc(s["diag_used"], 1)


def output_projection(nc, m, l):
    with stage(nc, m, "w_loaded", "x_loaded0", "x_loaded1", "x_loaded2", "diag", "diag_used", "rows_ready", "projected",
               "scaled", "updated", "stored0", "stored1", "stored2") as (block, s):
        @block.sync
        def _(sp):
            sp.dma_start(m.wo[:, :, :], m.d["w_out"][l].rearrange("(k p) n -> p k n", p=P)).then_inc(s["w_loaded"], 16)
            for t in range(NT):
                if t >= 3:
                    sp.wait_ge(s[f"stored{t % 3}"], 16 * (t // 3))
                sp.dma_start(m.xr[:, t % 3], m.x_dram[t * P:(t + 1) * P, :]).then_inc(s[f"x_loaded{t % 3}"], 16)

        @block.tensor
        def _(pe):
            gate_rows(nc, m, (None, pe), s, 0)
            pe.wait_ge(s["w_loaded"], 16)
            for t in range(NT):
                if t >= 2:
                    pe.wait_ge(s["scaled"], t - 1)
                for h in range(2):
                    for k in range(KD):
                        at = (t % 2) * 1024 + h * 512
                        last = nc.tensor.matmul(m.ps[:, at:at + 512], m.oT[:, k, t * P:(t + 1) * P],
                                                m.wo[:, k, h * 512:(h + 1) * 512], start=(k == 0), stop=(k == KD - 1))
                last.then_inc(s["projected"], 1)

        @block.vector
        def _(dve):
            gate_rows(nc, m, (dve, None), s, 0)
            dve.wait_ge(s["rows_ready"], 1)
            for t in range(NT):
                g = 0 if t < LT else 1
                dve.wait_ge(s["projected"], t + 1)
                if t >= 2:
                    dve.wait_ge(s["updated"], t - 1)
                nc.vector.tensor_tensor(m.dx[:, t % 2], m.ps[:, (t % 2) * 1024:(t % 2 + 1) * 1024], m.gb[:, g, :],
                                        ALU.mult).then_inc(s["scaled"], 1)
                dve.wait_ge(s[f"x_loaded{t % 3}"], 16 * (t // 3 + 1))
                dve.wait_ge(s["scaled"], t + 1)
                nc.vector.tensor_tensor(m.xr[:, t % 3], m.xr[:, t % 3], m.dx[:, t % 2], ALU.add)\
                    .then_inc(s["updated"], 1)

        @block.scalar
        def _(act):
            act.wait_ge(s["diag_used"], 16)
            nc.scalar.activation(m.gb.rearrange("p g n -> p (g n)"), m.ps[:, 2048:4096], ACT.Copy)\
                .then_inc(s["rows_ready"], 1)
            for t in range(NT):
                act.wait_ge(s["updated"], t + 1)
                act.dma_start(m.x_dram[t * P:(t + 1) * P, :], m.xr[:, t % 3]).then_inc(s[f"stored{t % 3}"], 16)
            for b in range(3):
                act.wait_ge(s[f"stored{b}"], 16 * 3)


def route(nc, m, l):
    with stage(nc, m, "w_loaded", "logits", "centred", "exps", "aff", "turned", "aff_t", "found", "cast",
               "sel_turned", "spread", "one_hot", "hot_turned", "gathered") as (block, s):
        RL, RP = CAP_L // 8, CAP_P // 8

        @block.sync
        def _(sp):
            sp.dma_start(m.wr[:, :, :], m.d["w_router"][l].rearrange("(k p) e -> p k e", p=P))\
                .then_inc(s["w_loaded"], 16)

        @block.tensor
        def _(pe):
            pe.wait_ge(s["w_loaded"], 16)
            for t in range(NT):
                for k in range(KD):
                    last = nc.tensor.matmul(m.ps[:, t * E:(t + 1) * E], m.hT[:, k, t * P:(t + 1) * P],
                                            m.wr[:, k, :], start=(k == 0), stop=(k == KD - 1))
            last.then_inc(s["logits"], 1)
            pe.wait_ge(s["aff"], 1)
            for t in range(NT):
                last = nc.tensor.transpose(m.ps[0:E, 512 + t * P:512 + (t + 1) * P], m.aff[:, t, :], m.ident[:, :])
            last.then_inc(s["turned"], 1)
            pe.wait_ge(s["cast"], 2)
            for n, src in enumerate((m.topv, m.topf)):
                nc.tensor.matmul(m.ps[:, 2560 + n * 256:2560 + (n + 1) * 256], m.ones[0:E, :], m.spread[0:E, n],
                                 start=True, stop=True)
                last = nc.tensor.transpose(m.ps[:, 2048 + n * 32:2048 + n * 32 + E], src[0:E, 0:CAP_L],
                                           m.ident[0:E, 0:E])
            last.then_inc(s["sel_turned"], 1)
            pe.wait_ge(s["one_hot"], 1)
            for k in range(KD):
                at = (k % 2) * 512
                if k >= 2:
                    pe.wait_ge(s["gathered"], k - 1)
                nc.tensor.matmul(m.ps[:, at:at + E * CAP_P], m.xbuf[:, NT - 1, k * P:(k + 1) * P],
                                 m.hot[:, 0], start=True, stop=True).then_inc(s["hot_turned"], 1)
            pe.wait_ge(s["one_hot"], 2)
            for g in range(2):
                last = nc.tensor.transpose(m.ps[:, 3072 + g * P:3072 + (g + 1) * P], m.hot[:, 1, g * P:(g + 1) * P],
                                           m.ident[:, :])
            last.then_inc(s["hot_turned"], 1)

        @block.scalar
        def _(act):
            act.wait_ge(s["centred"], 1)
            nc.scalar.activation(m.aff[:, :, :], m.aff[:, :, :], ACT.Exp).then_inc(s["exps"], 1)
            act.wait_ge(s["turned"], 1)
            nc.scalar.activation(m.aff_t[0:E, :], m.ps[0:E, 512:512 + TOK], ACT.Copy).then_inc(s["aff_t"], 1)

        @block.vector
        def _(dve):
            c = Count(s["found"])
            sm = m.small[:, 0:NT]
            lg = m.ps[:, 0:NT * E].rearrange("p (t e) -> p t e", e=E)
            dve.wait_ge(s["logits"], 1)
            c.then_wait(dve, nc.vector.tensor_reduce(sm, lg, AX.X, ALU.max))
            nc.vector.tensor_tensor(m.aff[:, :, :], lg, sm.unsqueeze(2).to_broadcast([P, NT, E]), ALU.subtract)\
                .then_inc(s["centred"], 1)
            dve.wait_ge(s["exps"], 1)
            c.then_wait(dve, nc.vector.tensor_reduce(sm, m.aff[:, :, :], AX.X, ALU.add))
            c.then_wait(dve, nc.vector.reciprocal(sm, sm))
            nc.vector.tensor_tensor(m.aff[:, :, :], m.aff[:, :, :], sm.unsqueeze(2).to_broadcast([P, NT, E]),
                                    ALU.mult).then_inc(s["aff"], 1)
            dve.wait_ge(s["aff_t"], 1)
            for a, b, r0, rounds in ((0, LAT, 0, RL), (LAT, TOK, CAP_L, RP)):
                v = m.aff_t[0:E, a:b]
                for r in range(rounds):
                    best = m.topv[0:E, r0 + 8 * r:r0 + 8 * (r + 1)]
                    c.then_wait(dve, nc.vector.max(best, v))
                    c.done(nc.vector.max_index(m.topi[0:E, r0 + 8 * r:r0 + 8 * (r + 1)], best, v))
                    dve.wait_ge(s["found"], c.n)
                    c.then_wait(dve, nc.vector.match_replace(v, best, v, -1.0))
            nc.vector.tensor_copy(m.topf[0:E, :], m.topi[0:E, :]).then_inc(s["spread"], 1)
            dve.wait_ge(s["spread"], 1)
            for n, src in enumerate((m.topv, m.topf)):
                nc.vector.tensor_tensor(m.spread[0:E, n].rearrange("p (e c) -> p e c", c=CAP_P),
                                        src[0:E, CAP_L:CAP].unsqueeze(1).to_broadcast([E, E, CAP_P]),
                                        m.ident[0:E, 0:E].unsqueeze(2).to_broadcast([E, E, CAP_P]), ALU.mult)\
                    .then_inc(s["cast"], 1)
            dve.wait_ge(s["sel_turned"], 1)
            nc.vector.tensor_scalar(m.hot[:, 0], m.ps[:, 2816:3072], m.row_number[:, 0:1], None, ALU.is_equal)\
                .then_inc(s["one_hot"], 1)
            dve.wait_ge(s["one_hot"], 1)
            nc.vector.tensor_tensor(m.hot[:, 1], m.ps[:, 2560:2816], m.hot[:, 0], ALU.mult).then_inc(s["one_hot"], 1)
            nc.vector.tensor_copy(m.gate_l[:, 0:E], m.ps[:, 2048:2048 + E])
            nc.vector.tensor_copy(m.idx_l[:, 0:E], m.ps[:, 2080:2080 + E])
            nc.vector.memset(m.idx_l[:, E:E + 1], 0)
            nc.vector.memset(m.xp[:, :, E * CAP_P:], 0.0)
            for k in range(KD):
                dve.wait_ge(s["hot_turned"], k + 1)
                nc.vector.tensor_scalar(m.xp[:, k, 0:E * CAP_P], m.ps[:, (k % 2) * 512:(k % 2) * 512 + E * CAP_P],
                                        m.mod[:, 4 * KD + k, 1:2], m.mod[:, 3 * KD + k, 1:2], ALU.mult, ALU.add)\
                    .then_inc(s["gathered"], 1)
            dve.wait_ge(s["hot_turned"], KD + 1)
            nc.vector.tensor_copy(m.combine.rearrange("p g t -> p (g t)"), m.ps[:, 3072:3328])


def experts(nc, m, l):
    CH = ("gate0", "up0", "gate1", "up1", "down0", "down1")
    HK = KD // 2
    names = [f"w_{c}" for c in CH] + [f"w_{c}_used" for c in CH]
    with stage(nc, m, *names, "zeros", "cleared", "index", "go", "sw_rows_l0", "sw_rows_l1", "rows_turned", "x_ready",
               "gu_done", "silu", "hid_ready", "down_done", "y_ready", "y_turned", "gates", "out_l",
               "sw_scattered_l", "p_turned", "p_rows", "p_summed", "p_out", "p_stored") as (block, s):
        yp_of = m.yp.rearrange("p k (e c) -> p e k c", c=CAP_P)
        xp_of = m.xp.rearrange("p k (e c) -> p e k c", c=CAP_P)

        @block.sync
        def _(sp):
            sp.wait_ge(s["zeros"], 1)
            for t in range(LT):
                sp.dma_start(m.acc_dram[t * P:(t + 1) * P, :], m.zero[:, :]).then_inc(s["cleared"], 16)
            wg = m.d["w_gate"][l].rearrange("(i j) (k p) (h n) -> i j h p k n", j=2, p=P, n=512)
            wu = m.d["w_up"][l].rearrange("(i j) (k p) (h n) -> i j h p k n", j=2, p=P, n=512)
            wd = m.d["w_down"][l].rearrange("(i j) (k p) (h n) -> i j h p k n", j=2, p=P, n=512)
            with sp.Fori(0, E // 2) as i:
                for j in range(2):
                    for c, (w, h) in enumerate(((wg, 0), (wu, 0), (wg, 1), (wu, 1), (wd, 0), (wd, 1))):
                        sp.wait_ge(s[f"w_{CH[c]}_used"], i * 2 + j + 1)
                        sp.dma_start(m.wbuf[:, c], w[i, j, h]).then_inc(s[f"w_{CH[c]}"], 16)
            sp.wait_ge(s["p_out"], 2)
            sp.dma_start(m.acc_dram[LAT:TOK, :], m.p_sum[:, :]).then_inc(s["p_stored"], 16)
            sp.wait_ge(s["p_stored"], 16)

        @block.gpsimd
        def _(pool):
            nc.gpsimd.memset(m.zero[:, :], 0.0).then_inc(s["zeros"], 1)

            def gather(e, j, first=False):
                if not first:
                    pool.wait_ge(s["rows_turned"], 2 * (e - 1) + 1)
                nc.gpsimd.tensor_copy(m.ib_l[:, j:j + 1], m.idx_l[:, bass.ds(e, 1)]).then_inc(s["index"], 1)
                pool.wait_ge(s["index"], e + 1)
                pool.sem_inc(s["go"], 1)
                pool.indirect_dma_start(m.rows_l[:, j], None, m.xn_dram,
                                        bass.IndirectOffsetOnAxis(ap=m.ib_l[:, j:j + 1], axis=0))\
                    .then_inc(s[f"sw_rows_l{j}"], 16)

            gather(0, 0, True)
            pool.wait_ge(s["cleared"], 16 * LT)
            with pool.Fori(0, E // 2) as i:
                for j in range(2):
                    e = i * 2 + j
                    gather(e + 1, (j + 1) % 2)
                    pool.wait_ge(s["out_l"], e + 2)
                    pool.sem_inc(s["go"], 1)
                    pool.indirect_dma_start(m.acc_dram, bass.IndirectOffsetOnAxis(ap=m.ib_l[:, j:j + 1], axis=0),
                                            m.y_l[:, j], None, compute_op=ALU.add).then_inc(s["sw_scattered_l"], 16)
                    pool.wait_ge(s["sw_scattered_l"], e * 16 + 16)
            pool.wait_ge(s["sw_rows_l0"], 16 * (E // 2 + 1))

        @block.tensor
        def _(pe):
            def turn_rows(e, loads, j):
                pe.wait_ge(s[f"sw_rows_l{j}"], loads * 16)
                pe.wait_ge(s["x_ready"], e + 1)
                for g in range(2):
                    for k in range(g * HK, (g + 1) * HK):
                        last = nc.tensor.transpose(m.ps[:, 3072 + k * P:3072 + (k + 1) * P],
                                                   m.rows_l[:, j, k * P:(k + 1) * P], m.ident[:, :])
                    last.then_inc(s["rows_turned"], 1)

            for n in [f"w_{c}_used" for c in CH] + ["rows_turned"]:
                pe.sem_inc(s[n], 1)
            turn_rows(0, 1, 0)
            with pe.Fori(0, E // 2) as i:
                for j in range(2):
                    e = i * 2 + j
                    pe.wait_ge(s["x_ready"], e + 2)
                    for h in range(2):
                        pe.wait_ge(s[f"w_gate{h}"], (e + 1) * 16)
                        pe.wait_ge(s[f"w_up{h}"], (e + 1) * 16)
                        for q in range(4):
                            n = h * 4 + q
                            pe.wait_ge(s["hid_ready"], e * 8 + max(n - 1, 0) + 1)
                            for which in range(2):
                                at = ((n % 2) * 2 + which) * 512
                                for k in range(KD):
                                    last = nc.tensor.matmul(m.ps[:, at:at + CAP],
                                                            m.wbuf[:, 2 * h + which, k, q * P:(q + 1) * P],
                                                            m.xe[:, j, k, :], start=(k == 0), stop=(k == KD - 1))
                            last.then_inc(s["gu_done"], 1)
                            if q == 0 and h == 1:
                                pe.wait_ge(s["gu_done"], e * 8 + 4)
                                pe.sem_inc(s["w_gate0_used"], 1)
                                pe.sem_inc(s["w_up0_used"], 1)
                    pe.wait_ge(s["out_l"], e + 1)
                    for h in range(2):
                        pe.wait_ge(s[f"w_down{h}"], (e + 1) * 16)
                        for q in range(4):
                            n = h * 4 + q
                            if n >= 2:
                                pe.wait_ge(s["y_ready"], e * 8 + n - 1)
                            at = (4 + n % 2) * 512
                            for k in range(KD):
                                if n == 0 and k == KD - 1:
                                    pe.wait_ge(s["hid_ready"], e * 8 + 9)
                                elif n == 0 and k == KD - 2:
                                    pe.wait_ge(s["hid_ready"], e * 8 + 8)
                                last = nc.tensor.matmul(m.ps[:, at:at + CAP], m.wbuf[:, 4 + h, k, q * P:(q + 1) * P],
                                                        m.hid[:, k, :], start=(k == 0), stop=(k == KD - 1))
                            last.then_inc(s["down_done"], 1)
                            if n == 0:
                                pe.wait_ge(s["gu_done"], e * 8 + 8)
                                pe.sem_inc(s["w_gate1_used"], 1)
                                pe.sem_inc(s["w_up1_used"], 1)
                            if n == 4:
                                pe.wait_ge(s["down_done"], e * 8 + 4)
                                pe.sem_inc(s["w_down0_used"], 1)
                    turn_rows(e + 1, i + 1 + j, (j + 1) % 2)
                    pe.wait_ge(s["down_done"], e * 8 + 8)
                    pe.sem_inc(s["w_down1_used"], 1)
                    pe.wait_ge(s["y_ready"], e * 8 + 8)
                    for k in range(KD):
                        last = nc.tensor.transpose(m.ps[:, 2048 + k * P:2048 + (k + 1) * P], m.yT[:, k, 0:CAP_L],
                                                   m.ident[:, :])
                    last.then_inc(s["y_turned"], 1)
            pe.wait_ge(s["out_l"], E + 1)
            for g in range(2):
                for k in range(KD):
                    last = nc.tensor.transpose(m.ps[:, g * D + k * P:g * D + (k + 1) * P],
                                               m.yp[:, k, g * P:(g + 1) * P], m.ident[:, :])
                last.then_inc(s["p_turned"], 1)
            pe.wait_ge(s["p_rows"], 2)
            for h in range(2):
                for g in range(2):
                    last = nc.tensor.matmul(m.ps[:, 2048 + h * 512:2048 + (h + 1) * 512], m.combine[:, g, :],
                                            m.p_y[:, g, h * 512:(h + 1) * 512], start=(g == 0), stop=(g == 1))
                last.then_inc(s["p_summed"], 1)

        @block.scalar
        def _(act):
            with act.Fori(0, E // 2) as i:
                for j in range(2):
                    e = i * 2 + j
                    for n in range(8):
                        act.wait_ge(s["gu_done"], e * 8 + n + 1)
                        act.wait_ge(s["hid_ready"], e * 8 + max(n - 1, 0) + 1)
                        at = (n % 2) * 1024
                        nc.scalar.activation(m.sg[:, n % 2, :], m.ps[:, at:at + CAP], ACT.Silu)\
                            .then_inc(s["silu"], 1)
                    act.wait_ge(s["out_l"], e + 1)
                    for n in range(8):
                        act.wait_ge(s["down_done"], e * 8 + n + 1)
                        at = (4 + n % 2) * 512
                        nc.scalar.activation(m.yT[:, n, :], m.ps[:, at:at + CAP], ACT.Copy).then_inc(s["y_ready"], 1)
            act.wait_ge(s["p_turned"], 2)
            nc.scalar.activation(m.p_y[:, 1], m.ps[:, D:2 * D], ACT.Copy).then_inc(s["p_rows"], 1)
            act.wait_ge(s["p_summed"], 2)
            nc.scalar.activation(m.p_sum[:, 512:D], m.ps[:, 2560:3072], ACT.Copy).then_inc(s["p_out"], 1)

        @block.vector
        def _(dve):
            for n in ("x_ready", "hid_ready", "out_l"):
                dve.sem_inc(s[n], 1)

            def shape_x(e, j):
                for g in range(2):
                    dve.wait_ge(s["rows_turned"], 2 * e + g + 2)
                    if g == 0:
                        nc.vector.tensor_copy(m.xe[:, j:j + 1, :, CAP_L:CAP], xp_of[:, bass.ds(e, 1)])
                    for k in range(g * HK, (g + 1) * HK):
                        last = nc.vector.tensor_scalar(m.xe[:, j, k, 0:CAP_L], m.ps[:, 3072 + k * P:3072 + (k + 1) * P],
                                                       m.mod[:, 4 * KD + k, 0:1], m.mod[:, 3 * KD + k, 0:1],
                                                       ALU.mult, ALU.add)
                last.then_inc(s["x_ready"], 1)

            shape_x(0, 0)
            with dve.Fori(0, E // 2) as i:
                for j in range(2):
                    e = i * 2 + j
                    nc.vector.tensor_copy(m.gb_l[:, j:j + 1], m.gate_l[:, bass.ds(e, 1)]).then_inc(s["gates"], 1)
                    for n in range(8):
                        dve.wait_ge(s["silu"], e * 8 + n + 1)
                        at = (n % 2) * 1024 + 512
                        nc.vector.tensor_tensor(m.hid[:, n, :], m.sg[:, n % 2, :], m.ps[:, at:at + CAP], ALU.mult)\
                            .then_inc(s["hid_ready"], 1)
                    shape_x(e + 1, (j + 1) % 2)
                    dve.wait_ge(s["y_turned"], e + 1)
                    dve.wait_ge(s["gates"], e + 1)
                    nc.vector.tensor_copy(yp_of[:, bass.ds(e, 1)], m.yT[:, :, CAP_L:CAP].unsqueeze(1))
                    nc.vector.tensor_scalar(m.y_l[:, j], m.ps[:, 2048:3072], m.gb_l[:, j:j + 1], None, ALU.mult)\
                        .then_inc(s["out_l"], 1)
            dve.wait_ge(s["p_turned"], 1)
            nc.vector.tensor_copy(m.p_y[:, 0], m.ps[:, 0:D]).then_inc(s["p_rows"], 1)
            dve.wait_ge(s["p_summed"], 1)
            nc.vector.tensor_copy(m.p_sum[:, 0:512], m.ps[:, 2048:2560]).then_inc(s["p_out"], 1)


def expert_residual(nc, m, l):
    with stage(nc, m, *(f"x_loaded{t}" for t in range(NT)), "diag", "diag_used", "rows_ready", "scaled", "updated",
               "stored") as (block, s):
        @block.sync
        def _(sp):
            for t in range(NT):
                sp.dma_start(m.er_d[:, t], m.acc_dram[t * P:(t + 1) * P, :]).then_inc(s[f"x_loaded{t}"], 16)
                sp.dma_start(m.er_x[:, t], m.x_dram[t * P:(t + 1) * P, :]).then_inc(s[f"x_loaded{t}"], 16)

        @block.tensor
        def _(pe):
            gate_rows(nc, m, (None, pe), s, 1)

        @block.vector
        def _(dve):
            gate_rows(nc, m, (dve, None), s, 1)
            dve.wait_ge(s["rows_ready"], 1)
            for t in range(NT + 1):
                if t < NT:
                    dve.wait_ge(s[f"x_loaded{t}"], 32)
                    nc.vector.tensor_tensor(m.er_d[:, t], m.er_d[:, t], m.gb[:, 0 if t < LT else 1, :],
                                            ALU.mult).then_inc(s["scaled"], 1)
                if t >= 1:
                    dve.wait_ge(s["scaled"], t)
                    nc.vector.tensor_tensor(m.er_x[:, t - 1], m.er_x[:, t - 1], m.er_d[:, t - 1], ALU.add)\
                        .then_inc(s["updated"], 1)

        @block.scalar
        def _(act):
            act.wait_ge(s["diag_used"], 16)
            nc.scalar.activation(m.gb.rearrange("p g n -> p (g n)"), m.ps[:, 2048:4096], ACT.Copy)\
                .then_inc(s["rows_ready"], 1)
            for t in range(NT):
                act.wait_ge(s["updated"], t + 1)
                act.dma_start(m.x_dram[t * P:(t + 1) * P, :], m.er_x[:, t]).then_inc(s["stored"], 16)
            act.wait_ge(s["stored"], 16 * NT)


def epilogue(nc, m):
    with stage(nc, m, "g_loaded", "squared", "mean", "root", "inverse", "gained", "stored") as (block, s):
        gain = m.gb[:, 0, :]
        G = 3

        @block.sync
        def _(sp):
            sp.dma_start(gain, m.d["final_norm_g"].partition_broadcast(P)).then_inc(s["g_loaded"], 16)
            for t in range(NT):
                sp.wait_ge(s["gained"], t + 1)
                sp.dma_start(m.o["x"][t * P:(t + 1) * P, :], m.er_x[:, t]).then_inc(s["stored"], 16)
            sp.wait_ge(s["stored"], 16 * NT)

        @block.scalar
        def _(act):
            for a in range(NT // G):
                for t in range(a * G, (a + 1) * G):
                    nc.scalar.activation(m.er_d[:, t], m.er_x[:, t], ACT.Square, accum_out=m.ss[:, t:t + 1])\
                        .then_inc(s["squared"], 1)
                act.wait_ge(s["mean"], a + 1)
                nc.scalar.activation(m.rt[:, a * G:(a + 1) * G], m.ms[:, a * G:(a + 1) * G], ACT.Sqrt)\
                    .then_inc(s["root"], 1)

        @block.vector
        def _(dve):
            for a in range(NT // G):
                r = slice(a * G, (a + 1) * G)
                dve.wait_ge(s["squared"], (a + 1) * G)
                nc.vector.tensor_scalar(m.ms[:, r], m.ss[:, r], 1.0 / D, EPS, ALU.mult, ALU.add)\
                    .then_inc(s["mean"], 1)
                dve.wait_ge(s["root"], a + 1)
                nc.vector.reciprocal(m.rs[:, r], m.rt[:, r]).then_inc(s["inverse"], 1)
                dve.wait_ge(s["inverse"], a + 1)
                if a == 0:
                    dve.wait_ge(s["g_loaded"], 16)
                for t in range(a * G, (a + 1) * G):
                    nc.vector.scalar_tensor_tensor(m.er_x[:, t], m.er_x[:, t], m.rs[:, t:t + 1], gain,
                                                   ALU.mult, ALU.mult).then_inc(s["gained"], 1)


def norm_two(nc, m, l):
    norm_to_channels(nc, m, 1)


class Mem:
    pass


ARENA = 52400


def build(nc, d, outs):
    m = Mem()
    m.d = d
    m.o = outs
    with ExitStack() as ctx:
        def sb(name, shape, dt=F32):
            return ctx.enter_context(nc.sbuf_tensor(name, shape, dt))

        m.ps = ctx.enter_context(nc.psum_tensor("ps", [P, 8 * 512], F32))
        m.ident = sb("ident", [P, P])
        m.ones = sb("ones", [P, P])
        m.cond = sb("cond", [P, KD, 2])
        m.mod = sb("mod", [P, NMOD * KD, 2])
        m.b_mod = sb("b_mod_sb", [P, NMOD * KD])
        m.norm_g = sb("norm_g_sb", [P, 2 * KD])
        m.ss, m.ms, m.rt, m.rs = (sb(n, [P, 16]) for n in ("ss", "ms", "rt", "rs"))
        m.small = sb("small", [P, 64])
        m.dec = sb("dec", [P, 4, NT])
        m.lb = sb("lb", [P, 36])
        m.lam = sb("lam", [P, 4])
        m.lay = sb("lay", [P, 4])
        m.hg_gain = sb("hg_gain", [P, DQ])
        arena = sb("arena", [P, ARENA])

        def view(at, *dims):
            n = int(np.prod(dims))
            assert at + n <= ARENA, (at, dims)
            a = arena[:, at:at + n]
            names = "abcd"[:len(dims)]
            if len(dims) == 1:
                return a
            return a.rearrange(f"p ({' '.join(names)}) -> p {' '.join(names)}", **dict(zip(names, dims)))
        m.view = view
        m.R_OT, m.R_ZC, m.R_ZT, m.R_W, m.R_FREE = 0, 9216, 25344, 34560, 42752
        m.hT = m.oT = view(m.R_OT, KD, TOK)
        m.zc = view(m.R_ZC, 14, TOK)
        m.zt = view(m.R_ZT, NT, D)
        m.W = view(m.R_W, 2, KD, 512)
        m.xbuf = view(9216, NT, D)
        m.sq = view(m.R_W + 2 * D, D)
        m.qe = view(2 * TOK, 4, TOK)
        m.S = [view(6 * TOK, 2, NT, P), view(49572, 2, NT, P)]
        m.A = view(m.R_W, 4, NT, P + 1)
        m.X = view(39204, 2, TOK)
        m.E = view(41508, 2, TOK)
        m.ke_t = view(43812, NT, 4, P)
        m.att = view(43812, 2, 2, NT, P)
        m.mask = view(48420, 2, 9, 64).bitcast(U32)
        m.o_sb = m.zt[:, :, 0:256]
        m.kraw = view(34560, 2, HEADS, P)
        m.kctx = view(35584, HEADS, PAST)
        m.vctx = view(36608, 2, HEADS, DV)
        m.cos, m.sin = view(37632, LAT), view(38656, LAT)
        m.rot = view(39680, 2, LAT)
        m.prob = view(41728, 2, 2, LAT + PAST)
        m.aT = view(46848, 2, (LAT + PAST) // P, P)
        m.kout = view(49408, HEADS, P)
        m.lamv = view(49920, 4 * DQ)
        m.nmax, m.sums, m.rsum = (view(50176 + 80 * j, 40, 2) for j in range(3))
        m.mix = view(50416, 40)
        m.sub_gain = view(50456, DV)
        m.o_att = view(m.R_ZC, NT, 512)
        m.hy_pos, m.hy_h, m.hy_a, m.hy_k = (view(9216 + 1024 * j, 1024) for j in range(4))
        m.hy_w3 = view(13312, 1024)
        m.hy_w1, m.hy_w2 = view(14336, HID), view(14400, HID)
        m.hy_bf = view(14464, 4)
        m.mag = view(16128, 2, 1024)
        m.fold = view(18176, 4, 512)
        m.decay = view(20224, LT, HYW)
        m.zraw = view(9216, 6, TOK)
        m.hv = view(16128, 6, TOK)
        m.hf = view(23040, LT, 1024)
        m.hy = view(23040, 2, LT, HYW)
        m.htmp = view(27136, LT, HYW)
        m.table = view(43520, 2, 1024)
        m.tcos, m.tsin = m.table, view(45568, 2, 1024)
        m.hu = view(47616, NT, HYW)
        m.hy_rn = view(49920, 512)
        m.alt = sb("alt_sb", [P, 1])
        m.row_number = sb("row_number_sb", [P, 1])
        m.hy_cw, m.hy_cb, m.hy_skip = sb("hy_cw", [P, 18]), sb("hy_cb", [P, 6]), sb("hy_sk", [P, 4])

        def geometry(name, length, t0, at, nyq_at):
            g = Mem()
            n = length // P
            g.L, g.nt, g.t0 = length, n, t0
            g.fre, g.fim, g.nyq = view(at, n, 512), view(at + 512 * n, n, 512), view(nyq_at, 512)
            g.pos, g.decay, g.cos, g.sin, g.sin_t = (d[f"{k}_{name}"] for k in
                                                     ("pos", "decay", "dft_cos", "dft_sin", "dft_sin_t"))
            return g
        m.geo_lat = geometry("lat", LAT, 0, 31232, 39424)
        m.geo_ctx = geometry("ctx", CTX, LAT, 39936, 40960)
        m.wo = view(m.R_W, KD, D)
        m.xr = view(9216, 3, D)
        m.dx = view(12288, 2, D)
        m.gb = view(14336, 2, D)
        m.er_d, m.er_x = view(17408, NT, D), view(26624, NT, D)
        m.diag = view(16384, 4, P)
        m.wr = view(9216, KD, E)
        m.aff = view(9344, NT, E)
        m.aff_t = view(9488, TOK)
        m.topv, m.topf = view(10640, CAP), view(10784, CAP)
        m.topi = view(10928, CAP).bitcast(U32)
        m.gate_l = view(11072, E)
        m.idx_l = view(11104, E + 1).bitcast(I32)
        m.ib_l = view(11138, 2).bitcast(I32)
        m.gb_l = view(11142, 2)
        m.zero = view(11264, D)
        m.rows_l = view(12288, 2, D)
        m.xp = view(14336, KD, (E + 1) * CAP_P)
        m.y_l = view(16512, 2, D)
        m.yp = view(18560, KD, E * CAP_P)
        m.xe, m.hid = view(20608, 2, KD, CAP), view(22912, KD, CAP)
        m.sg = view(24064, 2, CAP)
        m.combine, m.yT = view(49152, 2, P), view(49408, KD, CAP)
        m.hot, m.spread = view(50560, 2, E * CAP_P), view(51072, 2, E * CAP_P)
        m.p_y, m.p_sum = view(0, 2, D), view(2048, D)
        m.wbuf = view(24576, 6, KD, 512)
        m.mod_rows = view(0, NMOD * D)
        m.acc_dram = nc.dram_tensor("expert_sum", (TOK, D), F32, kind="Internal").ap()
        m.zstage = view(m.R_FREE, 2, TOK)

        m.x_dram = nc.dram_tensor("x_rows", (TOK, D), F32, kind="Internal").ap()
        m.xn_dram = nc.dram_tensor("x_normed", (TOK, D), F32, kind="Internal").ap()
        m.zhy_dram = nc.dram_tensor("z_hyena", (6 * P, TOK), F32, kind="Internal").ap()
        m.sw_sems = {n: ctx.enter_context(nc.semaphore(n)) for n in
                     ("sw_rows_l0", "sw_rows_l1", "sw_scattered_l")}
        prologue(nc, m)
        with nc.Fori(0, DEPTH) as l:
            modulation(nc, m, l)
            norm_to_channels(nc, m, 0)
            projection(nc, m, l)
            hgrn_gates(nc, m, l)
            hgrn_states(nc, m, l)
            hgrn_outputs(nc, m, l)
            hgrn_finish(nc, m, l)
            attention_prepare(nc, m, l)
            attention(nc, m, l)
            attention_finish(nc, m, l)
            hyena(nc, m, l)
            output_projection(nc, m, l)
            norm_two(nc, m, l)
            route(nc, m, l)
            experts(nc, m, l)
            expert_residual(nc, m, l)
        epilogue(nc, m)


def prologue(nc, m):
    with stage(nc, m, "loaded", "copied", "silu") as (block, s):
        @block.sync
        def _(sp):
            sp.dma_start(m.x_dram, m.d["x"]).then_inc(s["copied"], 16)
            sp.dma_start(m.cond[:, :, :], m.d["cond"]).then_inc(s["loaded"], 16)
            sp.dma_start(m.row_number[:, :], m.d["row_number"]).then_inc(s["loaded"], 16)
            sp.dma_start(m.ident[:, :], m.d["ident"]).then_inc(s["loaded"], 16)
            sp.wait_ge(s["copied"], 16)
            sp.wait_ge(s["loaded"], 48)

        @block.vector
        def _(dve):
            nc.vector.memset(m.ones[:, :], 1.0)

        @block.scalar
        def _(act):
            act.wait_ge(s["loaded"], 48)
            nc.scalar.activation(m.cond[:, :, :], m.cond[:, :, :], ACT.Silu)


def host_arrays(i):
    f = np.float32
    a = {}
    a["x"] = np.concatenate([i["x_sample"][0], i["x_prompt"][0]], axis=0)
    a["cond"] = np.ascontiguousarray(np.stack([i["c"][0], i["c_ctx"]], axis=-1).reshape(KD, P, 2).transpose(1, 0, 2))
    a["w_mod"] = i["w_mod"]
    a["b_mod"] = np.ascontiguousarray(i["b_mod"].reshape(DEPTH, NMOD * KD, P).transpose(0, 2, 1))
    a["norm_g"] = np.ascontiguousarray(i["norm_g"].reshape(DEPTH, 2 * KD, P).transpose(0, 2, 1))
    a["w_in"] = i["w_in"]
    a["ident"] = np.eye(P, dtype=f)
    a["lb_logits"] = np.ascontiguousarray(i["hgrn_lb_logits"].reshape(DEPTH * 4, P).T)
    a["layer_const"] = np.array([[min(l, 1), (min(l, 1) - 1) * 1e30, LAM_INIT[l], 1 - LAM_INIT[l]]
                                 for l in range(2)], dtype=f)
    a["state"] = i["state_hgrn"][0].reshape(2, 2, 2, P, DQ)
    a["hgrn_norm_g"] = i["hgrn_norm_g"]
    mask = np.zeros((P, 2, len(LEVELS) + 2, 64), np.uint32)
    key = np.arange(P)[:, None]
    col = np.arange(64)
    for n, h in enumerate(LEVELS):
        blk = (col // h)[None]
        mask[:, 0, n] = (key // (2 * h) == blk) & (key % (2 * h) < h)
        mask[:, 1, n] = (key // (2 * h) == blk) & (key % (2 * h) >= h)
    for par in range(2):
        mask[:, :, len(LEVELS) + par] = (key == 2 * col + par)[:, None]
    a["hg_mask"] = mask
    pos = np.arange(LAT)
    sub = np.arange(P) % DQ
    inv = (f(10000.0) ** (-np.arange(0, 32, 2).astype(f) / f(32))).astype(f)
    where = np.where((sub < 32)[:, None], (pos // 64)[None], (pos % 64)[None]).astype(f)
    ang = where * inv[sub % 16][:, None]
    a["rope_cos"] = np.cos(ang).astype(f)
    a["rope_sin"] = (np.sin(ang) * np.where(sub % 32 < 16, -1, 1)[:, None]).astype(f)
    a["cache_k"] = i["cache_diff_k"][0]
    a["cache_v"] = i["cache_diff_v"][0]
    a["diff_lambda"] = i["diff_lambda"].reshape(DEPTH, 4 * DQ)
    a["diff_subln_g"] = i["diff_subln_g"]
    a["hy_w1"], a["hy_w2"], a["hy_w3"] = i["hy_filt_w1"], i["hy_filt_w2"], i["hy_filt_w3"]
    a["hy_bf"] = np.stack([i["hy_filt_b1"], i["hy_filt_b2"], i["hy_filt_freq"][:, 0], i["hy_filt_freq"][:, 1]], axis=-1)
    a["hy_conv_w"] = np.ascontiguousarray(i["hy_conv_w"].reshape(DEPTH, 3, 6, P).transpose(0, 3, 2, 1).reshape(DEPTH, P, 18))
    a["hy_conv_b"] = np.ascontiguousarray(i["hy_conv_b"].reshape(DEPTH, 6, P).transpose(0, 2, 1))
    a["hy_skip"] = np.ascontiguousarray(i["hy_skip"].reshape(DEPTH, 4, P).transpose(0, 2, 1))
    a["row_number"] = np.arange(P, dtype=f)[:, None]
    a["alt"] = np.where(np.arange(P) % 2, -1, 1).astype(f)[:, None]
    lo, hi = math.log(1e-2) / 1.5, math.log(1e-2) / 0.3
    deltas = np.linspace(lo, hi, HYW, dtype=f)
    for name, length in (("lat", LAT), ("ctx", CTX)):
        t = np.linspace(0.0, 1.0, length, dtype=f)[:, None]
        fr = np.linspace(1e-4, (POS - 1) // 2 - 1, (POS - 1) // 2, dtype=f)[None]
        w = (f(2.0 * math.pi) * np.arange(length, dtype=f)[:, None] / f(length)).astype(f)
        a[f"pos_{name}"] = np.ascontiguousarray(np.concatenate([t, np.cos(fr * w), -np.sin(fr * w)], axis=-1).T)
        a[f"decay_{name}"] = np.ascontiguousarray(np.exp(-t * np.abs(deltas)).astype(f)
                                                  .reshape(length // P, P, HYW).transpose(1, 0, 2))
        n = np.arange(length)
        ang = np.pi * (np.outer(n, n) % (2 * length)) / length
        a[f"dft_cos_{name}"] = np.cos(ang).astype(f)
        sin = np.sin(ang)
        sin[:, 0] = np.where(n % 2, -1, 1)
        a[f"dft_sin_{name}"] = sin.astype(f)
        a[f"dft_sin_t_{name}"] = np.ascontiguousarray(sin.T.astype(f))
    for n in ("w_out", "w_router", "w_gate", "w_up", "w_down", "final_norm_g"):
        a[n] = i[n]
    return a


OUTS = {"x": (TOK, D), "k": (DEPTH, HEADS, 2, CTX, DQ), "v": (DEPTH, HEADS, CTX, DV),
        "s": (DEPTH, 2, HEADS, DQ, DQ)}


def kernel(**inputs):
    import concourse.bacc as bacc
    from concourse.bass_utils import run_bass_kernel_spmd

    nc = bacc.Bacc("TRN2", target_bir_lowering=False, num_devices=1)
    arrays = {n: np.ascontiguousarray(a) for n, a in host_arrays(inputs).items()}
    ins = {n: nc.dram_tensor("in_" + n, a.shape, mybir.dt.from_np(a.dtype), kind="ExternalInput").ap()
           for n, a in arrays.items()}
    outs = {n: nc.dram_tensor("out_" + n, shape, F32, kind="ExternalOutput").ap() for n, shape in OUTS.items()}
    build(nc, ins, outs)
    r = run_bass_kernel_spmd(nc, [{"in_" + n: a for n, a in arrays.items()}], core_ids=[0]).results[0]
    x = r["out_x"]
    return (x[LAT:][None], x[:LAT][None], r["out_k"][None], r["out_v"][None], r["out_s"][None])
```

```python
import math
from contextlib import ExitStack, contextmanager

import numpy as np

import concourse.bass as bass
from concourse import mybir

F32 = mybir.dt.float32
U32 = mybir.dt.uint32
I32 = mybir.dt.int32
ALU = mybir.AluOpType
ACT = mybir.ActivationFunctionType
AX = mybir.AxisListType

P = 128
D = 1024
KD = D // P
LAT, CTX = 1024, 128
TOK = LAT + CTX
NT = TOK // P
LT = LAT // P
DEPTH = 2
PAST = 256
D_IN = 3584
NMOD = 6
HEADS = 4
DQ = 64
DV = 128
HYW = 256
HID = 64
POS = 33
E = 16
CAP_L, CAP_P = 2 * LAT // E, 2 * CTX // E
CAP = CAP_L + CAP_P
FF = 1024
EPS = 1e-6
LEVELS = [64, 32, 16, 8, 4, 2, 1]
TC = 384
LAM_INIT = [0.8 - 0.6 * math.exp(-0.3 * l) for l in range(DEPTH)]


class Count:

    def __init__(self, sem):
        self.sem, self.n = sem, 0

    def done(self, ins):
        self.n += 1
        ins.then_inc(self.sem, 1)
        return self.n

    def then_wait(self, engine, ins):
        self.done(ins)
        engine.wait_ge(self.sem, self.n)


@contextmanager
def stage(nc, m, *names):
    with ExitStack() as ctx:
        sems = {n: ctx.enter_context(nc.semaphore(n)) for n in names if n[:3] != "sw_"}
        sems.update({n: m.sw_sems[n] for n in names if n[:3] == "sw_"})
        with nc.Block() as block:
            yield block, sems
        soft = [n for n in names if n[:3] == "sw_"]
        if soft:
            nc.gpsimd.dma_reset()
            nc.all_engine_barrier()
        for s in sems.values():
            nc.sync.sem_clear(s)
        nc.all_engine_barrier()


def modulation(nc, m, l):
    NBUF, PC = 6, 512
    HB = NMOD * D // PC
    with stage(nc, m, *(f"w_loaded{b}" for b in range(NBUF)), "w_used", "small_loaded", "rows_kept", "turned",
               "mod_ready") as (block, s):
        @block.sync
        def _(sp):
            sp.dma_start(m.b_mod[:, :], m.d["b_mod"][l]).then_inc(s["small_loaded"], 16)
            sp.dma_start(m.norm_g[:, :], m.d["norm_g"][l]).then_inc(s["small_loaded"], 16)
            w = m.d["w_mod"][l].rearrange("(k p) (b n) -> b p k n", p=P, n=PC)
            for b in range(HB):
                if b >= NBUF:
                    sp.wait_ge(s["w_used"], b - NBUF + 1)
                sp.dma_start(m.wbuf[:, b % NBUF], w[b]).then_inc(s[f"w_loaded{b % NBUF}"], 16)

        @block.tensor
        def _(pe):
            def turn(b):
                pe.wait_ge(s["rows_kept"], b + 1)
                for q in range(PC // P):
                    at = 3584 + (b * (PC // P) + q) * 2
                    last = nc.tensor.transpose(m.ps[:, at:at + 2],
                                               m.mod_rows[0:2, b * PC + q * P:b * PC + (q + 1) * P], m.ident[0:2, 0:2])
                last.then_inc(s["turned"], 1)

            for b in range(HB):
                pe.wait_ge(s[f"w_loaded{b % NBUF}"], 16 * (b // NBUF + 1))
                if b >= 4:
                    pe.wait_ge(s["rows_kept"], b - 3)
                for k in range(KD):
                    last = nc.tensor.matmul(m.ps[0:2, (b % 4) * 512:(b % 4 + 1) * 512], m.cond[:, k, :],
                                            m.wbuf[:, b % NBUF, k, :], start=(k == 0), stop=(k == KD - 1))
                last.then_inc(s["w_used"], 1)
                if b >= 1:
                    turn(b - 1)
            turn(HB - 1)

        @block.scalar
        def _(act):
            for b in range(HB):
                act.wait_ge(s["w_used"], b + 1)
                nc.scalar.activation(m.mod_rows[0:2, b * PC:(b + 1) * PC],
                                     m.ps[0:2, (b % 4) * 512:(b % 4 + 1) * 512], ACT.Copy).then_inc(s["rows_kept"], 1)

        @block.vector
        def _(dve):
            dve.wait_ge(s["small_loaded"], 32)
            dve.wait_ge(s["turned"], HB)
            c = Count(s["mod_ready"])
            c.then_wait(dve, nc.vector.tensor_tensor(
                m.mod[:, :, :], m.ps[:, 3584:3584 + 2 * NMOD * KD].rearrange("p (j g) -> p j g", g=2),
                m.b_mod[:, :].unsqueeze(2).to_broadcast([P, NMOD * KD, 2]), ALU.add))
            for n in range(2):
                sc = m.mod[:, (3 * n + 1) * KD:(3 * n + 2) * KD, :]
                g = m.norm_g[:, n * KD:(n + 1) * KD].unsqueeze(2).to_broadcast([P, KD, 2])
                nc.vector.scalar_tensor_tensor(sc, sc, 1.0, g, ALU.add, ALU.mult)


def norm_to_channels(nc, m, l, n):
    shift, scale = 3 * n * KD, (3 * n + 1) * KD
    G = 3
    with stage(nc, m, *(f"x_loaded{t}" for t in range(NT)), "squared", "mean", "root", "inverse", "row_normed",
               "transposed", "h_ready", "h_ready_act", "stored",
               "next_w") as (block, s):
        @block.sync
        def _(sp):
            for t in range(NT):
                sp.dma_start(m.xbuf[:, t], m.x_dram[t * P:(t + 1) * P, :]).then_inc(s[f"x_loaded{t}"], 16)
            if n == 0:
                for b in range(2):
                    sp.dma_start(m.W[:, b], w_in_blocks(m, l)[b]).then_inc(s["next_w"], 16)
                sp.wait_ge(s["next_w"], 32)
            if n == 1:
                for t in range(NT):
                    sp.wait_ge(s["row_normed"], t + 1)
                    sp.dma_start(m.xn_dram[t * P:(t + 1) * P, :], m.xbuf[:, t]).then_inc(s["stored"], 16)
                sp.wait_ge(s["stored"], 16 * NT)

        @block.scalar
        def _(act):
            def squares(a):
                for t in range(a * G, (a + 1) * G):
                    act.wait_ge(s[f"x_loaded{t}"], 16)
                    if t >= 1:
                        act.wait_ge(s["squared"], t)
                    nc.scalar.activation(m.sq[:, :], m.xbuf[:, t], ACT.Square,
                                         accum_out=m.ss[:, t:t + 1]).then_inc(s["squared"], 1)
                act.wait_ge(s["mean"], a + 1)
                nc.scalar.activation(m.rt[:, a * G:(a + 1) * G], m.ms[:, a * G:(a + 1) * G], ACT.Sqrt)                    .then_inc(s["root"], 1)

            def shape_h(a):
                for t in range(a * G, (a + 1) * G):
                    g = 0 if t < LT else 1
                    act.wait_ge(s["transposed"], 2 * t + 1)
                    for k in range(4):
                        at = (t % 4) * 1024 + k * P
                        last = nc.scalar.activation(m.hT[:, k, t * P:(t + 1) * P], m.ps[:, at:at + P], ACT.Identity,
                                                    bias=m.mod[:, shift + k, g:g + 1],
                                                    scale=m.mod[:, scale + k, g:g + 1])
                    last.then_inc(s["h_ready_act"], 1)

            squares(0)
            squares(1)
            shape_h(0)
            squares(2)
            shape_h(1)
            shape_h(2)

        @block.vector
        def _(dve):
            def inverse(a):
                r = slice(a * G, (a + 1) * G)
                dve.wait_ge(s["squared"], (a + 1) * G)
                nc.vector.tensor_scalar(m.ms[:, r], m.ss[:, r], 1.0 / D, EPS, ALU.mult, ALU.add)                    .then_inc(s["mean"], 1)
                dve.wait_ge(s["root"], a + 1)
                nc.vector.reciprocal(m.rs[:, r], m.rt[:, r]).then_inc(s["inverse"], 1)
                dve.wait_ge(s["inverse"], a + 1)

            def norm_row(t):
                nc.vector.tensor_scalar(m.xbuf[:, t], m.xbuf[:, t], m.rs[:, t:t + 1], None,
                                        ALU.mult).then_inc(s["row_normed"], 1)

            def shape_h(t):
                g = 0 if t < LT else 1
                dve.wait_ge(s["transposed"], 2 * t + 2)
                for k in range(4, 8):
                    at = (t % 4) * 1024 + k * P
                    last = nc.vector.tensor_scalar(m.hT[:, k, t * P:(t + 1) * P], m.ps[:, at:at + P],
                                                   m.mod[:, scale + k, g:g + 1], m.mod[:, shift + k, g:g + 1],
                                                   ALU.mult, ALU.add)
                last.then_inc(s["h_ready"], 1)

            inverse(0)
            for t in range(G):
                norm_row(t)
            for a in range(1, NT // G):
                inverse(a)
                for t in range(a * G, (a + 1) * G):
                    norm_row(t)
                    shape_h(t - G)
            for t in range(NT - G, NT):
                shape_h(t)

        @block.tensor
        def _(pe):
            for t in range(NT):
                pe.wait_ge(s["row_normed"], t + 1)
                if t >= 4:
                    pe.wait_ge(s["h_ready"], t - 3)
                    pe.wait_ge(s["h_ready_act"], t - 3)
                for k in range(KD):
                    last = nc.tensor.transpose(m.ps[:, (t % 4) * 1024 + k * P:(t % 4) * 1024 + (k + 1) * P],
                                               m.xbuf[:, t, k * P:(k + 1) * P], m.ident[:, :])
                    if k in (3, 7):
                        last.then_inc(s["transposed"], 1)


def zc_slot(j):
    if j < 6:
        return "c", j
    if j < 10:
        return "t", (j - 6) * P
    if j < 18:
        return "c", j - 4
    if j < 22:
        return "t", (j - 14) * P
    return "d", j - 22


def w_in_blocks(m, l):
    return m.d["w_in"][l].rearrange("(k p) (b n) -> b p k n", p=P, n=4 * P)


def projection(nc, m, l):
    NB, BC = 7, 4
    jobs = []
    for j in range(NB * BC):
        kind, at = zc_slot(j)
        if kind == "t":
            if j % 2 == 0:
                jobs += [("t", j, at, t) for t in range(NT)]
        else:
            jobs.append((kind, j, at, 0))
    chan = [x for x in jobs if x[0] != "t"]
    tok = [x for x in jobs if x[0] == "t"]
    with stage(nc, m, "w_loaded0", "w_loaded1", "w_used", "chan_done", "chan_taken", "tok_done", "tok_taken",
               "hy_stored0", "hy_stored1") as (block, s):
        w = w_in_blocks(m, l)
        first_hy = next(i for i, x in enumerate(chan) if x[0] == "d")

        @block.sync
        def _(sp):
            for b in range(2, NB):
                sp.wait_ge(s["w_used"], b - 1)
                sp.dma_start(m.W[:, b % 2], w[b]).then_inc(s[f"w_loaded{b % 2}"], 16)
            for i in range(6):
                sp.wait_ge(s["chan_taken"], first_hy + i + 1)
                sp.dma_start(m.zhy_dram[i * P:(i + 1) * P, :], m.zstage[:, i % 2]).then_inc(s[f"hy_stored{i % 2}"], 16)
            sp.wait_ge(s["hy_stored0"], 16 * 3)
            sp.wait_ge(s["hy_stored1"], 16 * 3)

        @block.tensor
        def _(pe):
            for b in range(2):
                pe.sem_inc(s[f"w_loaded{b}"], 16)
            nchan = ntok = 0
            for kind, j, at, t in jobs:
                b, jj = divmod(j, BC)
                pe.wait_ge(s[f"w_loaded{b % 2}"], 16 * (b // 2 + 1))
                if kind != "t":
                    if nchan >= 2:
                        pe.wait_ge(s["chan_taken"], nchan - 1)
                    base = (nchan % 2) * 3 * 512
                    for q in range(3):
                        for k in range(KD):
                            last = nc.tensor.matmul(m.ps[:, base + q * 512:base + q * 512 + TC],
                                                    m.W[:, b % 2, k, jj * P:(jj + 1) * P],
                                                    m.hT[:, k, q * TC:(q + 1) * TC],
                                                    start=(k == 0), stop=(k == KD - 1))
                    last.then_inc(s["chan_done"], 1)
                    nchan += 1
                else:
                    if ntok >= 2:
                        pe.wait_ge(s["tok_taken"], ntok - 1)
                    base = (6 + ntok % 2) * 512
                    for k in range(KD):
                        last = nc.tensor.matmul(m.ps[:, base:base + 256], m.hT[:, k, t * P:(t + 1) * P],
                                                m.W[:, b % 2, k, jj * P:(jj + 2) * P],
                                                start=(k == 0), stop=(k == KD - 1))
                    last.then_inc(s["tok_done"], 1)
                    ntok += 1
                if jj == BC - 1 or (kind == "t" and jj == BC - 2 and t == NT - 1):
                    if kind == "t":
                        pe.wait_ge(s["tok_done"], ntok)
                    else:
                        pe.wait_ge(s["chan_done"], nchan)
                    pe.sem_inc(s["w_used"], 1)

        @block.scalar
        def _(act):
            for i, (kind, j, at, _) in enumerate(chan):
                act.wait_ge(s["chan_done"], i + 1)
                if kind == "d" and at >= 2:
                    act.wait_ge(s[f"hy_stored{at % 2}"], 16 * (at // 2))
                out = m.zc[:, at] if kind == "c" else m.zstage[:, at % 2]
                scale = DQ ** -0.5 if 10 <= j < 14 else 1.0
                base = (i % 2) * 3 * 512
                nc.scalar.activation(out.rearrange("p (q n) -> p q n", n=TC),
                                     m.ps[:, base:base + 1536].rearrange("p (q n) -> p q n", n=512)[:, :, 0:TC],
                                     ACT.Copy, scale=scale).then_inc(s["chan_taken"], 1)

        @block.vector
        def _(dve):
            for i, (_, j, at, t) in enumerate(tok):
                dve.wait_ge(s["tok_done"], i + 1)
                base = (6 + i % 2) * 512
                nc.vector.tensor_copy(m.zt[:, t, at:at + 256], m.ps[:, base:base + 256]).then_inc(s["tok_taken"], 1)

def hgrn_gates(nc, m, l):
    lb = m.lb
    with stage(nc, m, "loaded", "dve_small", "act_small", "softplus_x", "logsig", "keys", "diff",
               "softplus_d", "act_step", "gate_step") as (block, s):
        T1 = [m.qe[:, i] for i in range(4)]
        T2 = [m.ke_t.rearrange("p c i n -> p (c i n)")[:, i * TOK:(i + 1) * TOK] for i in range(4)]
        T3 = [m.A.rearrange("p i c n -> p (i c n)")[:, i * TOK:(i + 1) * TOK] for i in range(4)]
        f = [m.zc[:, 2 + i] for i in range(4)]

        @block.sync
        def _(sp):
            sp.dma_start(lb[:, 0:8], m.d["lb_logits"]).then_inc(s["loaded"], 16)
            sp.dma_start(m.lay[:, :], m.d["layer_const"][l].partition_broadcast(P)).then_inc(s["loaded"], 16)

        @block.vector
        def _(dve):
            c = Count(s["dve_small"])
            dve.wait_ge(s["loaded"], 32)
            c.then_wait(dve, nc.vector.tensor_tensor(lb[:, 8:12], lb[:, 4:8], lb[:, 0:4], ALU.subtract))
            c.then_wait(dve, nc.vector.scalar_tensor_tensor(lb[:, 12:16], lb[:, 8:12], -1.0, lb[:, 8:12],
                                                            ALU.mult, ALU.max))
            dve.wait_ge(s["act_small"], 2)
            c.then_wait(dve, nc.vector.scalar_tensor_tensor(lb[:, 16:20], lb[:, 8:12], 0.0, lb[:, 12:16],
                                                            ALU.min, ALU.subtract))
            c.then_wait(dve, nc.vector.scalar_tensor_tensor(lb[:, 20:24], lb[:, 8:12], 0.0, lb[:, 12:16],
                                                            ALU.max, ALU.add))
            c.then_wait(dve, nc.vector.tensor_scalar(lb[:, 24:28], lb[:, 16:20], m.lay[:, 0:1], m.lay[:, 1:2],
                                                     ALU.mult, ALU.add))
            c.then_wait(dve, nc.vector.tensor_scalar(lb[:, 28:32], lb[:, 20:24], m.lay[:, 0:1], -1.0,
                                                     ALU.mult, ALU.mult))
            c.then_wait(dve, nc.vector.tensor_tensor(lb[:, 32:36], lb[:, 28:32], lb[:, 24:28], ALU.subtract))
            for i in range(4):
                dve.wait_ge(s["softplus_x"], i + 1)
                nc.vector.scalar_tensor_tensor(T3[i], f[i], 0.0, T2[i], ALU.max, ALU.add)
                nc.vector.scalar_tensor_tensor(T1[i], f[i], 0.0, T2[i], ALU.min, ALU.subtract)\
                    .then_inc(s["logsig"], 1)
            dve.wait_ge(s["keys"], 4)
            g = Count(s["gate_step"])
            nc.vector.memset(m.A[:, :, :, 0], 0.0)
            for i in range(4):
                dve.wait_ge(s["diff"], i + 1)
                g.done(nc.vector.tensor_scalar(T1[i], T1[i], lb[:, 28 + i:29 + i], lb[:, 24 + i:25 + i],
                                               ALU.add, ALU.max))
            for i in range(4):
                dve.wait_ge(s["softplus_d"], i + 1)
                dve.wait_ge(s["gate_step"], i + 1)
                g.done(nc.vector.tensor_tensor(m.A[:, i, :, 1:], T1[i].rearrange("p (c t) -> p c t", t=P),
                                               T2[i].rearrange("p (c t) -> p c t", t=P), ALU.add))
            for i in range(4):
                dve.wait_ge(s["gate_step"], 4 + i + 1)
                for ch in range(NT):
                    nc.vector.tensor_tensor_scan(m.A[:, i, ch, 1:], m.ones[:, :], m.A[:, i, ch, 1:], 0.0,
                                                 ALU.mult, ALU.add)

        @block.scalar
        def _(act):
            c = Count(s["act_step"])
            act.wait_ge(s["dve_small"], 2)
            nc.scalar.activation(lb[:, 12:16], lb[:, 12:16], ACT.Exp, scale=-1.0).then_inc(s["act_small"], 1)
            act.wait_ge(s["act_small"], 1)
            nc.scalar.activation(lb[:, 12:16], lb[:, 12:16], ACT.Ln, bias=1.0).then_inc(s["act_small"], 1)

            def softplus(out):
                for i in range(4):
                    act.wait_ge(s["act_step"], c.n - 3)
                    c.done(nc.scalar.activation(T2[i], T2[i], ACT.Exp, scale=-1.0))
                for i in range(4):
                    act.wait_ge(s["act_step"], c.n - 3 + i)
                    nc.scalar.activation(T2[i], T2[i], ACT.Ln, bias=1.0).then_inc(s[out], 1)

            for i in range(4):
                c.done(nc.scalar.activation(T2[i], f[i], ACT.Abs))
            softplus("softplus_x")
            act.wait_ge(s["dve_small"], 7)
            for i in range(4):
                act.wait_ge(s["logsig"], i + 1)
                nc.scalar.activation(T2[i], T1[i], ACT.Abs, bias=lb[:, 32 + i:33 + i]).then_inc(s["diff"], 1)
            act.wait_ge(s["diff"], 4)
            softplus("softplus_d")
            for i in range(4):
                act.wait_ge(s["logsig"], i + 1)
                nc.scalar.activation(f[i], T3[i], ACT.Exp, bias=lb[:, 28 + i:29 + i], scale=-1.0)\
                    .then_inc(s["keys"], 1)


def hgrn_states(nc, m, l):
    def A(i, off):
        return m.A[:, i, :, off:off + P]

    def end(i):
        return m.A[:, i, :, P:P + 1].to_broadcast([P, NT, P])

    def tiles(x):
        return x.rearrange("p (c t) -> p c t", t=P)

    with stage(nc, m, "state_loaded", "rest", "from_a", "from_rest", "queries", "keys", "transposed", "keys_taken",
               "decay", "update", "chained", "stored", "cleared") as (block, s):
        steps = []
        for n in range(LT - 1):
            steps.append([(0, n), (1, LT - 1 - n)])
        steps.append([(0, LT), (1, LT)])

        @block.sync
        def _(sp):
            sp.wait_ge(s["cleared"], 1)
            for d in range(2):
                for ct in range(2):
                    for hh in range(2):
                        r, cols = slice(hh * DQ, (hh + 1) * DQ), slice(hh * DQ, (hh + 1) * DQ)
                        sp.dma_start(m.S[d][r, ct, 0 if d == 0 else LT - 1, cols], m.d["state"][l, d, ct, r, :])\
                            .then_inc(s["state_loaded"], 16)
            sp.wait_ge(s["chained"], 8 * LT)
            for d in range(2):
                for ct in range(2):
                    for hh in range(2):
                        r = slice(hh * DQ, (hh + 1) * DQ)
                        sp.dma_start(m.o["s"][l, d, 2 * ct + hh], m.S[d][r, ct, LT, r]).then_inc(s["stored"], 16)
            sp.wait_ge(s["stored"], 128)

        @block.gpsimd
        def _(pool):
            for d in range(2):
                last = nc.gpsimd.memset(m.S[d][:, :, :, :], 0.0)
            last.then_inc(s["cleared"], 1)

        @block.vector
        def _(dve):
            for i in range(4):
                if i >= 2:
                    dve.wait_ge(s["transposed"], i - 1)
                    dve.wait_ge(s["queries"], i - 1)
                if i < 2:
                    nc.vector.tensor_tensor(tiles(m.E[:, i % 2, 0:TOK]), end(i), A(i, 1), ALU.subtract)\
                        .then_inc(s["rest"], 1)
                else:
                    nc.vector.tensor_tensor(tiles(m.E[:, i % 2, 0:TOK]), end(i), A(i, 0), ALU.subtract)\
                        .then_inc(s["rest"], 1)
                wq, wk = (m.X, m.E) if i < 2 else (m.E, m.X)
                dve.wait_ge(s["from_a"], i + 1)
                dve.wait_ge(s["from_rest"], i + 1)
                nc.vector.tensor_tensor(m.qe[:, i], m.zc[:, i % 2], wq[:, i % 2, 0:TOK], ALU.mult)\
                    .then_inc(s["queries"], 1)
                nc.vector.tensor_tensor(wk[:, i % 2, 0:TOK], m.zc[:, 2 + i], wk[:, i % 2, 0:TOK], ALU.mult)\
                    .then_inc(s["keys"], 1)
            dve.wait_ge(s["state_loaded"], 128)
            dve.wait_ge(s["cleared"], 1)
            dve.wait_ge(s["decay"], 1)
            dve.wait_ge(s["update"], len(steps))
            for n, pair in enumerate(steps):
                for d, ch in pair:
                    for ct in range(2):
                        i = 2 * d + ct
                        if n and ch != LT:
                            dve.wait_ge(s["chained"], 8 * (n - 1) + 2 * i + 2)
                        for hh in range(2):
                            r = slice(hh * DQ, (hh + 1) * DQ)
                            u = m.ps[r, (n * 4 + i) * DQ:(n * 4 + i + 1) * DQ]
                            if ch == LT:
                                nc.vector.tensor_copy(m.S[d][r, ct, ch, r], u).then_inc(s["chained"], 1)
                            else:
                                nxt = ch + 1 if d == 0 else ch - 1
                                nc.vector.scalar_tensor_tensor(m.S[d][r, ct, nxt, r], m.S[d][r, ct, ch, r],
                                                               m.dec[r, i, ch:ch + 1], u, ALU.mult, ALU.add)\
                                    .then_inc(s["chained"], 1)

        @block.scalar
        def _(act):
            def take(i):
                act.wait_ge(s["transposed"], i + 1)
                nc.scalar.activation(m.ke_t[:, :, i, :],
                                     m.ps[:, (i % 2) * 1536:(i % 2) * 1536 + TOK].rearrange("p (c n) -> p c n", n=P),
                                     ACT.Copy).then_inc(s["keys_taken"], 1)
            nc.scalar.activation(m.dec[:, :, :], m.A[:, :, :, P], ACT.Exp).then_inc(s["decay"], 1)
            for i in range(4):
                if i >= 2:
                    take(i - 2)
                    act.wait_ge(s["queries"], i - 1)
                nc.scalar.activation(tiles(m.X[:, i % 2, 0:TOK]), A(i, 1 if i < 2 else 0), ACT.Exp)\
                    .then_inc(s["from_a"], 1)
                act.wait_ge(s["rest"], i + 1)
                nc.scalar.activation(m.E[:, i % 2, 0:TOK], m.E[:, i % 2, 0:TOK], ACT.Exp)\
                    .then_inc(s["from_rest"], 1)
            take(2)
            take(3)

        @block.tensor
        def _(pe):
            for i in range(4):
                pe.wait_ge(s["keys"], i + 1)
                if i >= 2:
                    pe.wait_ge(s["keys_taken"], i - 1)
                src = (m.E if i < 2 else m.X)[:, i % 2]
                for ch in range(NT):
                    at = (i % 2) * 1536 + ch * P
                    last = nc.tensor.transpose(m.ps[:, at:at + P], src[:, ch * P:(ch + 1) * P], m.ident[:, :])
                last.then_inc(s["transposed"], 1)
            pe.wait_ge(s["keys_taken"], 4)
            for n, pair in enumerate(steps):
                for d, ch in pair:
                    for ct in range(2):
                        i = 2 * d + ct
                        at = (n * 4 + i) * DQ
                        for hh in range(2):
                            h = 2 * ct + hh
                            last = nc.tensor.matmul(m.ps[hh * DQ:(hh + 1) * DQ, at:at + DQ],
                                                    m.ke_t[:, ch, i, hh * DQ:(hh + 1) * DQ],
                                                    m.zt[:, ch, h * DQ:(h + 1) * DQ], start=True, stop=True)
                last.then_inc(s["update"], 1)


def hgrn_outputs(nc, m, l):
    NL = len(LEVELS) + 2
    seq = []
    for ct in range(2):
        seq += [(ct, d, lev) for d in range(2) for lev in range(len(LEVELS))]
        seq += [(ct, 1, lev) for lev in range(len(LEVELS), NL)]

    def halves(x, h):
        v = x.rearrange("p (c b two j) -> p c b two j", c=NT, two=2, j=h)
        return v[:, :, :, 0, :], v[:, :, :, 1, :]

    def queries(b, hh, h):
        return m.xq[hh * DQ:(hh + 1) * DQ, b, :, hh].rearrange("p c (b j) -> p c b j", j=h)

    with stage(nc, m, "mask_loaded", "att_cleared", "span_lo", "span", "cleared", "weight", "operand", "plain", "scores", "placed",
               "out_done", "out_taken") as (block, s):
        @block.sync
        def _(sp):
            sp.dma_start(m.mask[:, :, :, :], m.d["hg_mask"]).then_inc(s["mask_loaded"], 16)

        @block.vector
        def _(dve):
            dve.wait_ge(s["mask_loaded"], 16)
            dve.wait_ge(s["cleared"], 1)

            def span(n):
                ct, d, lev = seq[n]
                if lev >= len(LEVELS):
                    return
                i, h, b = 2 * d + ct, LEVELS[lev], n % 2
                if n >= 2:
                    dve.wait_ge(s["operand"], ops[n - 2])
                a = m.A[:, i]
                nb = P // (2 * h)
                lo, hi = halves(m.E[:, b, 0:TOK], h)
                mid = a[:, :, 0:P].rearrange("p c (b w) -> p c b w", w=2 * h)[:, :, :, h:h + 1]\
                    .to_broadcast([P, NT, nb, h])
                shift = 1 if d == 0 else 0
                w = a[:, :, shift:shift + P].rearrange("p c (b two j) -> p c b two j", two=2, j=h)
                left, right = w[:, :, :, 0, :], w[:, :, :, 1, :]
                nc.vector.tensor_tensor(lo, mid, left, ALU.subtract).then_inc(s["span_lo"], 1)
                nc.vector.tensor_tensor(hi, right, mid, ALU.subtract).then_inc(s["span"], 1)

            def operands(n):
                ct, d, lev = seq[n]
                if lev >= len(LEVELS):
                    return
                i, h, b = 2 * d + ct, LEVELS[lev], n % 2
                if n >= 2:
                    dve.wait_ge(s["scores"], n - 1)
                lo, hi = halves(m.E[:, b, 0:TOK], h)
                dve.wait_ge(s["weight"], ops[n])
                xlo, xhi = halves(m.X[:, b, 0:TOK], h)
                qlo, qhi = halves(m.zc[:, ct], h)
                klo, khi = halves(m.zc[:, 2 + i], h)
                keys, wk, k0, wq, q0 = (xlo, lo, klo, hi, qhi) if d == 0 else (xhi, hi, khi, lo, qlo)
                nc.vector.tensor_tensor(keys, wk, k0, ALU.mult)
                for hh in range(2):
                    r = slice(hh * DQ, (hh + 1) * DQ)
                    last = nc.vector.tensor_tensor(queries(b, hh, h), wq[r], q0[r], ALU.mult)
                last.then_inc(s["operand"], 1)

            def place(n):
                ct, d, lev = seq[n]
                dve.wait_ge(s["scores"], n + 1)
                if (d, lev) == (0, 0):
                    dve.wait_ge(s["att_cleared"], ct + 1)
                else:
                    dve.wait_ge(s["placed"], n)
                att = m.att[:, ct]
                h = LEVELS[lev] if lev < len(LEVELS) else 1
                dat = m.ps[:, (n % 2) * 2048:(n % 2) * 2048 + TOK]\
                    .rearrange("p (c hh b j) -> p hh c b j", c=NT, hh=2, j=h)
                msk = m.mask[:, d, lev].rearrange("p (b j) -> p b j", j=h)
                half = (1 if d == 0 else 0) if lev < len(LEVELS) else lev - len(LEVELS)
                out = att.rearrange("p hh c (b two j) -> p hh c b two j", two=2, j=h)[:, :, :, :, half, :]
                msk = msk.unsqueeze(1).unsqueeze(1).to_broadcast([P, 2, NT, 64 // h, h])
                nc.vector.copy_predicated(out, msk, dat).then_inc(s["placed"], 1)

            ops = [sum(lev < len(LEVELS) for _, _, lev in seq[:n + 1]) for n in range(len(seq))]
            span(0)
            span(1)
            operands(0)
            for n in range(len(seq)):
                if n + 2 < len(seq):
                    span(n + 2)
                if n + 1 < len(seq):
                    operands(n + 1)
                place(n)

        @block.gpsimd
        def _(pool):
            nc.gpsimd.memset(m.X[:, :, :], 0.0)
            nc.gpsimd.memset(m.xq[:, :, :, :, :], 0.0).then_inc(s["cleared"], 1)
            for ct in range(2):
                nc.gpsimd.memset(m.att[:, ct], 0.0).then_inc(s["att_cleared"], 1)

        @block.scalar
        def _(act):
            k = 0
            out_n = 0

            def take(ct):
                nonlocal out_n
                for c0 in range(0, NT, 4):
                    nch = min(4, NT - c0)
                    act.wait_ge(s["out_done"], out_n + 1)
                    at = c0 * P
                    nc.scalar.activation(m.o_sb[:, c0:c0 + nch, ct * P:(ct + 1) * P],
                                         m.ps[:, at:at + nch * P].rearrange("p (c n) -> p c n", n=P), ACT.Copy)\
                        .then_inc(s["out_taken"], 1)
                    out_n += 1
            for n, (ct, d, lev) in enumerate(seq):
                if lev < len(LEVELS):
                    k += 1
                    act.wait_ge(s["span"], k)
                    nc.scalar.activation(m.E[:, n % 2, 0:TOK], m.E[:, n % 2, 0:TOK], ACT.Exp)\
                        .then_inc(s["weight"], 1)
                else:
                    act.wait_ge(s["scores"], n - 1)
                    for hh in range(2):
                        r = slice(hh * DQ, (hh + 1) * DQ)
                        last = nc.scalar.activation(
                            m.xq[r, n % 2, :, hh],
                            m.zc[r, ct].rearrange("p (c j two) -> p c j two", c=NT, two=2)[:, :, :, lev - len(LEVELS)],
                            ACT.Copy)
                    last.then_inc(s["plain"], 1)
                if (ct, d, lev) == (1, 0, 0):
                    take(0)
            take(1)

        @block.tensor
        def _(pe):
            ops = plain = 0
            for n, (ct, d, lev) in enumerate(seq):
                if n >= 2:
                    pe.wait_ge(s["placed"], n - 1)
                if lev < len(LEVELS):
                    ops += 1
                    pe.wait_ge(s["operand"], ops)
                else:
                    plain += 1
                    pe.wait_ge(s["plain"], plain)
                operands = [m.X[:, n % 2]] if lev < len(LEVELS) else [m.zc[:, 2 + ct], m.zc[:, 4 + ct]]
                for ch in range(NT):
                    at = (n % 2) * 2048 + ch * P
                    for keys in operands:
                        last = nc.tensor.matmul(m.ps[:, at:at + P], keys[:, ch * P:(ch + 1) * P],
                                                m.xq[:, n % 2, ch].rearrange("p hh t -> p (hh t)"),
                                                start=keys is operands[0], stop=keys is operands[-1])
                last.then_inc(s["scores"], 1)
                if (d, lev) != (1, NL - 1):
                    continue
                pe.wait_ge(s["placed"], n + 1)
                for ch in range(NT):
                    at = ch * P
                    if ch < LT:
                        for dd in range(2):
                            nc.tensor.matmul(m.ps[:, at:at + P], m.qe[:, 2 * dd + ct, ch * P:(ch + 1) * P],
                                             m.S[dd][:, ct, ch, :], start=(dd == 0), stop=False)
                    for hh in range(2):
                        h = 2 * ct + hh
                        last = nc.tensor.matmul(m.ps[:, at + hh * DQ:at + (hh + 1) * DQ], m.att[:, ct, hh, ch, :],
                                                m.zt[:, ch, h * DQ:(h + 1) * DQ], start=(ch == LT),
                                                stop=(hh == 1 or ch == LT))
                    if ch % 4 == 3 or ch == NT - 1:
                        last.then_inc(s["out_done"], 1)
                if ct == 0:
                    pe.wait_ge(s["out_taken"], 3)


def hgrn_finish(nc, m, l):
    n = NT * HEADS
    o4 = m.o_sb.rearrange("p c (h v) -> p c h v", v=DQ)
    sm = m.small[:, 0:n].rearrange("p (c h) -> p c h", h=HEADS)
    with stage(nc, m, "g_loaded", "step", "root", "gate", "out_ready", "transposed") as (block, s):
        sq = m.view(m.R_W, NT, 256)
        sq4 = sq.rearrange("p c (h v) -> p c h v", v=DQ)
        gate = m.view(m.R_W + NT * 256, NT, 256)

        @block.sync
        def _(sp):
            sp.dma_start(m.hg_gain[:, :], m.d["hgrn_norm_g"][l].partition_broadcast(P)).then_inc(s["g_loaded"], 16)

        @block.scalar
        def _(act):
            nc.scalar.activation(gate[:, :, :], m.zt[:, :, 256:512], ACT.Silu).then_inc(s["gate"], 1)
            act.wait_ge(s["step"], 3)
            nc.scalar.activation(m.small[:, 0:n], m.small[:, 0:n], ACT.Sqrt).then_inc(s["root"], 1)
            for ct in range(2):
                act.wait_ge(s["transposed"], ct + 1)
                nc.scalar.activation(m.oT[:, ct], m.ps[:, ct * 1536:ct * 1536 + TOK], ACT.Copy)

        @block.vector
        def _(dve):
            c = Count(s["step"])
            c.then_wait(dve, nc.vector.tensor_tensor(sq[:, :, :], m.o_sb[:, :, :], m.o_sb[:, :, :], ALU.mult))
            c.then_wait(dve, nc.vector.tensor_reduce(sm, sq4, AX.X, ALU.add))
            c.then_wait(dve, nc.vector.tensor_scalar(m.small[:, 0:n], m.small[:, 0:n], 1.0 / DQ, EPS, ALU.mult,
                                                     ALU.add))
            dve.wait_ge(s["root"], 1)
            c.then_wait(dve, nc.vector.reciprocal(m.small[:, 0:n], m.small[:, 0:n]))
            c.then_wait(dve, nc.vector.tensor_tensor(o4, o4, sm.unsqueeze(3).to_broadcast([P, NT, HEADS, DQ]),
                                                     ALU.mult))
            dve.wait_ge(s["g_loaded"], 16)
            c.then_wait(dve, nc.vector.tensor_tensor(o4, o4, m.hg_gain[:, :].unsqueeze(1).unsqueeze(1).to_broadcast([P, NT, HEADS, DQ]),
                                                     ALU.mult))
            dve.wait_ge(s["gate"], 1)
            nc.vector.tensor_tensor(m.o_sb[:, :, :], m.o_sb[:, :, :], gate[:, :, :], ALU.mult)\
                .then_inc(s["out_ready"], 1)

        @block.tensor
        def _(pe):
            pe.wait_ge(s["out_ready"], 1)
            for ct in range(2):
                for t in range(NT):
                    last = nc.tensor.transpose(m.ps[:, ct * 1536 + t * P:ct * 1536 + (t + 1) * P],
                                               m.o_sb[:, t, ct * P:(ct + 1) * P], m.ident[:, :])
                last.then_inc(s["transposed"], 1)

def attention_prepare(nc, m, l):
    with stage(nc, m, "tables_loaded", "keys_loaded", "values_loaded", "lambda_loaded", "shuffled", "turned", "kept",
               "transposed", "taken", "stored", "lam_step", "lam_exp", "padded", "roped", "second_kept") as (block, s):
        @block.sync
        def _(sp):
            sp.dma_start(m.cos[:, :], m.d["rope_cos"]).then_inc(s["tables_loaded"], 16)
            sp.dma_start(m.sin[:, :], m.d["rope_sin"]).then_inc(s["tables_loaded"], 16)
            sp.dma_start(m.lamv[:, :], m.d["diff_lambda"][l].partition_broadcast(P)).then_inc(s["lambda_loaded"], 16)
            for j in range(2):
                for h in range(HEADS):
                    sp.dma_start(m.kraw[:, j, h, :].rearrange("p (m d) -> p m d", d=DQ),
                                 m.d["cache_k"][l, h, :, j * P:(j + 1) * P, :].rearrange("m t d -> t m d"))\
                        .then_inc(s["keys_loaded"], 16)
            for j in range(2):
                sp.dma_start(m.vctx[:, j], m.d["cache_v"][l, :, j * P:(j + 1) * P, :].rearrange("h t v -> t h v"))\
                    .then_inc(s["values_loaded"], 16)
            sp.dma_start(m.o["v"][l].rearrange("h t v -> t h v"),
                         m.zt[:, LT, 512:1024].rearrange("p (h v) -> p h v", v=DV)).then_inc(s["stored"], 16)
            sp.wait_ge(s["taken"], 3)
            for h in range(HEADS):
                sp.dma_start(m.o["k"][l, h].rearrange("m t d -> t m d"),
                             m.kout[:, h].rearrange("p (m d) -> p m d", d=DQ)).then_inc(s["stored"], 16)
            sp.wait_ge(s["values_loaded"], 32)
            sp.wait_ge(s["stored"], 16 * (HEADS + 1))

        @block.gpsimd
        def _(pool):
            nc.gpsimd.memset(m.q1[0:DQ], 0.0).then_inc(s["padded"], 1)
            pool.wait_ge(s["tables_loaded"], 32)
            for i in range(8):
                pool.wait_ge(s["shuffled"], i + 1)
                x = m.zc[:, 6 + i, 0:LAT]
                nc.gpsimd.tensor_tensor(x, x, m.cos[:, :], ALU.mult).then_inc(s["kept"], 1)

        @block.vector
        def _(dve):
            c = Count(s["lam_step"])
            dve.wait_ge(s["lambda_loaded"], 16)
            v = m.lamv[:, :].rearrange("p (a b d) -> p a b d", a=2, b=2)
            c.then_wait(dve, nc.vector.tensor_tensor(v[:, :, 0], v[:, :, 0], v[:, :, 1], ALU.mult))
            c.then_wait(dve, nc.vector.tensor_reduce(m.lam[:, 0:2], v[:, :, 0], AX.X, ALU.add))
            dve.wait_ge(s["lam_exp"], 1)
            c.then_wait(dve, nc.vector.tensor_tensor(m.lam[:, 2:3], m.lam[:, 1:2], m.lam[:, 0:1], ALU.subtract))
            nc.vector.tensor_tensor(m.lam[:, 3:4], m.lam[:, 2:3], m.lay[:, 2:3], ALU.subtract)
            dve.wait_ge(s["tables_loaded"], 32)
            t = Count(s["turned"])
            for i in range(8):
                x = m.zc[:, 6 + i, 0:LAT]
                r = m.rot[:, i % 2]
                nc.vector.stream_shuffle(r, x, [(k + 16) % 32 for k in range(32)]).then_inc(s["shuffled"], 1)
                dve.wait_ge(s["shuffled"], i + 1)
                t.then_wait(dve, nc.vector.tensor_tensor(r, r, m.sin[:, :], ALU.mult))
                dve.wait_ge(s["kept"], i + 1)
                last = nc.vector.tensor_tensor(x, x, r, ALU.add)
                if i < HEADS:
                    last.then_inc(s["roped"], 1)
                else:
                    dve.wait_ge(s["second_kept"], i - HEADS + 1)
                    nc.vector.memset(m.zc[DQ:P, 2 + i, :], 0.0)

        @block.scalar
        def _(act):
            act.wait_ge(s["lam_step"], 2)
            nc.scalar.activation(m.lam[:, 0:2], m.lam[:, 0:2], ACT.Exp).then_inc(s["lam_exp"], 1)
            for h in range(HEADS):
                act.wait_ge(s["roped"], h + 1)
                nc.scalar.activation(m.q1[DQ:P, h], m.zc[DQ:P, 6 + h, :], ACT.Copy).then_inc(s["second_kept"], 1)
            for j in range(2):
                act.wait_ge(s["transposed"], j + 1)
                nc.scalar.activation(m.kctx[:, :, j * P:(j + 1) * P],
                                     m.ps[:, j * 512:(j + 1) * 512].rearrange("p (h n) -> p h n", n=P), ACT.Copy)\
                    .then_inc(s["taken"], 1)
            act.wait_ge(s["transposed"], 3)
            nc.scalar.activation(m.kout[:, :, :], m.ps[:, 1024:1536].rearrange("p (h n) -> p h n", n=P), ACT.Copy)\
                .then_inc(s["taken"], 1)

        @block.tensor
        def _(pe):
            pe.wait_ge(s["keys_loaded"], 16 * 8)
            for j in range(2):
                for h in range(HEADS):
                    last = nc.tensor.transpose(m.ps[:, j * 512 + h * P:j * 512 + (h + 1) * P], m.kraw[:, j, h, :],
                                               m.ident[:, :])
                last.then_inc(s["transposed"], 1)
            for h in range(HEADS):
                last = nc.tensor.transpose(m.ps[:, 1024 + h * P:1024 + (h + 1) * P], m.zc[:, 10 + h, LAT:TOK],
                                           m.ident[:, :])
            last.then_inc(s["transposed"], 1)


def attention(nc, m, l):
    jobs = [(qt, h) for qt in range(NT) for h in range(HEADS)]
    NJ = len(jobs)

    def pieces(qt, h):
        if qt == LT:
            return [(0, m.zc[:, 10 + h, LAT:TOK])]
        return [(0, m.zc[:, 10 + h, 0:512]), (512, m.zc[:, 10 + h, 512:1024]), (1024, m.kctx[:, h, :])]

    def nkeys(qt):
        return CTX if qt == LT else LAT + PAST

    def rounds(qt):
        n = nkeys(qt) // P
        return [range(a, min(a + 4, n)) for a in range(0, n, 4)]

    first_round = [0]
    for qt, _ in jobs:
        first_round.append(first_round[-1] + len(rounds(qt)))

    with stage(nc, m, "score0", "score1", "score_most0", "score_most1", "max0", "max1", "prob0", "prob1", "ratio", "combined",
               "turned", "taken", "valued", "row_out") as (block, s):
        @block.tensor
        def _(pe):
            def score(n, mp):
                if n >= NJ:
                    return
                qt, h = jobs[n]
                if n:
                    pe.wait_ge(s[f"prob{mp}"], n)
                q = (m.q1[:, h] if mp else m.zc[:, 6 + h])[:, qt * P:(qt + 1) * P]
                for col, keys in pieces(qt, h):
                    at = mp * 1536 + col
                    last = nc.tensor.matmul(m.ps[:, at:at + keys.shape[1]], q, keys, start=True, stop=True)
                    if col == 512:
                        last.then_inc(s[f"score_most{mp}"], 1)
                last.then_inc(s[f"score{mp}"], 1)

            def turn(n, r):
                qt, h = jobs[n]
                if r >= len(rounds(qt)):
                    return
                g = first_round[n] + r
                if g:
                    pe.wait_ge(s["taken"], g)
                if r < 2:
                    pe.wait_ge(s["combined"], 2 * n + (r if qt < LT else 1) + 1)
                for k, j in enumerate(rounds(qt)[r]):
                    last = nc.tensor.transpose(m.ps[:, 3072 + k * P:3072 + (k + 1) * P],
                                               m.prob[:, n % 2, 0, j * P:(j + 1) * P], m.ident[:, :])
                last.then_inc(s["turned"], 1)

            def values(n, r):
                qt, h = jobs[n]
                if r >= len(rounds(qt)):
                    return
                pe.wait_ge(s["taken"], first_round[n] + r + 1)
                if n and r == 0:
                    pe.wait_ge(s["row_out"], n)
                nk = nkeys(qt) // P
                for j in rounds(qt)[r]:
                    if qt == LT:
                        v = m.zt[:, LT, 512 + h * DV:512 + (h + 1) * DV]
                    elif j < LT:
                        v = m.zt[:, j, 512 + h * DV:512 + (h + 1) * DV]
                    else:
                        v = m.vctx[:, j - LT, h, :]
                    last = nc.tensor.matmul(m.ps[:, 3584:3584 + DV], m.aT[:, n % 2, j, :], v, start=(j == 0),
                                            stop=(j == nk - 1))
                if j == nk - 1:
                    last.then_inc(s["valued"], 1)

            score(0, 0)
            score(0, 1)
            for n in range(NJ):
                score(n + 1, 0)
                turn(n, 0)
                score(n + 1, 1)
                turn(n, 1)
                values(n, 0)
                turn(n, 2)
                values(n, 1)
                values(n, 2)

        @block.vector
        def _(dve):
            c = Count(s["ratio"])

            def maxima(n):
                if n >= NJ:
                    return
                for mp in range(2):
                    at, best = mp * 1536, m.nmax[:, n, mp:mp + 1]
                    if jobs[n][0] == LT:
                        dve.wait_ge(s[f"score{mp}"], n + 1)
                        nc.vector.tensor_reduce(best, m.ps[:, at:at + CTX], AX.X, ALU.max, negate=True)\
                            .then_inc(s[f"max{mp}"], 1)
                        continue
                    dve.wait_ge(s[f"score_most{mp}"], n + 1)
                    nc.vector.tensor_reduce(m.nmax2[:, mp, 0:1], m.ps[:, at:at + LAT], AX.X, ALU.max, negate=True)
                    dve.wait_ge(s[f"score{mp}"], n + 1)
                    c.then_wait(dve, nc.vector.tensor_reduce(m.nmax2[:, mp, 1:2], m.ps[:, at + LAT:at + LAT + PAST],
                                                             AX.X, ALU.max, negate=True))
                    nc.vector.tensor_tensor(best, m.nmax2[:, mp, 0:1], m.nmax2[:, mp, 1:2], ALU.min)\
                        .then_inc(s[f"max{mp}"], 1)

            def combine(n):
                qt = jobs[n][0]
                p = m.prob[:, n % 2, :, 0:nkeys(qt)]
                dve.wait_ge(s["prob0"], n + 1)
                dve.wait_ge(s["prob1"], n + 1)
                c.then_wait(dve, nc.vector.reciprocal(m.rsum[:, n, :], m.sums[:, n, :]))
                c.then_wait(dve, nc.vector.scalar_tensor_tensor(m.mix[:, n:n + 1], m.sums[:, n, 0:1], m.lam[:, 3:4],
                                                                m.rsum[:, n, 1:2], ALU.mult, ALU.mult))
                for a, b in ((0, 512), (512, LAT + PAST)) if qt < LT else ((0, CTX // 2), (CTX // 2, CTX)):
                    nc.vector.scalar_tensor_tensor(p[:, 0, a:b], p[:, 1, a:b], m.mix[:, n:n + 1], p[:, 0, a:b],
                                                   ALU.mult, ALU.add).then_inc(s["combined"], 1)

            def out(n):
                qt, h = jobs[n]
                dve.wait_ge(s["valued"], n + 1)
                nc.vector.tensor_scalar(m.o_att[:, qt, h * DV:(h + 1) * DV], m.ps[:, 3584:3584 + DV],
                                        m.rsum[:, n, 0:1], None, ALU.mult).then_inc(s["row_out"], 1)

            def take_last(n):
                qt, h = jobs[n]
                if len(rounds(qt)) < 3:
                    return
                js = rounds(qt)[2]
                dve.wait_ge(s["turned"], first_round[n] + 3)
                nc.vector.tensor_copy(m.aT[:, n % 2, js[0]:js[-1] + 1, :].rearrange("p a b -> p (a b)"),
                                      m.ps[:, 3072:3072 + len(js) * P]).then_inc(s["taken"], 1)

            maxima(0)
            for n in range(NJ):
                combine(n)
                if n:
                    out(n - 1)
                maxima(n + 1)
                take_last(n)
            out(NJ - 1)

        @block.scalar
        def _(act):
            def probs(n, mp):
                if n >= NJ:
                    return
                if n >= 2 and mp == 0:
                    act.wait_ge(s["turned"], first_round[n - 1])
                act.wait_ge(s[f"max{mp}"], n + 1)
                nk = nkeys(jobs[n][0])
                nc.scalar.activation(m.prob[:, n % 2, mp, 0:nk], m.ps[:, mp * 1536:mp * 1536 + nk], ACT.Exp,
                                     bias=m.nmax[:, n, mp:mp + 1], accum_out=m.sums[:, n, mp:mp + 1])\
                    .then_inc(s[f"prob{mp}"], 1)

            def take(n, r):
                qt, h = jobs[n]
                if r >= len(rounds(qt)):
                    return
                js = rounds(qt)[r]
                act.wait_ge(s["turned"], first_round[n] + r + 1)
                if n >= 2 and r == 0:
                    act.wait_ge(s["valued"], n - 1)
                nc.scalar.activation(m.aT[:, n % 2, js[0]:js[-1] + 1, :].rearrange("p a b -> p (a b)"),
                                     m.ps[:, 3072:3072 + len(js) * P], ACT.Copy).then_inc(s["taken"], 1)

            probs(0, 0)
            probs(0, 1)
            for n in range(NJ):
                take(n, 0)
                probs(n + 1, 0)
                take(n, 1)
                probs(n + 1, 1)


def attention_finish(nc, m, l):
    n = NT * HEADS
    o4 = m.o_att.rearrange("p c (h v) -> p c h v", v=DV)
    sm = m.small[:, 0:n].rearrange("p (c h) -> p c h", h=HEADS)
    with stage(nc, m, "g_loaded", "step", "root", "out_ready", "transposed", "taken") as (block, s):
        sq = m.view(m.R_W, NT, 512)
        sq4 = sq.rearrange("p c (h v) -> p c h v", v=DV)

        @block.sync
        def _(sp):
            sp.dma_start(m.sub_gain[:, :], m.d["diff_subln_g"][l].partition_broadcast(P)).then_inc(s["g_loaded"], 16)

        @block.scalar
        def _(act):
            act.wait_ge(s["step"], 3)
            nc.scalar.activation(m.small[:, 0:n], m.small[:, 0:n], ACT.Sqrt).then_inc(s["root"], 1)
            for ct in range(4):
                act.wait_ge(s["transposed"], ct + 1)
                at = (ct % 2) * 1536
                nc.scalar.activation(m.oT[:, 2 + ct], m.ps[:, at:at + TOK], ACT.Copy).then_inc(s["taken"], 1)

        @block.vector
        def _(dve):
            c = Count(s["step"])
            c.then_wait(dve, nc.vector.tensor_tensor(sq[:, :, :], m.o_att[:, :, :], m.o_att[:, :, :], ALU.mult))
            c.then_wait(dve, nc.vector.tensor_reduce(sm, sq4, AX.X, ALU.add))
            c.then_wait(dve, nc.vector.tensor_scalar(m.small[:, 0:n], m.small[:, 0:n], 1.0 / DV, EPS, ALU.mult,
                                                     ALU.add))
            dve.wait_ge(s["root"], 1)
            c.then_wait(dve, nc.vector.reciprocal(m.small[:, 0:n], m.small[:, 0:n]))
            c.then_wait(dve, nc.vector.tensor_tensor(o4, o4, sm.unsqueeze(3).to_broadcast([P, NT, HEADS, DV]),
                                                     ALU.mult))
            dve.wait_ge(s["g_loaded"], 16)
            c.then_wait(dve, nc.vector.tensor_scalar(m.sub_gain[:, :], m.sub_gain[:, :], m.lay[:, 3:4], None,
                                                     ALU.mult))
            nc.vector.tensor_tensor(o4, o4, m.sub_gain[:, :].unsqueeze(1).unsqueeze(1)
                                    .to_broadcast([P, NT, HEADS, DV]), ALU.mult).then_inc(s["out_ready"], 1)

        @block.tensor
        def _(pe):
            pe.wait_ge(s["out_ready"], 1)
            for ct in range(4):
                if ct >= 2:
                    pe.wait_ge(s["taken"], ct - 1)
                for t in range(NT):
                    at = (ct % 2) * 1536 + t * P
                    last = nc.tensor.transpose(m.ps[:, at:at + P], m.o_att[:, t, ct * P:(ct + 1) * P], m.ident[:, :])
                last.then_inc(s["transposed"], 1)

MAGIC = 12582912.0
TWO_PI_HI = 6.28125
TWO_PI_LO = 2 * math.pi - 6.28125
PI_BELOW = 3.1415925


def hyena_filters(nc, m, l, g):
    L, nt = g.L, g.nt
    W = min(L, 512)
    halves = range(L // W)
    with stage(nc, m, "small_loaded", "decay_loaded", "biased", "hidden", "argued", "reduced", "sine", "taps_done",
               "taps", "magnitude", "mag_used", "folded", "copied", "table0", "table1", "summed", "norm",
               "unit0", "unit1", "unit2", "unit3", "spectrum", "taken", "edge") as (block, s):
        @block.sync
        def _(sp):
            for dst, src in ((m.hy_pos[0:POS, 0:L], g.pos), (m.hy_w1[0:POS, :], m.d["hy_w1"][l]),
                             (m.hy_w2[0:HID, :], m.d["hy_w2"][l]), (m.hy_w3[0:HID, :], m.d["hy_w3"][l]),
                             (m.hy_bf[0:HID, :], m.d["hy_bf"][l]), (m.alt[:, :], m.d["alt"])):
                sp.dma_start(dst, src).then_inc(s["small_loaded"], 16)
            sp.dma_start(m.decay[:, 0:nt, :], g.decay).then_inc(s["decay_loaded"], 16)
            for u in range(8 if g.split else 0):
                if u >= 4:
                    sp.wait_ge(s["spectrum"], u - 3)
                sp.dma_start(m.units[:, u % 4], m.d["dft_units"][u]).then_inc(s[f"unit{u % 4}"], 16)
            for k in range(0 if g.split else 2 * nt):
                if k >= 2:
                    sp.wait_ge(s["spectrum"], k - 1)
                src = g.cos if k < nt else g.sin
                sp.dma_start(m.table[:, k % 2, 0:L], src[(k % nt) * P:(k % nt + 1) * P, :])\
                    .then_inc(s[f"table{k % 2}"], 16)

        @block.tensor
        def _(pe):
            pe.wait_ge(s["small_loaded"], 16 * 6)
            for h in halves:
                last = nc.tensor.matmul(m.ps[0:HID, h * 512:h * 512 + W], m.hy_w1[0:POS, :],
                                        m.hy_pos[0:POS, h * W:(h + 1) * W], start=True, stop=True)
            last.then_inc(s["hidden"], 1)
            pe.wait_ge(s["sine"], 1)
            for h in halves:
                last = nc.tensor.matmul(m.ps[0:HID, h * 512:h * 512 + W], m.hy_w2[0:HID, :],
                                        m.hy_h[0:HID, h * W:(h + 1) * W], start=True, stop=True)
            last.then_inc(s["hidden"], 1)
            pe.wait_ge(s["sine"], 2)

            def column_sums(t):
                pe.wait_ge(s["magnitude"], t + 1)
                for d in range(2):
                    last = nc.tensor.matmul(m.ps[:, 3584:4096], m.ones[:, :],
                                            m.mag[:, t % 2, d * 512:(d + 1) * 512],
                                            start=(t == 0 and d == 0), stop=(t == nt - 1 and d == 1))
                last.then_inc(s["mag_used"], 1)

            for t in range(nt):
                if t >= 2:
                    pe.wait_ge(s["taps"], t - 1)
                for d in range(2):
                    last = nc.tensor.matmul(m.ps[:, (t % 2) * 1024 + d * 512:(t % 2) * 1024 + (d + 1) * 512],
                                            m.hy_h[0:HID, t * P:(t + 1) * P], m.hy_w3[0:HID, d * 512:(d + 1) * 512],
                                            start=True, stop=True)
                last.then_inc(s["taps_done"], 1)
                if t:
                    column_sums(t - 1)
            column_sums(nt - 1)
            pe.wait_ge(s["norm"], 1)
            pe.wait_ge(s["copied"], nt)
            pe.wait_ge(s["folded"], 2 * nt)
            if g.split:
                for u in range(8):
                    part, par = u // 4, u // 2 % 2
                    pe.wait_ge(s[f"unit{u % 4}"], 16 * (u // 4 + 1))
                    if part and u % 2 == 0:
                        pe.wait_ge(s["taken"], 4 * (par + 1))
                    for i in range(2):
                        jt = 2 * (u % 2) + i
                        for ft in range(4):
                            last = nc.tensor.matmul(m.ps[:, par * 2048 + ft * 512:par * 2048 + (ft + 1) * 512],
                                                    m.units[:, u % 4, i, ft * P:(ft + 1) * P],
                                                    m.hf[:, 4 * par + jt, part * 512:(part + 1) * 512],
                                                    start=(jt == 0), stop=(jt == 3))
                    last.then_inc(s["spectrum"], 1)
                pe.wait_ge(s["taken"], 12)
                for k in range(4):
                    last = nc.tensor.matmul(m.ps[0:1, 0:512], m.alt[:, 0:1], m.hf[:, k, 0:512], start=(k == 0),
                                            stop=(k == 3))
                last.then_inc(s["spectrum"], 1)
                return
            for part in range(2):
                if part:
                    pe.wait_ge(s["taken"], nt)
                for k in range(nt):
                    kk = part * nt + k
                    pe.wait_ge(s[f"table{kk % 2}"], 16 * (kk // 2 + 1))
                    for ft in range(nt):
                        last = nc.tensor.matmul(m.ps[:, ft * 512:(ft + 1) * 512],
                                                m.table[:, kk % 2, ft * P:(ft + 1) * P],
                                                m.hf[:, k, part * 512:(part + 1) * 512],
                                                start=(k == 0), stop=(k == nt - 1))
                    last.then_inc(s["spectrum"], 1)
            pe.wait_ge(s["taken"], 2 * nt)
            for k in range(nt):
                last = nc.tensor.matmul(m.ps[0:1, 0:512], m.alt[:, 0:1], m.hf[:, k, 0:512], start=(k == 0),
                                        stop=(k == nt - 1))
            last.then_inc(s["spectrum"], 1)

        @block.scalar
        def _(act):
            act.wait_ge(s["biased"], 1)
            for layer in range(2):
                act.wait_ge(s["hidden"], layer + 1)
                nc.scalar.activation(m.hy_a[0:HID, 0:L], m.ps[0:HID, 0:L], ACT.Identity,
                                     bias=m.hy_bf[0:HID, layer:layer + 1], scale=m.hy_bf[0:HID, 2 + layer:3 + layer])\
                    .then_inc(s["argued"], 1)
                act.wait_ge(s["reduced"], layer + 1)
                nc.scalar.activation(m.hy_h[0:HID, 0:L], m.hy_a[0:HID, 0:L], ACT.Sin).then_inc(s["sine"], 1)
            for t in range(nt):
                act.wait_ge(s["taps"], t + 1)
                if t >= 2:
                    act.wait_ge(s["mag_used"], t - 1)
                nc.scalar.activation(m.mag[:, t % 2, :], m.hf[:, t, :], ACT.Abs).then_inc(s["magnitude"], 1)
            for t in range(nt):
                act.wait_ge(s["folded"], 2 * t + 2)
                nc.scalar.activation(m.hf[:, t, 0:512], m.fold[:, t % 4, :], ACT.Copy).then_inc(s["copied"], 1)

        @block.vector
        def _(dve):
            dve.wait_ge(s["small_loaded"], 16 * 6)
            nc.vector.tensor_tensor(m.hy_bf[0:HID, 0:2], m.hy_bf[0:HID, 0:2], m.hy_bf[0:HID, 2:4], ALU.mult)\
                .then_inc(s["biased"], 1)
            a, k = m.hy_a[0:HID, 0:L], m.hy_k[0:HID, 0:L]
            c = Count(s["edge"])
            for layer in range(2):
                dve.wait_ge(s["argued"], layer + 1)
                c.then_wait(dve, nc.vector.tensor_scalar(k, a, 1.0 / (2 * math.pi), None, ALU.mult))
                c.then_wait(dve, nc.vector.tensor_scalar(k, k, MAGIC, None, ALU.add))
                c.then_wait(dve, nc.vector.tensor_scalar(k, k, MAGIC, None, ALU.subtract))
                c.then_wait(dve, nc.vector.scalar_tensor_tensor(a, k, -TWO_PI_HI, a, ALU.mult, ALU.add))
                c.then_wait(dve, nc.vector.scalar_tensor_tensor(a, k, -TWO_PI_LO, a, ALU.mult, ALU.add))
                nc.vector.tensor_scalar(a, a, PI_BELOW, -PI_BELOW, ALU.min, ALU.max).then_inc(s["reduced"], 1)
            dve.wait_ge(s["decay_loaded"], 16)
            for t in range(nt):
                dve.wait_ge(s["taps_done"], t + 1)
                nc.vector.tensor_tensor(m.hf[:, t, :].rearrange("p (a c) -> p a c", c=HYW),
                                        m.ps[:, (t % 2) * 1024:(t % 2 + 1) * 1024].rearrange("p (a c) -> p a c", c=HYW),
                                        m.decay[:, t, :].unsqueeze(1).to_broadcast([P, 4, HYW]), ALU.mult)\
                    .then_inc(s["taps"], 1)
            dve.wait_ge(s["mag_used"], nt)
            c.then_wait(dve, nc.vector.reciprocal(m.hy_rn[:, :], m.ps[:, 3584:4096]))
            nc.vector.tensor_scalar(m.hy_rn[:, :], m.hy_rn[:, :], (2.0 if g.split else 1.0) / L, None, ALU.mult)\
                .then_inc(s["norm"], 1)
            c.then_wait(dve, nc.vector.memset(m.hf[0:1, 0, 512:1024], 0.0))
            for t in range(nt):
                if t >= 4:
                    dve.wait_ge(s["copied"], t - 3)
                nc.vector.tensor_tensor(m.fold[:, t % 4, :], m.hf[:, t, 0:512], m.hf[:, t, 512:1024], ALU.add)\
                    .then_inc(s["folded"], 1)
                dve.wait_ge(s["folded"], 2 * t + 1)
                nc.vector.tensor_tensor(m.hf[:, t, 512:1024], m.hf[:, t, 0:512], m.hf[:, t, 512:1024],
                                        ALU.subtract).then_inc(s["folded"], 1)
            dve.wait_ge(s["norm"], 1)
            if g.split:
                for n in range(4):
                    dve.wait_ge(s["spectrum"], 2 * (n + 1))
                    for ft in range(4):
                        at = (n % 2) * 2048 + ft * 512
                        nc.vector.tensor_tensor(g.f[:, n, ft, :], m.ps[:, at:at + 512], m.hy_rn[:, :], ALU.mult)\
                            .then_inc(s["taken"], 1)
                dve.wait_ge(s["taken"], 16)
                for n, src in enumerate((0, 1, 1)):
                    c.done(nc.vector.tensor_copy(g.mid[:, n, :], g.f[:, src, 0, :]))
                dve.wait_ge(s["edge"], c.n)
                for n, sign in ((1, 0.5), (2, -0.5)):
                    c.done(nc.vector.tensor_scalar(g.mid[0:1, n, :], g.f[0:1, 3, 0, :], sign, None, ALU.mult))
                for n in range(2):
                    c.done(nc.vector.tensor_scalar(g.f[0:1, n, 0, :], g.f[0:1, n, 0, :], 0.5, None, ALU.mult))
                dve.wait_ge(s["edge"], c.n)
                nc.vector.memset(g.f[0:1, 2:4, 0, :], 0.0)
                dve.wait_ge(s["spectrum"], 9)
                nc.vector.scalar_tensor_tensor(g.mid[0:1, 0, :], m.ps[0:1, 0:512], 0.5, m.hy_rn[0:1, :],
                                               ALU.mult, ALU.mult)
                return
            for part, f in enumerate((g.fre, g.fim)):
                dve.wait_ge(s["spectrum"], (part + 1) * nt)
                for ft in range(nt):
                    nc.vector.tensor_tensor(f[:, ft, :], m.ps[:, ft * 512:(ft + 1) * 512], m.hy_rn[:, :], ALU.mult)\
                        .then_inc(s["taken"], 1)
            dve.wait_ge(s["taken"], 2 * nt)
            c.then_wait(dve, nc.vector.memset(g.fim[0:1, 0, :], 0.0))
            c.then_wait(dve, nc.vector.tensor_copy(g.nyq[:, :], g.fre[:, 0, :]))
            c.then_wait(dve, nc.vector.tensor_scalar(g.fre[0:1, 0, :], g.fre[0:1, 0, :], 0.5, None, ALU.mult))
            dve.wait_ge(s["spectrum"], 2 * nt + 1)
            nc.vector.scalar_tensor_tensor(g.nyq[0:1, :], m.ps[0:1, 0:512], 0.5, m.hy_rn[0:1, :], ALU.mult, ALU.mult)


def token_tile(x, t):
    if t == LT:
        return x[:, LAT:TOK]
    half = LT // 2
    return x[:, 0:LAT].rearrange("p (j n two) -> p two j n", two=2, n=P)[:, t // half, t % half]


def hyena_short(nc, m, l):
    with stage(nc, m, "z_loaded0", "z_loaded1", "w_loaded", "tap", "mixed", "transposed", "taken") as (block, s):
        @block.sync
        def _(sp):
            for dst, src in ((m.hy_cw, "hy_conv_w"), (m.hy_cb, "hy_conv_b"), (m.hy_skip, "hy_skip")):
                sp.dma_start(dst[:, :], m.d[src][l]).then_inc(s["w_loaded"], 16)
            for n in range(2):
                sp.dma_start(m.zraw[:, 3 * n:3 * n + 3, :],
                             m.zhy_dram[3 * n * P:3 * (n + 1) * P, :].rearrange("(j p) t -> p j t", p=P))\
                    .then_inc(s[f"z_loaded{n}"], 16)

        @block.vector
        def _(dve):
            c = Count(s["tap"])
            dve.wait_ge(s["w_loaded"], 48)
            for j in range(6):
                dve.wait_ge(s[f"z_loaded{j // 3}"], 16)
                z, o = m.zraw[:, j], m.hv[:, j]
                w = [m.hy_cw[:, 3 * j + k:3 * j + k + 1] for k in range(3)]
                c.then_wait(dve, nc.vector.tensor_scalar(o, z, w[1], m.hy_cb[:, j:j + 1], ALU.mult, ALU.add))
                for a, b in ((0, LAT), (LAT, TOK)):
                    c.done(nc.vector.scalar_tensor_tensor(o[:, a + 1:b], z[:, a:b - 1], w[0], o[:, a + 1:b],
                                                          ALU.mult, ALU.add))
                dve.wait_ge(s["tap"], c.n)
                for a, b in ((0, LAT), (LAT, TOK)):
                    last = nc.vector.scalar_tensor_tensor(o[:, a:b - 1], z[:, a + 1:b], w[2], o[:, a:b - 1],
                                                          ALU.mult, ALU.add)
                    c.done(last)
            for j in range(2):
                dve.wait_ge(s["transposed"], j + 1)
                nc.vector.tensor_copy(m.hu[:, :, j * P:(j + 1) * P],
                                      m.ps[:, j * 1536:j * 1536 + TOK].rearrange("p (t n) -> p t n", n=P))

        @block.tensor
        def _(pe):
            for j in range(2):
                pe.wait_ge(s["tap"], 5 * (j + 1))
                for t in range(NT):
                    last = nc.tensor.transpose(m.ps[:, j * 1536 + t * P:j * 1536 + (t + 1) * P],
                                               token_tile(m.hv[:, j], t), m.ident[:, :])
                last.then_inc(s["transposed"], 1)


def hyena_conv(nc, m, l, g, order):
    L, nt, t0 = g.L, g.nt, g.t0
    W = min(L, 512)
    nh = L // W
    cols = slice(order * HYW, (order + 1) * HYW)
    ur = m.ps[:, 0:nt * HYW].rearrange("p (f c) -> p f c", c=HYW)
    ui = m.ps[:, 2048:2048 + nt * HYW].rearrange("p (f c) -> p f c", c=HYW)
    src = m.hv[:, 0:2, t0:t0 + L]
    gate = m.hv[:, 2 + 2 * order:4 + 2 * order, t0:t0 + L]
    with stage(nc, m, "fc0", "fc1", "fs0", "fs1", "forward", "product", "spectra", "inverse", "result",
               "transposed") as (block, s):
        @block.sync
        def _(sp):
            for k in range(2 * nt):
                if k >= 2:
                    sp.wait_ge(s["forward"], min(k - 1, nt))
                    if k - 2 >= nt:
                        sp.wait_ge(s["inverse"], k - 1 - nt)
                rows = slice((k % nt) * P, (k % nt + 1) * P)
                sp.dma_start(m.tcos[:, k % 2, 0:L], g.cos[rows, :]).then_inc(s[f"fc{k % 2}"], 16)
                sp.dma_start(m.tsin[:, k % 2, 0:L], (g.sin if k < nt else g.sin_t)[rows, :])\
                    .then_inc(s[f"fs{k % 2}"], 16)

        @block.tensor
        def _(pe):
            for k in range(nt):
                pe.wait_ge(s[f"fc{k % 2}"], 16 * (k // 2 + 1))
                pe.wait_ge(s[f"fs{k % 2}"], 16 * (k // 2 + 1))
                for table, out in ((m.tcos, ur), (m.tsin, ui)):
                    for ft in range(nt):
                        last = nc.tensor.matmul(out[:, ft, :], table[:, k % 2, ft * P:(ft + 1) * P],
                                                m.hu[:, t0 // P + k, :], start=(k == 0 and ft % 2 == 0),
                                                stop=(k == nt - 1), skip_group_check=True)
                last.then_inc(s["forward"], 1)
            pe.wait_ge(s["spectra"], 2)
            for k in range(nt):
                kk = nt + k
                pe.wait_ge(s[f"fc{kk % 2}"], 16 * (kk // 2 + 1))
                pe.wait_ge(s[f"fs{kk % 2}"], 16 * (kk // 2 + 1))
                for part, table in enumerate((m.tcos, m.tsin)):
                    for ct in range(2):
                        for h in range(nh):
                            at = (ct * 2 + h) * 512
                            last = nc.tensor.matmul(m.ps[:, at:at + W], m.hy[:, part, k, ct * P:(ct + 1) * P],
                                                    table[:, kk % 2, h * W:(h + 1) * W],
                                                    start=(k == 0 and part == 0), stop=(k == nt - 1 and part == 1))
                last.then_inc(s["inverse"], 1)
            if order == 0:
                pe.wait_ge(s["result"], 4)
                for ct in range(2):
                    for t in range(nt):
                        at = 2048 + ct * 1024 + t * P
                        last = nc.tensor.transpose(m.ps[:, at:at + P], src[:, ct, t * P:(t + 1) * P], m.ident[:, :])
                    last.then_inc(s["transposed"], 1)

        @block.vector
        def _(dve):
            fre, fim = g.fre[:, :, cols], g.fim[:, :, cols]
            yr, yi, tmp = m.hy[:, 0, 0:nt], m.hy[:, 1, 0:nt], m.htmp[:, 0:nt, :]
            dve.wait_ge(s["forward"], nt)
            c = Count(s["product"])
            c.done(nc.vector.tensor_tensor(yr, ur, fre, ALU.mult))
            c.then_wait(dve, nc.vector.tensor_tensor(tmp, ui, fim, ALU.mult))
            nc.vector.tensor_tensor(yr, yr, tmp, ALU.subtract).then_inc(s["spectra"], 1)
            dve.wait_ge(s["spectra"], 1)
            c.then_wait(dve, nc.vector.tensor_tensor(yi, ur, fim, ALU.mult))
            if nt > 1:
                c.done(nc.vector.tensor_tensor(tmp[:, 1:nt], ui[:, 1:nt], fre[:, 1:nt], ALU.mult))
            c.then_wait(dve, nc.vector.tensor_tensor(tmp[:, 0], ui[:, 0], g.nyq[:, cols], ALU.mult))
            nc.vector.tensor_tensor(yi, yi, tmp, ALU.add).then_inc(s["spectra"], 1)
            dve.wait_ge(s["inverse"], nt)
            r = Count(s["result"])
            for ct in range(2):
                y = m.ps[:, ct * 1024:ct * 1024 + L]
                r.then_wait(dve, nc.vector.scalar_tensor_tensor(src[:, ct], src[:, ct],
                                                                m.hy_skip[:, 2 * order + ct:2 * order + ct + 1], y,
                                                                ALU.mult, ALU.add))
                out = src[:, ct] if order == 0 else m.oT[:, 6 + ct, t0:t0 + L]
                r.done(nc.vector.tensor_tensor(out, src[:, ct], gate[:, ct], ALU.mult))
            if order == 0:
                for ct in range(2):
                    dve.wait_ge(s["transposed"], ct + 1)
                    nc.vector.tensor_copy(m.hu[:, t0 // P:t0 // P + nt, ct * P:(ct + 1) * P],
                                          m.ps[:, 2048 + ct * 1024:2048 + ct * 1024 + L]
                                          .rearrange("p (t n) -> p t n", n=P))


def hyena_conv_split(nc, m, l, g, order):
    H = LAT // 2
    HT = H // P
    cols = slice(order * HYW, (order + 1) * HYW)
    a, b, c_, d_ = (m.ps[:, n * 1024:(n + 1) * 1024].rearrange("p (f c) -> p f c", c=HYW) for n in range(4))
    src = m.hv[:, 0:2, 0:LAT]
    gate = m.hv[:, 2 + 2 * order:4 + 2 * order, 0:LAT]
    with stage(nc, m, "unit0", "unit1", "unit2", "unit3", "unit_used", "product", "spectra", "result",
               "transposed") as (block, s):
        @block.sync
        def _(sp):
            for u in range(16):
                if u >= 4:
                    sp.wait_ge(s["unit_used"], u - 3)
                sp.dma_start(m.units[:, u % 4], m.d["dft_units"][u]).then_inc(s[f"unit{u % 4}"], 16)

        @block.tensor
        def _(pe):
            for u in range(8):
                pe.wait_ge(s[f"unit{u % 4}"], 16 * (u // 4 + 1))
                out = (a, b, c_, d_)[u // 2]
                for i in range(2):
                    jt = 2 * (u % 2) + i
                    for ft in range(HT):
                        last = nc.tensor.matmul(out[:, ft, :], m.units[:, u % 4, i, ft * P:(ft + 1) * P],
                                                m.hu[:, HT * (u // 2 % 2) + jt, :], start=(jt == 0 and ft % 2 == 0),
                                                stop=(jt == HT - 1), skip_group_check=True)
                last.then_inc(s["unit_used"], 1)
            for u in range(8, 16):
                par, kt = divmod(u - 8, HT)
                pe.wait_ge(s[f"unit{u % 4}"], 16 * (u // 4 + 1))
                pe.wait_ge(s["spectra"], par + 1)
                for i in range(2):
                    for ct in range(2):
                        at = ct * 1024 + par * 512
                        last = nc.tensor.matmul(m.ps[:, at:at + H], m.hys[:, 2 * par + i, kt, ct * P:(ct + 1) * P],
                                                m.units[:, u % 4, i, :], start=(kt == 0 and i == 0),
                                                stop=(kt == HT - 1 and i == 1))
                last.then_inc(s["unit_used"], 1)
            if order == 0:
                for ct in range(2):
                    pe.wait_ge(s["result"], 2 * ct + 2)
                    for t in range(LT):
                        at = 2048 + ct * 1024 + t * P
                        last = nc.tensor.transpose(m.ps[:, at:at + P], token_tile(src[:, ct], t), m.ident[:, :])
                    last.then_inc(s["transposed"], 1)

        @block.vector
        def _(dve):
            fa, fb, fc, fd = (g.f[:, n, :, cols] for n in range(4))
            er, ei, orr, oi = (m.hys[:, n] for n in range(4))
            t = [m.htmp[:, 0:HT, :], m.htmp[:, HT:2 * HT, :]]
            c = Count(s["product"])

            def times(out, x, f, mid=None):
                if mid is None:
                    c.done(nc.vector.tensor_tensor(out, x, f, ALU.mult))
                else:
                    c.done(nc.vector.tensor_tensor(out[:, 0], x[:, 0], g.mid[:, mid, cols], ALU.mult))
                    c.done(nc.vector.tensor_tensor(out[:, 1:HT], x[:, 1:HT], f[:, 1:HT], ALU.mult))

            def add(out, x, op):
                dve.wait_ge(s["product"], c.n)
                c.then_wait(dve, nc.vector.tensor_tensor(out, out, x, op))

            dve.wait_ge(s["unit_used"], 4)
            for out, f0, f1 in ((er, fa, fb), (orr, fb, fa), (ei, fc, fd), (oi, fd, fc)):
                times(out, a, f0)
                times(t[0], b, f1)
                add(out, t[0], ALU.add)
            dve.wait_ge(s["unit_used"], 8)
            for re, im, r0, r1, i0, i1 in ((er, ei, fc, fd, (fa, 0), (fb, 2)), (orr, oi, fd, fc, (fb, 1), (fa, 0))):
                times(t[0], c_, r0)
                times(t[1], d_, r1)
                add(re, t[0], ALU.subtract)
                c.then_wait(dve, nc.vector.tensor_tensor(re, re, t[1], ALU.subtract))
                times(t[0], c_, *i0)
                times(t[1], d_, *i1)
                add(im, t[0], ALU.add)
                last = nc.vector.tensor_tensor(im, im, t[1], ALU.add)
                last.then_inc(s["spectra"], 1)
                dve.wait_ge(s["spectra"], 1)
            dve.wait_ge(s["unit_used"], 16)
            r = Count(s["result"])
            for ct in range(2):
                y = m.ps[:, ct * 1024:ct * 1024 + LAT].rearrange("p (two j) -> p j two", two=2)
                x = src[:, ct].rearrange("p (j two) -> p j two", two=2)
                r.then_wait(dve, nc.vector.scalar_tensor_tensor(x, x, m.hy_skip[:, 2 * order + ct:2 * order + ct + 1],
                                                                y, ALU.mult, ALU.add))
                out = src[:, ct] if order == 0 else m.oT[:, 6 + ct, 0:LAT]
                r.done(nc.vector.tensor_tensor(out, src[:, ct], gate[:, ct], ALU.mult))
            if order == 0:
                for ct in range(2):
                    dve.wait_ge(s["transposed"], ct + 1)
                    nc.vector.tensor_copy(m.hu[:, 0:LT, ct * P:(ct + 1) * P],
                                          m.ps[:, 2048 + ct * 1024:2048 + ct * 1024 + LAT]
                                          .rearrange("p (t n) -> p t n", n=P))


def hyena(nc, m, l):
    for g in (m.geo_lat, m.geo_ctx):
        hyena_filters(nc, m, l, g)
    hyena_short(nc, m, l)
    for order in range(2):
        hyena_conv_split(nc, m, l, m.geo_lat, order)
    for order in range(2):
        hyena_conv(nc, m, l, m.geo_ctx, order)


def gate_rows(nc, m, block_engines, s, which):
    dve, pe = block_engines
    col = (3 * which + 2) * KD
    if dve is not None:
        c = 0
        for g in range(2):
            for k in range(KD):
                n = g * KD + k
                if n >= 4:
                    dve.wait_ge(s["diag_used"], n - 3)
                nc.vector.tensor_scalar(m.diag[:, n % 4, :], m.ident[:, :], m.mod[:, col + k, g:g + 1], None,
                                        ALU.mult).then_inc(s["diag"], 1)
    if pe is not None:
        for g in range(2):
            for k in range(KD):
                n = g * KD + k
                pe.wait_ge(s["diag"], n + 1)
                nc.tensor.matmul(m.ps[:, 2048 + n * P:2048 + (n + 1) * P], m.ones[:, :], m.diag[:, n % 4, :],
                                 start=True, stop=True).then_inc(s["diag_used"], 1)


def output_projection(nc, m, l):
    with stage(nc, m, "w_loaded0", "w_loaded1", "x_loaded0", "x_loaded1", "x_loaded2", "diag", "diag_used", "rows_ready", "projected",
               "scaled", "updated", "stored0", "stored1", "stored2") as (block, s):
        @block.sync
        def _(sp):
            w = m.d["w_out"][l].rearrange("(k p) (h n) -> h p k n", p=P, n=512)
            for h in range(2):
                sp.dma_start(m.wo[:, :, h * 512:(h + 1) * 512], w[h]).then_inc(s[f"w_loaded{h}"], 16)
            for t in range(NT):
                if t >= 3:
                    sp.wait_ge(s[f"stored{t % 3}"], 16 * (t // 3))
                sp.dma_start(m.xr[:, t % 3], m.x_dram[t * P:(t + 1) * P, :]).then_inc(s[f"x_loaded{t % 3}"], 16)

        @block.tensor
        def _(pe):
            gate_rows(nc, m, (None, pe), s, 0)
            for t in range(NT):
                if t >= 2:
                    pe.wait_ge(s["scaled"], t - 1)
                for h in range(2):
                    if t == 0:
                        pe.wait_ge(s[f"w_loaded{h}"], 16)
                    for k in range(KD):
                        at = (t % 2) * 1024 + h * 512
                        last = nc.tensor.matmul(m.ps[:, at:at + 512], m.oT[:, k, t * P:(t + 1) * P],
                                                m.wo[:, k, h * 512:(h + 1) * 512], start=(k == 0), stop=(k == KD - 1))
                last.then_inc(s["projected"], 1)

        @block.vector
        def _(dve):
            gate_rows(nc, m, (dve, None), s, 0)
            dve.wait_ge(s["rows_ready"], 1)
            for t in range(NT):
                g = 0 if t < LT else 1
                dve.wait_ge(s["projected"], t + 1)
                if t >= 2:
                    dve.wait_ge(s["updated"], t - 1)
                nc.vector.tensor_tensor(m.dx[:, t % 2], m.ps[:, (t % 2) * 1024:(t % 2 + 1) * 1024], m.gb[:, g, :],
                                        ALU.mult).then_inc(s["scaled"], 1)
                dve.wait_ge(s[f"x_loaded{t % 3}"], 16 * (t // 3 + 1))
                dve.wait_ge(s["scaled"], t + 1)
                nc.vector.tensor_tensor(m.xr[:, t % 3], m.xr[:, t % 3], m.dx[:, t % 2], ALU.add)\
                    .then_inc(s["updated"], 1)

        @block.scalar
        def _(act):
            act.wait_ge(s["diag_used"], 16)
            nc.scalar.activation(m.gb.rearrange("p g n -> p (g n)"), m.ps[:, 2048:4096], ACT.Copy)\
                .then_inc(s["rows_ready"], 1)
            for t in range(NT):
                act.wait_ge(s["updated"], t + 1)
                act.dma_start(m.x_dram[t * P:(t + 1) * P, :], m.xr[:, t % 3]).then_inc(s[f"stored{t % 3}"], 16)
            for b in range(3):
                act.wait_ge(s[f"stored{b}"], 16 * 3)


def route(nc, m, l):
    with stage(nc, m, "w_loaded", "by_expert", "kept", "logits", "centred", "exps", "aff", "turned", "aff_t", "found", "cast",
               "sel_turned", "spread", "one_hot", "hot_turned", "gathered", "first_loaded", "zeros",
               "cleared") as (block, s):
        RL, RP = CAP_L // 8, CAP_P // 8

        @block.sync
        def _(sp):
            sp.dma_start(m.wr[:, :, :], m.d["w_router"][l].rearrange("(k p) e -> p k e", p=P))\
                .then_inc(s["w_loaded"], 16)
            for c, (name, h) in enumerate(EXPERT_CHUNKS):
                sp.dma_start(m.wbuf[:, c], m.d[name][l, 0].rearrange("(k p) (h n) -> h p k n", p=P, n=512)[h])\
                    .then_inc(s["first_loaded"], 16)
            sp.wait_ge(s["zeros"], 1)
            for t in range(LT):
                sp.dma_start(m.acc_dram[t * P:(t + 1) * P, :], m.zero[:, :]).then_inc(s["cleared"], 16)
            sp.wait_ge(s["first_loaded"], 16 * len(EXPERT_CHUNKS))
            sp.wait_ge(s["cleared"], 16 * LT)

        @block.gpsimd
        def _(pool):
            nc.gpsimd.memset(m.zero[:, :], 0.0).then_inc(s["zeros"], 1)

        @block.tensor
        def _(pe):
            pe.wait_ge(s["w_loaded"], 16)
            for q in range(TOK // TC):
                for k in range(KD):
                    last = nc.tensor.matmul(m.ps[0:E, 2560 + q * 512:2560 + q * 512 + TC], m.wr[:, k, :],
                                            m.hT[:, k, q * TC:(q + 1) * TC], start=(k == 0), stop=(k == KD - 1))
                last.then_inc(s["by_expert"], 1)
            for q in range(TOK // TC):
                pe.wait_ge(s["kept"], q + 1)
                for t in range(q * TC // P, (q + 1) * TC // P):
                    last = nc.tensor.transpose(m.ps[:, t * E:(t + 1) * E], m.aff_t[0:E, t * P:(t + 1) * P],
                                               m.ident[0:E, 0:E])
            last.then_inc(s["logits"], 1)
            pe.wait_ge(s["aff"], 1)
            for t in range(NT):
                last = nc.tensor.transpose(m.ps[0:E, 512 + t * P:512 + (t + 1) * P], m.aff[:, t, :], m.ident[:, :])
            last.then_inc(s["turned"], 1)
            pe.wait_ge(s["cast"], 2)
            for n, src in enumerate((m.topv, m.topf)):
                nc.tensor.matmul(m.ps[:, 2560 + n * 256:2560 + (n + 1) * 256], m.ones[0:E, :], m.spread[0:E, n],
                                 start=True, stop=True)
                last = nc.tensor.transpose(m.ps[:, 2048 + n * 32:2048 + n * 32 + E], src[0:E, 0:CAP_L],
                                           m.ident[0:E, 0:E])
            last.then_inc(s["sel_turned"], 1)
            pe.wait_ge(s["one_hot"], 1)
            for k in range(KD):
                at = (k % 2) * 512
                if k >= 2:
                    pe.wait_ge(s["gathered"], k - 1)
                nc.tensor.matmul(m.ps[:, at:at + E * CAP_P], m.xbuf[:, NT - 1, k * P:(k + 1) * P],
                                 m.hot[:, 0], start=True, stop=True).then_inc(s["hot_turned"], 1)
            pe.wait_ge(s["one_hot"], 2)
            for g in range(2):
                last = nc.tensor.transpose(m.ps[:, 3072 + g * P:3072 + (g + 1) * P], m.hot[:, 1, g * P:(g + 1) * P],
                                           m.ident[:, :])
            last.then_inc(s["hot_turned"], 1)

        @block.scalar
        def _(act):
            for q in range(TOK // TC):
                act.wait_ge(s["by_expert"], q + 1)
                nc.scalar.activation(m.aff_t[0:E, q * TC:(q + 1) * TC], m.ps[0:E, 2560 + q * 512:2560 + q * 512 + TC],
                                     ACT.Copy).then_inc(s["kept"], 1)
            act.wait_ge(s["centred"], 1)
            nc.scalar.activation(m.aff[:, :, :], m.aff[:, :, :], ACT.Exp).then_inc(s["exps"], 1)
            act.wait_ge(s["turned"], 1)
            nc.scalar.activation(m.aff_t[0:E, :], m.ps[0:E, 512:512 + TOK], ACT.Copy).then_inc(s["aff_t"], 1)

        @block.vector
        def _(dve):
            c = Count(s["found"])
            sm = m.small[:, 0:NT]
            lg = m.ps[:, 0:NT * E].rearrange("p (t e) -> p t e", e=E)
            dve.wait_ge(s["logits"], 1)
            c.then_wait(dve, nc.vector.tensor_reduce(sm, lg, AX.X, ALU.max))
            nc.vector.tensor_tensor(m.aff[:, :, :], lg, sm.unsqueeze(2).to_broadcast([P, NT, E]), ALU.subtract)\
                .then_inc(s["centred"], 1)
            dve.wait_ge(s["exps"], 1)
            c.then_wait(dve, nc.vector.tensor_reduce(sm, m.aff[:, :, :], AX.X, ALU.add))
            c.then_wait(dve, nc.vector.reciprocal(sm, sm))
            nc.vector.tensor_tensor(m.aff[:, :, :], m.aff[:, :, :], sm.unsqueeze(2).to_broadcast([P, NT, E]),
                                    ALU.mult).then_inc(s["aff"], 1)
            dve.wait_ge(s["aff_t"], 1)
            for a, b, r0, rounds in ((0, LAT, 0, RL), (LAT, TOK, CAP_L, RP)):
                v = m.aff_t[0:E, a:b]
                for r in range(rounds):
                    best = m.topv[0:E, r0 + 8 * r:r0 + 8 * (r + 1)]
                    c.then_wait(dve, nc.vector.max(best, v))
                    c.done(nc.vector.max_index(m.topi[0:E, r0 + 8 * r:r0 + 8 * (r + 1)], best, v))
                    dve.wait_ge(s["found"], c.n)
                    c.then_wait(dve, nc.vector.match_replace(v, best, v, -1.0))
            nc.vector.tensor_copy(m.topf[0:E, :], m.topi[0:E, :]).then_inc(s["spread"], 1)
            dve.wait_ge(s["spread"], 1)
            for n, src in enumerate((m.topv, m.topf)):
                nc.vector.tensor_tensor(m.spread[0:E, n].rearrange("p (e c) -> p e c", c=CAP_P),
                                        src[0:E, CAP_L:CAP].unsqueeze(1).to_broadcast([E, E, CAP_P]),
                                        m.ident[0:E, 0:E].unsqueeze(2).to_broadcast([E, E, CAP_P]), ALU.mult)\
                    .then_inc(s["cast"], 1)
            dve.wait_ge(s["sel_turned"], 1)
            nc.vector.tensor_scalar(m.hot[:, 0], m.ps[:, 2816:3072], m.row_number[:, 0:1], None, ALU.is_equal)\
                .then_inc(s["one_hot"], 1)
            dve.wait_ge(s["one_hot"], 1)
            nc.vector.tensor_tensor(m.hot[:, 1], m.ps[:, 2560:2816], m.hot[:, 0], ALU.mult).then_inc(s["one_hot"], 1)
            nc.vector.tensor_copy(m.gate_l[:, 0:E], m.ps[:, 2048:2048 + E])
            nc.vector.tensor_copy(m.idx_l[:, 0:E], m.ps[:, 2080:2080 + E])
            nc.vector.memset(m.idx_l[:, E:E + 1], 0)
            nc.vector.memset(m.xp[:, :, E * CAP_P:], 0.0)
            for k in range(KD):
                dve.wait_ge(s["hot_turned"], k + 1)
                nc.vector.tensor_scalar(m.xp[:, k, 0:E * CAP_P], m.ps[:, (k % 2) * 512:(k % 2) * 512 + E * CAP_P],
                                        m.mod[:, 4 * KD + k, 1:2], m.mod[:, 3 * KD + k, 1:2], ALU.mult, ALU.add)\
                    .then_inc(s["gathered"], 1)
            dve.wait_ge(s["hot_turned"], KD + 1)
            nc.vector.tensor_copy(m.combine.rearrange("p g t -> p (g t)"), m.ps[:, 3072:3328])


EXPERT_CHUNKS = (("w_gate", 0), ("w_up", 0), ("w_gate", 1), ("w_up", 1), ("w_down", 0), ("w_down", 1))


def experts(nc, m, l):
    CH = ("gate0", "up0", "gate1", "up1", "down0", "down1")
    HK = KD // 2
    names = [f"w_{c}" for c in CH] + [f"w_{c}_used" for c in CH]
    with stage(nc, m, *names, "index", "go", "sw_rows_l0", "sw_rows_l1", "rows_turned", "x_ready",
               "gu_done", "silu", "hid_ready", "down_done", "y_ready", "y_turned", "gates", "out_l",
               "sw_scattered_l", "p_turned", "p_rows", "p_summed", "p_out", "p_stored", "x_rows") as (block, s):
        yp_of = m.yp.rearrange("p k (e c) -> p e k c", c=CAP_P)
        xp_of = m.xp.rearrange("p k (e c) -> p e k c", c=CAP_P)

        @block.sync
        def _(sp):
            for t in range(NT):
                sp.dma_start(m.er_x[:, t], m.x_dram[t * P:(t + 1) * P, :]).then_inc(s["x_rows"], 16)
            mid = [m.d[name][l, 1:E - 1].rearrange("(i j) (k p) (h n) -> i j h p k n", j=2, p=P, n=512)
                   for name, _ in EXPERT_CHUNKS]
            with sp.Fori(0, (E - 2) // 2) as i:
                for j in range(2):
                    for c, (_, h) in enumerate(EXPERT_CHUNKS):
                        sp.wait_ge(s[f"w_{CH[c]}_used"], i * 2 + j + 2)
                        sp.dma_start(m.wbuf[:, c], mid[c][i, j, h]).then_inc(s[f"w_{CH[c]}"], 16)
            for c, (name, h) in enumerate(EXPERT_CHUNKS):
                sp.wait_ge(s[f"w_{CH[c]}_used"], E)
                sp.dma_start(m.wbuf[:, c], m.d[name][l, E - 1].rearrange("(k p) (h n) -> h p k n", p=P, n=512)[h])\
                    .then_inc(s[f"w_{CH[c]}"], 16)
            sp.wait_ge(s["p_out"], 2)
            sp.dma_start(m.acc_dram[LAT:TOK, :], m.p_sum[:, :]).then_inc(s["p_stored"], 16)
            sp.wait_ge(s["p_stored"], 16)
            sp.wait_ge(s["x_rows"], 16 * NT)

        @block.gpsimd
        def _(pool):
            def gather(e, j, first=False):
                if not first:
                    pool.wait_ge(s["rows_turned"], 2 * (e - 1) + 1)
                nc.gpsimd.tensor_copy(m.ib_l[:, j:j + 1], m.idx_l[:, bass.ds(e, 1)]).then_inc(s["index"], 1)
                pool.wait_ge(s["index"], e + 1)
                pool.sem_inc(s["go"], 1)
                pool.indirect_dma_start(m.rows_l[:, j], None, m.xn_dram,
                                        bass.IndirectOffsetOnAxis(ap=m.ib_l[:, j:j + 1], axis=0))\
                    .then_inc(s[f"sw_rows_l{j}"], 16)

            gather(0, 0, True)
            with pool.Fori(0, E // 2) as i:
                for j in range(2):
                    e = i * 2 + j
                    gather(e + 1, (j + 1) % 2)
                    pool.wait_ge(s["out_l"], e + 2)
                    pool.sem_inc(s["go"], 1)
                    pool.indirect_dma_start(m.acc_dram, bass.IndirectOffsetOnAxis(ap=m.ib_l[:, j:j + 1], axis=0),
                                            m.y_l[:, j], None, compute_op=ALU.add).then_inc(s["sw_scattered_l"], 16)
                    pool.wait_ge(s["sw_scattered_l"], e * 16 + 16)
            pool.wait_ge(s["sw_rows_l0"], 16 * (E // 2 + 1))

        @block.tensor
        def _(pe):
            def turn_rows(e, loads, j, g):
                if g == 0:
                    pe.wait_ge(s[f"sw_rows_l{j}"], loads * 16)
                    pe.wait_ge(s["x_ready"], e + 1)
                for k in range(g * HK, (g + 1) * HK):
                    last = nc.tensor.transpose(m.ps[:, 3072 + k * P:3072 + (k + 1) * P],
                                               m.rows_l[:, j, k * P:(k + 1) * P], m.ident[:, :])
                last.then_inc(s["rows_turned"], 1)

            for n in [f"w_{c}_used" for c in CH] + ["rows_turned"]:
                pe.sem_inc(s[n], 1)
            for c in CH:
                pe.sem_inc(s[f"w_{c}"], 16)
            for g in range(2):
                turn_rows(0, 1, 0, g)
            with pe.Fori(0, E // 2) as i:
                for j in range(2):
                    e = i * 2 + j
                    pe.wait_ge(s["x_ready"], e + 2)
                    for h in range(2):
                        pe.wait_ge(s[f"w_gate{h}"], (e + 1) * 16)
                        pe.wait_ge(s[f"w_up{h}"], (e + 1) * 16)
                        for q in range(4):
                            n = h * 4 + q
                            pe.wait_ge(s["hid_ready"], e * 8 + max(n - 1, 0) + 1)
                            for which in range(2):
                                at = ((n % 2) * 2 + which) * 512
                                for k in range(KD):
                                    last = nc.tensor.matmul(m.ps[:, at:at + CAP],
                                                            m.wbuf[:, 2 * h + which, k, q * P:(q + 1) * P],
                                                            m.xe[:, j, k, :], start=(k == 0), stop=(k == KD - 1))
                            last.then_inc(s["gu_done"], 1)
                            if q == 0 and h == 1:
                                pe.wait_ge(s["gu_done"], e * 8 + 4)
                                pe.sem_inc(s["w_gate0_used"], 1)
                                pe.sem_inc(s["w_up0_used"], 1)
                    turn_rows(e + 1, i + 1 + j, (j + 1) % 2, 0)
                    pe.wait_ge(s["out_l"], e + 1)
                    for h in range(2):
                        pe.wait_ge(s[f"w_down{h}"], (e + 1) * 16)
                        for q in range(4):
                            n = h * 4 + q
                            if n >= 2:
                                pe.wait_ge(s["y_ready"], e * 8 + n - 1)
                            at = (4 + n % 2) * 512
                            for k in range(KD):
                                if n == 0 and k == KD - 1:
                                    pe.wait_ge(s["hid_ready"], e * 8 + 9)
                                elif n == 0 and k == KD - 2:
                                    pe.wait_ge(s["hid_ready"], e * 8 + 8)
                                last = nc.tensor.matmul(m.ps[:, at:at + CAP], m.wbuf[:, 4 + h, k, q * P:(q + 1) * P],
                                                        m.hid[:, k, :], start=(k == 0), stop=(k == KD - 1))
                            last.then_inc(s["down_done"], 1)
                            if n == 0:
                                pe.wait_ge(s["gu_done"], e * 8 + 8)
                                pe.sem_inc(s["w_gate1_used"], 1)
                                pe.sem_inc(s["w_up1_used"], 1)
                            if n == 4:
                                pe.wait_ge(s["down_done"], e * 8 + 4)
                                pe.sem_inc(s["w_down0_used"], 1)
                    turn_rows(e + 1, i + 1 + j, (j + 1) % 2, 1)
                    pe.wait_ge(s["down_done"], e * 8 + 8)
                    pe.sem_inc(s["w_down1_used"], 1)
                    pe.wait_ge(s["y_ready"], e * 8 + 8)
                    for k in range(KD):
                        last = nc.tensor.transpose(m.ps[:, 2048 + k * P:2048 + (k + 1) * P], m.yT[:, k, 0:CAP_L],
                                                   m.ident[:, :])
                    last.then_inc(s["y_turned"], 1)
            pe.wait_ge(s["out_l"], E + 1)
            for g in range(2):
                for k in range(KD):
                    last = nc.tensor.transpose(m.ps[:, g * D + k * P:g * D + (k + 1) * P],
                                               m.yp[:, k, g * P:(g + 1) * P], m.ident[:, :])
                last.then_inc(s["p_turned"], 1)
            pe.wait_ge(s["p_rows"], 2)
            for h in range(2):
                for g in range(2):
                    last = nc.tensor.matmul(m.ps[:, 2048 + h * 512:2048 + (h + 1) * 512], m.combine[:, g, :],
                                            m.p_y[:, g, h * 512:(h + 1) * 512], start=(g == 0), stop=(g == 1))
                last.then_inc(s["p_summed"], 1)

        @block.scalar
        def _(act):
            with act.Fori(0, E // 2) as i:
                for j in range(2):
                    e = i * 2 + j
                    for n in range(8):
                        act.wait_ge(s["gu_done"], e * 8 + n + 1)
                        act.wait_ge(s["hid_ready"], e * 8 + max(n - 1, 0) + 1)
                        at = (n % 2) * 1024
                        nc.scalar.activation(m.sg[:, n % 2, :], m.ps[:, at:at + CAP], ACT.Silu)\
                            .then_inc(s["silu"], 1)
                    act.wait_ge(s["out_l"], e + 1)
                    for n in range(8):
                        act.wait_ge(s["down_done"], e * 8 + n + 1)
                        at = (4 + n % 2) * 512
                        nc.scalar.activation(m.yT[:, n, :], m.ps[:, at:at + CAP], ACT.Copy).then_inc(s["y_ready"], 1)
            act.wait_ge(s["p_turned"], 2)
            nc.scalar.activation(m.p_y[:, 1], m.ps[:, D:2 * D], ACT.Copy).then_inc(s["p_rows"], 1)
            act.wait_ge(s["p_summed"], 2)
            nc.scalar.activation(m.p_sum[:, 512:D], m.ps[:, 2560:3072], ACT.Copy).then_inc(s["p_out"], 1)

        @block.vector
        def _(dve):
            for n in ("x_ready", "hid_ready", "out_l"):
                dve.sem_inc(s[n], 1)

            def shape_x(e, j):
                for g in range(2):
                    dve.wait_ge(s["rows_turned"], 2 * e + g + 2)
                    if g == 0:
                        nc.vector.tensor_copy(m.xe[:, j:j + 1, :, CAP_L:CAP], xp_of[:, bass.ds(e, 1)])
                    for k in range(g * HK, (g + 1) * HK):
                        last = nc.vector.tensor_scalar(m.xe[:, j, k, 0:CAP_L], m.ps[:, 3072 + k * P:3072 + (k + 1) * P],
                                                       m.mod[:, 4 * KD + k, 0:1], m.mod[:, 3 * KD + k, 0:1],
                                                       ALU.mult, ALU.add)
                last.then_inc(s["x_ready"], 1)

            shape_x(0, 0)
            with dve.Fori(0, E // 2) as i:
                for j in range(2):
                    e = i * 2 + j
                    nc.vector.tensor_copy(m.gb_l[:, j:j + 1], m.gate_l[:, bass.ds(e, 1)]).then_inc(s["gates"], 1)
                    for n in range(8):
                        dve.wait_ge(s["silu"], e * 8 + n + 1)
                        at = (n % 2) * 1024 + 512
                        nc.vector.tensor_tensor(m.hid[:, n, :], m.sg[:, n % 2, :], m.ps[:, at:at + CAP], ALU.mult)\
                            .then_inc(s["hid_ready"], 1)
                    shape_x(e + 1, (j + 1) % 2)
                    dve.wait_ge(s["y_turned"], e + 1)
                    dve.wait_ge(s["gates"], e + 1)
                    nc.vector.tensor_copy(yp_of[:, bass.ds(e, 1)], m.yT[:, :, CAP_L:CAP].unsqueeze(1))
                    nc.vector.tensor_scalar(m.y_l[:, j], m.ps[:, 2048:3072], m.gb_l[:, j:j + 1], None, ALU.mult)\
                        .then_inc(s["out_l"], 1)
            dve.wait_ge(s["p_turned"], 1)
            nc.vector.tensor_copy(m.p_y[:, 0], m.ps[:, 0:D]).then_inc(s["p_rows"], 1)
            dve.wait_ge(s["p_summed"], 1)
            nc.vector.tensor_copy(m.p_sum[:, 0:512], m.ps[:, 2048:2560]).then_inc(s["p_out"], 1)


def expert_residual(nc, m, l):
    with stage(nc, m, *(f"x_loaded{t}" for t in range(NT)), "diag", "diag_used", "rows_ready", "scaled", "updated",
               "stored") as (block, s):
        @block.sync
        def _(sp):
            for t in range(NT):
                sp.dma_start(m.er_d[:, t], m.acc_dram[t * P:(t + 1) * P, :]).then_inc(s[f"x_loaded{t}"], 16)

        @block.tensor
        def _(pe):
            gate_rows(nc, m, (None, pe), s, 1)

        @block.vector
        def _(dve):
            gate_rows(nc, m, (dve, None), s, 1)
            dve.wait_ge(s["rows_ready"], 1)
            for t in range(NT + 1):
                if t < NT:
                    dve.wait_ge(s[f"x_loaded{t}"], 16)
                    nc.vector.tensor_tensor(m.er_d[:, t], m.er_d[:, t], m.gb[:, 0 if t < LT else 1, :],
                                            ALU.mult).then_inc(s["scaled"], 1)
                if t >= 1:
                    dve.wait_ge(s["scaled"], t)
                    nc.vector.tensor_tensor(m.er_x[:, t - 1], m.er_x[:, t - 1], m.er_d[:, t - 1], ALU.add)\
                        .then_inc(s["updated"], 1)

        @block.scalar
        def _(act):
            act.wait_ge(s["diag_used"], 16)
            nc.scalar.activation(m.gb.rearrange("p g n -> p (g n)"), m.ps[:, 2048:4096], ACT.Copy)\
                .then_inc(s["rows_ready"], 1)
            for t in range(NT):
                act.wait_ge(s["updated"], t + 1)
                act.dma_start(m.x_dram[t * P:(t + 1) * P, :], m.er_x[:, t]).then_inc(s["stored"], 16)
            act.wait_ge(s["stored"], 16 * NT)


def epilogue(nc, m):
    with stage(nc, m, "g_loaded", "squared", "mean", "root", "inverse", "gained", "stored") as (block, s):
        gain = m.gb[:, 0, :]
        G = 3

        @block.sync
        def _(sp):
            sp.dma_start(gain, m.d["final_norm_g"].partition_broadcast(P)).then_inc(s["g_loaded"], 16)
            for t in range(NT):
                sp.wait_ge(s["gained"], t + 1)
                sp.dma_start(m.o["x"][t * P:(t + 1) * P, :], m.er_x[:, t]).then_inc(s["stored"], 16)
            sp.wait_ge(s["stored"], 16 * NT)

        @block.scalar
        def _(act):
            for a in range(NT // G):
                for t in range(a * G, (a + 1) * G):
                    nc.scalar.activation(m.er_d[:, t], m.er_x[:, t], ACT.Square, accum_out=m.ss[:, t:t + 1])\
                        .then_inc(s["squared"], 1)
                act.wait_ge(s["mean"], a + 1)
                nc.scalar.activation(m.rt[:, a * G:(a + 1) * G], m.ms[:, a * G:(a + 1) * G], ACT.Sqrt)\
                    .then_inc(s["root"], 1)

        @block.vector
        def _(dve):
            for a in range(NT // G):
                r = slice(a * G, (a + 1) * G)
                dve.wait_ge(s["squared"], (a + 1) * G)
                nc.vector.tensor_scalar(m.ms[:, r], m.ss[:, r], 1.0 / D, EPS, ALU.mult, ALU.add)\
                    .then_inc(s["mean"], 1)
                dve.wait_ge(s["root"], a + 1)
                nc.vector.reciprocal(m.rs[:, r], m.rt[:, r]).then_inc(s["inverse"], 1)
                dve.wait_ge(s["inverse"], a + 1)
                if a == 0:
                    dve.wait_ge(s["g_loaded"], 16)
                for t in range(a * G, (a + 1) * G):
                    nc.vector.scalar_tensor_tensor(m.er_x[:, t], m.er_x[:, t], m.rs[:, t:t + 1], gain,
                                                   ALU.mult, ALU.mult).then_inc(s["gained"], 1)


def norm_two(nc, m, l):
    norm_to_channels(nc, m, l, 1)


class Mem:
    pass


ARENA = 52400


def build(nc, d, outs):
    m = Mem()
    m.d = d
    m.o = outs
    with ExitStack() as ctx:
        def sb(name, shape, dt=F32):
            return ctx.enter_context(nc.sbuf_tensor(name, shape, dt))

        m.ps = ctx.enter_context(nc.psum_tensor("ps", [P, 8 * 512], F32))
        m.ident = sb("ident", [P, P])
        m.ones = sb("ones", [P, P])
        m.cond = sb("cond", [P, KD, 2])
        m.mod = sb("mod", [P, NMOD * KD, 2])
        m.b_mod = sb("b_mod_sb", [P, NMOD * KD])
        m.norm_g = sb("norm_g_sb", [P, 2 * KD])
        m.ss, m.ms, m.rt, m.rs = (sb(n, [P, 16]) for n in ("ss", "ms", "rt", "rs"))
        m.small = sb("small", [P, 64])
        m.dec = sb("dec", [P, 4, NT])
        m.lb = sb("lb", [P, 36])
        m.lam = sb("lam", [P, 4])
        m.lay = sb("lay", [P, 4])
        m.hg_gain = sb("hg_gain", [P, DQ])
        arena = sb("arena", [P, ARENA])

        def view(at, *dims):
            n = int(np.prod(dims))
            assert at + n <= ARENA, (at, dims)
            a = arena[:, at:at + n]
            names = "abcd"[:len(dims)]
            if len(dims) == 1:
                return a
            return a.rearrange(f"p ({' '.join(names)}) -> p {' '.join(names)}", **dict(zip(names, dims)))
        m.view = view
        m.R_OT, m.R_ZC, m.R_ZT, m.R_W, m.R_FREE = 0, 9216, 25344, 34560, 42752
        m.hT = m.oT = view(m.R_OT, KD, TOK)
        m.zc = view(m.R_ZC, 14, TOK)
        m.zt = view(m.R_ZT, NT, D)
        m.W = view(m.R_W, 2, KD, 512)
        m.xbuf = view(9216, NT, D)
        m.sq = view(9216 + NT * D, D)
        m.qe = view(2 * TOK, 4, TOK)
        m.S = [view(6 * TOK, 2, NT, P), view(49572, 2, NT, P)]
        m.A = view(m.R_W, 4, NT, P + 1)
        m.X = view(39204, 2, TOK)
        m.E = view(41508, 2, TOK)
        m.xq = view(0, 2, NT, 2, 64)
        m.ke_t = view(43812, NT, 4, P)
        m.att = view(43812, 2, 2, NT, P)
        m.mask = view(48420, 2, 9, 64).bitcast(U32)
        m.o_sb = m.zt[:, :, 0:256]
        m.kraw = view(34560, 2, HEADS, P)
        m.kctx = view(35584, HEADS, PAST)
        m.vctx = view(36608, 2, HEADS, DV)
        m.cos, m.sin = view(37632, LAT), view(38656, LAT)
        m.rot = view(39680, 2, LAT)
        m.prob = view(41728, 2, 2, LAT + PAST)
        m.aT = view(46848, 2, (LAT + PAST) // P, P)
        m.kout = view(49408, HEADS, P)
        m.lamv = view(49920, 4 * DQ)
        m.nmax, m.sums, m.rsum = (view(50176 + 80 * j, 40, 2) for j in range(3))
        m.mix = view(50416, 40)
        m.nmax2 = view(50584, 2, 2)
        m.sub_gain = view(50456, DV)
        m.o_att = view(m.R_ZC, NT, 512)
        m.q1 = view(m.R_OT + 2 * TOK, HEADS, TOK)
        m.hy_pos, m.hy_h, m.hy_a, m.hy_k = (view(9216 + 1024 * j, 1024) for j in range(4))
        m.hy_w3 = view(13312, 1024)
        m.hy_w1, m.hy_w2 = view(14336, HID), view(14400, HID)
        m.hy_bf = view(14464, 4)
        m.mag = view(16128, 2, 1024)
        m.fold = view(18176, 4, 512)
        m.decay = view(20224, LT, HYW)
        m.zraw = view(9216, 6, TOK)
        m.hv = view(16128, 6, TOK)
        m.hf = view(23040, LT, 1024)
        m.hy = view(23040, 2, LT, HYW)
        m.htmp = view(27136, LT, HYW)
        m.table = view(43520, 2, 1024)
        m.tcos, m.tsin = m.table, view(45568, 2, 1024)
        m.hu = view(47616, NT, HYW)
        m.hy_rn = view(49920, 512)
        m.alt = sb("alt_sb", [P, 1])
        m.row_number = sb("row_number_sb", [P, 1])
        m.hy_cw, m.hy_cb, m.hy_skip = sb("hy_cw", [P, 18]), sb("hy_cb", [P, 6]), sb("hy_sk", [P, 4])

        def geometry(name, length, t0):
            g = Mem()
            g.L, g.nt, g.t0, g.split = length, length // P, t0, length == LAT
            g.pos, g.decay = d[f"pos_{name}"], d[f"decay_{name}"]
            return g
        m.geo_lat = geometry("lat", LAT, 0)
        m.geo_lat.f, m.geo_lat.mid = view(31232, 4, LT // 2, 512), view(39424, 3, 512)
        g = m.geo_ctx = geometry("ctx", CTX, LAT)
        g.fre, g.fim, g.nyq = view(40960, 1, 512), view(41472, 1, 512), view(41984, 512)
        g.cos, g.sin, g.sin_t = (d[f"{k}_ctx"] for k in ("dft_cos", "dft_sin", "dft_sin_t"))
        m.units = view(43520, 4, 2, LAT // 2)
        m.hys = view(23040, 4, LT // 2, HYW)
        m.wo = view(m.R_W, KD, D)
        m.xr = view(9216, 3, D)
        m.dx = view(12288, 2, D)
        m.gb = view(14336, 2, D)
        m.er_d, m.er_x = view(17408, NT, D), view(0, NT, D)
        m.diag = view(16384, 4, P)
        m.wr = view(9216, KD, E)
        m.aff = view(9344, NT, E)
        m.aff_t = view(9488, TOK)
        m.topv, m.topf = view(10640, CAP), view(10784, CAP)
        m.topi = view(10928, CAP).bitcast(U32)
        m.gate_l = view(11072, E)
        m.idx_l = view(11104, E + 1).bitcast(I32)
        m.ib_l = view(11138, 2).bitcast(I32)
        m.gb_l = view(11142, 2)
        m.zero = view(11264, D)
        m.rows_l = view(12288, 2, D)
        m.xp = view(14336, KD, (E + 1) * CAP_P)
        m.y_l = view(16512, 2, D)
        m.yp = view(18560, KD, E * CAP_P)
        m.xe, m.hid = view(20608, 2, KD, CAP), view(22912, KD, CAP)
        m.sg = view(24064, 2, CAP)
        m.combine, m.yT = view(49152, 2, P), view(49408, KD, CAP)
        m.hot, m.spread = view(50560, 2, E * CAP_P), view(51072, 2, E * CAP_P)
        m.p_y, m.p_sum = view(24576, 2, D), view(26624, D)
        m.wbuf = view(24576, 6, KD, 512)
        m.mod_rows = view(0, NMOD * D)
        m.acc_dram = nc.dram_tensor("expert_sum", (TOK, D), F32, kind="Internal").ap()
        m.zstage = view(m.R_FREE, 2, TOK)

        m.x_dram = nc.dram_tensor("x_rows", (TOK, D), F32, kind="Internal").ap()
        m.xn_dram = nc.dram_tensor("x_normed", (TOK, D), F32, kind="Internal").ap()
        m.zhy_dram = nc.dram_tensor("z_hyena", (6 * P, TOK), F32, kind="Internal").ap()
        m.sw_sems = {n: ctx.enter_context(nc.semaphore(n)) for n in
                     ("sw_rows_l0", "sw_rows_l1", "sw_scattered_l")}
        prologue(nc, m)
        with nc.Fori(0, DEPTH) as l:
            modulation(nc, m, l)
            norm_to_channels(nc, m, l, 0)
            projection(nc, m, l)
            hgrn_gates(nc, m, l)
            hgrn_states(nc, m, l)
            hgrn_outputs(nc, m, l)
            hgrn_finish(nc, m, l)
            attention_prepare(nc, m, l)
            attention(nc, m, l)
            attention_finish(nc, m, l)
            hyena(nc, m, l)
            output_projection(nc, m, l)
            norm_two(nc, m, l)
            route(nc, m, l)
            experts(nc, m, l)
            expert_residual(nc, m, l)
        epilogue(nc, m)


def prologue(nc, m):
    with stage(nc, m, "loaded", "copied", "silu") as (block, s):
        @block.sync
        def _(sp):
            sp.dma_start(m.x_dram, m.d["x"]).then_inc(s["copied"], 16)
            sp.dma_start(m.cond[:, :, :], m.d["cond"]).then_inc(s["loaded"], 16)
            sp.dma_start(m.row_number[:, :], m.d["row_number"]).then_inc(s["loaded"], 16)
            sp.dma_start(m.ident[:, :], m.d["ident"]).then_inc(s["loaded"], 16)
            sp.wait_ge(s["copied"], 16)
            sp.wait_ge(s["loaded"], 48)

        @block.vector
        def _(dve):
            nc.vector.memset(m.ones[:, :], 1.0)

        @block.scalar
        def _(act):
            act.wait_ge(s["loaded"], 48)
            nc.scalar.activation(m.cond[:, :, :], m.cond[:, :, :], ACT.Silu)


def host_arrays(i):
    f = np.float32
    a = {}
    a["x"] = np.concatenate([i["x_sample"][0], i["x_prompt"][0]], axis=0)
    a["cond"] = np.ascontiguousarray(np.stack([i["c"][0], i["c_ctx"]], axis=-1).reshape(KD, P, 2).transpose(1, 0, 2))
    a["w_mod"] = i["w_mod"]
    a["b_mod"] = np.ascontiguousarray(i["b_mod"].reshape(DEPTH, NMOD * KD, P).transpose(0, 2, 1))
    a["norm_g"] = np.ascontiguousarray(i["norm_g"].reshape(DEPTH, 2 * KD, P).transpose(0, 2, 1))
    a["w_in"] = i["w_in"]
    a["ident"] = np.eye(P, dtype=f)
    a["lb_logits"] = np.ascontiguousarray(i["hgrn_lb_logits"].reshape(DEPTH * 4, P).T)
    a["layer_const"] = np.array([[min(l, 1), (min(l, 1) - 1) * 1e30, LAM_INIT[l], 1 - LAM_INIT[l]]
                                 for l in range(2)], dtype=f)
    a["state"] = i["state_hgrn"][0].reshape(2, 2, 2, P, DQ)
    a["hgrn_norm_g"] = i["hgrn_norm_g"]
    mask = np.zeros((P, 2, len(LEVELS) + 2, 64), np.uint32)
    key = np.arange(P)[:, None]
    col = np.arange(64)
    for n, h in enumerate(LEVELS):
        blk = (col // h)[None]
        mask[:, 0, n] = (key // (2 * h) == blk) & (key % (2 * h) < h)
        mask[:, 1, n] = (key // (2 * h) == blk) & (key % (2 * h) >= h)
    for par in range(2):
        mask[:, :, len(LEVELS) + par] = (key == 2 * col + par)[:, None]
    a["hg_mask"] = mask
    pos = np.arange(LAT)
    sub = np.arange(P) % DQ
    inv = (f(10000.0) ** (-np.arange(0, 32, 2).astype(f) / f(32))).astype(f)
    where = np.where((sub < 32)[:, None], (pos // 64)[None], (pos % 64)[None]).astype(f)
    ang = where * inv[sub % 16][:, None]
    a["rope_cos"] = np.cos(ang).astype(f)
    a["rope_sin"] = (np.sin(ang) * np.where(sub % 32 < 16, -1, 1)[:, None]).astype(f)
    a["cache_k"] = i["cache_diff_k"][0]
    a["cache_v"] = i["cache_diff_v"][0]
    a["diff_lambda"] = i["diff_lambda"].reshape(DEPTH, 4 * DQ)
    a["diff_subln_g"] = i["diff_subln_g"]
    a["hy_w1"], a["hy_w2"], a["hy_w3"] = i["hy_filt_w1"], i["hy_filt_w2"], i["hy_filt_w3"]
    a["hy_bf"] = np.stack([i["hy_filt_b1"], i["hy_filt_b2"], i["hy_filt_freq"][:, 0], i["hy_filt_freq"][:, 1]], axis=-1)
    a["hy_conv_w"] = np.ascontiguousarray(i["hy_conv_w"].reshape(DEPTH, 3, 6, P).transpose(0, 3, 2, 1).reshape(DEPTH, P, 18))
    a["hy_conv_b"] = np.ascontiguousarray(i["hy_conv_b"].reshape(DEPTH, 6, P).transpose(0, 2, 1))
    a["hy_skip"] = np.ascontiguousarray(i["hy_skip"].reshape(DEPTH, 4, P).transpose(0, 2, 1))
    a["row_number"] = np.arange(P, dtype=f)[:, None]
    a["alt"] = np.where(np.arange(P) % 2, -1, 1).astype(f)[:, None]
    lo, hi = math.log(1e-2) / 1.5, math.log(1e-2) / 0.3
    deltas = np.linspace(lo, hi, HYW, dtype=f)
    for name, length in (("lat", LAT), ("ctx", CTX)):
        order = np.concatenate([np.arange(0, LAT, 2), np.arange(1, LAT, 2)]) if length == LAT else np.arange(CTX)
        t = np.linspace(0.0, 1.0, length, dtype=f)[:, None]
        fr = np.linspace(1e-4, (POS - 1) // 2 - 1, (POS - 1) // 2, dtype=f)[None]
        w = (f(2.0 * math.pi) * np.arange(length, dtype=f)[:, None] / f(length)).astype(f)
        pos = np.concatenate([t, np.cos(fr * w), -np.sin(fr * w)], axis=-1)
        a[f"pos_{name}"] = np.ascontiguousarray(pos[order].T)
        a[f"decay_{name}"] = np.ascontiguousarray(np.exp(-t * np.abs(deltas)).astype(f)[order]
                                                  .reshape(length // P, P, HYW).transpose(1, 0, 2))
    n = np.arange(CTX)
    ang = np.pi * (np.outer(n, n) % (2 * CTX)) / CTX
    a["dft_cos_ctx"] = np.cos(ang).astype(f)
    sin = np.sin(ang)
    sin[:, 0] = np.where(n % 2, -1, 1)
    a["dft_sin_ctx"] = sin.astype(f)
    a["dft_sin_t_ctx"] = np.ascontiguousarray(sin.T.astype(f))
    k = np.arange(LAT // 2)
    cos, sin = [], []
    for par in range(2):
        ang = np.pi * (np.outer(2 * k + par, k) % (2 * LAT)) / LAT
        cos.append(np.cos(ang))
        sin.append(np.sin(ang))
        sin[-1][:, 0] = np.where(k % 2, -1, 1)
    units = []
    for table in (cos, sin):
        for x in table:
            units += [np.stack([x[j * P:(j + 1) * P], x[(j + 1) * P:(j + 2) * P]], axis=1) for j in (0, 2)]
    for par in range(2):
        for j in range(LT // 2):
            units.append(np.stack([x[par].T[j * P:(j + 1) * P] for x in (cos, sin)], axis=1))
    a["dft_units"] = np.stack(units).astype(f)
    for n in ("w_out", "w_router", "w_gate", "w_up", "w_down", "final_norm_g"):
        a[n] = i[n]
    return a


OUTS = {"x": (TOK, D), "k": (DEPTH, HEADS, 2, CTX, DQ), "v": (DEPTH, HEADS, CTX, DV),
        "s": (DEPTH, 2, HEADS, DQ, DQ)}


def kernel(**inputs):
    import concourse.bacc as bacc
    from concourse.bass_utils import run_bass_kernel_spmd

    nc = bacc.Bacc("TRN2", target_bir_lowering=False, num_devices=1)
    arrays = {n: np.ascontiguousarray(a) for n, a in host_arrays(inputs).items()}
    ins = {n: nc.dram_tensor("in_" + n, a.shape, mybir.dt.from_np(a.dtype), kind="ExternalInput").ap()
           for n, a in arrays.items()}
    outs = {n: nc.dram_tensor("out_" + n, shape, F32, kind="ExternalOutput").ap() for n, shape in OUTS.items()}
    build(nc, ins, outs)
    r = run_bass_kernel_spmd(nc, [{"in_" + n: a for n, a in arrays.items()}], core_ids=[0]).results[0]
    x = r["out_x"]
    return (x[LAT:][None], x[:LAT][None], r["out_k"][None], r["out_v"][None], r["out_s"][None])
```
